# Optimizing a Trainium2 kernel written in Bass

```python
import jax, jax.numpy as jnp
from jax import lax
import numpy as np

D_MODEL = 1024
BATCH = 1
SEQ = 512
DEPTH = 1

CHUNK = 64
N_META = 16
Q_BLOCK = 128
N_PAD = Q_BLOCK - N_META
PREFIX = N_PAD + N_META
MIX_WIDTH = D_MODEL
RET_HEADS = 4
RET_DV = (MIX_WIDTH // 2) // RET_HEADS
RET_DK = RET_DV // 2
FOX_HEADS = 8
FOX_DH = (MIX_WIDTH // 2) // FOX_HEADS
D_FF = 2816
CONV_W = 3
ROPE_BASE = 10000.0
EPS = 1e-6
NEG = -1e30

RET_QK = RET_HEADS * RET_DK
RET_V = RET_HEADS * RET_DV
FOX_W = FOX_HEADS * FOX_DH
SPLIT_POINTS = (RET_QK, 2 * RET_QK, 2 * RET_QK + RET_V, 2 * RET_QK + 2 * RET_V,
                2 * RET_QK + 2 * RET_V + FOX_W, 2 * RET_QK + 2 * RET_V + 2 * FOX_W,
                2 * RET_QK + 2 * RET_V + 3 * FOX_W)
IN_WIDTH = 2 * RET_QK + 2 * RET_V + 3 * FOX_W + FOX_HEADS


def rms_norm(x, g):
    xf = x.astype(jnp.float32)
    y = xf * lax.rsqrt(jnp.mean(xf * xf, axis=-1, keepdims=True) + EPS)
    return (y * g.astype(jnp.float32)).astype(x.dtype)

def rotary(x, pos):
    half = x.shape[-1] // 2
    inv = 1.0 / (ROPE_BASE ** (jnp.arange(half, dtype=jnp.float32) / half))
    ang = pos.astype(jnp.float32)[:, None] * inv[None, :]
    cos = jnp.cos(ang)[None, :, None, :]
    sin = jnp.sin(ang)[None, :, None, :]
    x1 = x[..., :half].astype(jnp.float32)
    x2 = x[..., half:].astype(jnp.float32)
    return jnp.concatenate([x1 * cos - x2 * sin, x1 * sin + x2 * cos], axis=-1)

def retention(q, k, v, valid):
    B, L, H, dk = q.shape
    dv = v.shape[-1]
    nc = L // CHUNK
    f32 = jnp.float32
    log_g = jnp.log1p(-jnp.exp2(-5.0 - jnp.arange(H, dtype=f32)))
    pos = jnp.arange(L)
    qr = rotary(q, pos)
    kr = rotary(k, pos) * (dk ** -0.5) * valid.astype(f32)[None, :, None, None]
    qc = qr.reshape(B, nc, CHUNK, H, dk)
    kc = kr.reshape(B, nc, CHUNK, H, dk)
    vc = v.astype(f32).reshape(B, nc, CHUNK, H, dv)
    n = jnp.arange(CHUNK, dtype=f32)
    d_intra = jnp.exp(jnp.abs(n[:, None] - n[None, :])[None] * log_g[:, None, None])
    s = jnp.einsum('bcnhd,bcmhd->bchnm', qc, kc) * d_intra[None, None]
    intra = jnp.einsum('bchnm,bcmhe->bcnhe', s, vc)
    w_k = jnp.exp((CHUNK - 1.0 - n)[:, None] * log_g[None, :])
    u = jnp.einsum('bcmhd,bcmhe->bchde', kc * w_k[None, None, :, :, None], vc)
    g_chunk = jnp.exp(CHUNK * log_g)[None, :, None, None]

    def step(r, u_i):
        return g_chunk * r + u_i, r

    _, r_prev = lax.scan(step, jnp.zeros((B, H, dk, dv), f32), jnp.moveaxis(u, 1, 0))
    r_prev = jnp.moveaxis(r_prev, 0, 1)
    w_q = jnp.exp((n + 1.0)[:, None] * log_g[None, :])
    inter = jnp.einsum('bcnhd,bchde->bcnhe', qc * w_q[None, None, :, :, None], r_prev)
    return (intra + inter).reshape(B, L, H, dv)

def forgetting_attention(q, k, v, log_f, valid):
    B, L, H, dh = q.shape
    f32 = jnp.float32
    scale = dh ** -0.5
    c = jnp.cumsum(log_f.astype(f32), axis=1).transpose(0, 2, 1)
    qf, kf, vf = q.astype(f32), k.astype(f32), v.astype(f32)
    pos = jnp.arange(L)
    outs = []
    for blk in range(L // Q_BLOCK):
        q0, q1 = blk * Q_BLOCK, (blk + 1) * Q_BLOCK
        logits = jnp.einsum('bqhd,bkhd->bhqk', qf[:, q0:q1], kf[:, :q1]) * scale
        bias = c[:, :, q0:q1, None] - c[:, :, None, :q1]
        mask = (pos[None, :q1] <= pos[q0:q1, None]) & valid[None, :q1]
        logits = jnp.where(mask[None, None], logits + bias, NEG)
        p = jax.nn.softmax(logits, axis=-1)
        outs.append(jnp.einsum('bhqk,bkhd->bqhd', p, vf[:, :q1]))
    return jnp.concatenate(outs, axis=1)

def hybrid_mixer(h, w_in, forget_b, ret_norm_g, w_out, valid):
    B, L, _ = h.shape
    proj = jnp.einsum('bld,de->ble', h, w_in)
    rq, rk, rv, rg, fq, fk, fv, ff = jnp.split(proj, SPLIT_POINTS, axis=-1)
    o_r = retention(rq.reshape(B, L, RET_HEADS, RET_DK), rk.reshape(B, L, RET_HEADS, RET_DK),
                    rv.reshape(B, L, RET_HEADS, RET_DV), valid)
    o_r = o_r * lax.rsqrt(jnp.mean(o_r * o_r, axis=-1, keepdims=True) + EPS)
    o_r = o_r.reshape(B, L, RET_V) * ret_norm_g.astype(jnp.float32) * jax.nn.silu(rg.astype(jnp.float32))
    log_f = jax.nn.log_sigmoid(ff.astype(jnp.float32) + forget_b.astype(jnp.float32))
    o_f = forgetting_attention(fq.reshape(B, L, FOX_HEADS, FOX_DH), fk.reshape(B, L, FOX_HEADS, FOX_DH),
                               fv.reshape(B, L, FOX_HEADS, FOX_DH), log_f, valid).reshape(B, L, FOX_W)
    mixed = jnp.concatenate([o_r, o_f], axis=-1).astype(h.dtype)
    return jnp.einsum('ble,ed->bld', mixed, w_out)

def conv_ffn(h, w_up, conv_w, conv_b, w_down, valid):
    L = h.shape[1]
    up = jnp.einsum('bld,df->blf', h, w_up)
    a, b = jnp.split(up, 2, axis=-1)
    a = a * valid.astype(a.dtype)[None, :, None]
    a_pad = jnp.pad(a, ((0, 0), (CONV_W - 1, 0), (0, 0)))
    acc = conv_b
    for j in range(CONV_W):
        acc = acc + a_pad[:, j:j + L] * conv_w[j]
    return jnp.einsum('blf,fd->bld', jax.nn.silu(acc) * b, w_down)

def first_inputs(seed: int = 0) -> dict:
    key = jax.random.key(seed)
    ks = jax.random.split(key, 13)
    f32 = jnp.float32
    return {
        "x": jax.random.normal(ks[0], (BATCH, SEQ, D_MODEL), f32),
        "meta_tokens": jax.random.normal(ks[1], (N_META, D_MODEL), f32),
        "attn_norm_g": 1.0 + 0.02 * jax.random.normal(ks[2], (DEPTH, D_MODEL), f32),
        "w_in": jax.random.normal(ks[3], (DEPTH, D_MODEL, IN_WIDTH), f32) * D_MODEL ** -0.5,
        "fox_forget_b": jax.random.uniform(ks[4], (DEPTH, FOX_HEADS), f32, 1.0, 5.0),
        "ret_norm_g": 1.0 + 0.02 * jax.random.normal(ks[5], (DEPTH, RET_V), f32),
        "w_out": jax.random.normal(ks[6], (DEPTH, MIX_WIDTH, D_MODEL), f32) * MIX_WIDTH ** -0.5,
        "ffn_norm_g": 1.0 + 0.02 * jax.random.normal(ks[7], (DEPTH, D_MODEL), f32),
        "w_up": jax.random.normal(ks[8], (DEPTH, D_MODEL, 2 * D_FF), f32) * D_MODEL ** -0.5,
        "conv_w": jax.random.normal(ks[9], (DEPTH, CONV_W, D_FF), f32) * CONV_W ** -0.5,
        "conv_b": 0.02 * jax.random.normal(ks[10], (DEPTH, D_FF), f32),
        "w_down": jax.random.normal(ks[11], (DEPTH, D_FF, D_MODEL), f32) * D_FF ** -0.5,
        "final_norm_g": 1.0 + 0.02 * jax.random.normal(ks[12], (D_MODEL,), f32),
    }

def first_block(x, meta_tokens, attn_norm_g, w_in, fox_forget_b, ret_norm_g, w_out,
              ffn_norm_g, w_up, conv_w, conv_b, w_down, final_norm_g):
    B = x.shape[0]
    pad = jnp.zeros((B, N_PAD, D_MODEL), x.dtype)
    meta = jnp.broadcast_to(meta_tokens.astype(x.dtype)[None], (B, N_META, D_MODEL))
    h = jnp.concatenate([pad, meta, x], axis=1)
    valid = jnp.arange(h.shape[1]) >= N_PAD
    for layer in range(DEPTH):
        h = h + hybrid_mixer(rms_norm(h, attn_norm_g[layer]), w_in[layer], fox_forget_b[layer],
                             ret_norm_g[layer], w_out[layer], valid)
        h = h + conv_ffn(rms_norm(h, ffn_norm_g[layer]), w_up[layer], conv_w[layer], conv_b[layer],
                         w_down[layer], valid)
    return rms_norm(h, final_norm_g)[:, PREFIX:]


GRID_W = 64
CTX_LEN = 256
N_HEADS = 16
Q_RANK = 256
KV_RANK = 128
NOPE_DIM = 64
ROPE_DIM = 32
V_DIM = 64
ROPE_THETA = 10000.0
ATTN_SCALE = (NOPE_DIM + ROPE_DIM) ** -0.5
CONV_CH = D_MODEL
CONV_WIDTH = 31
CONV_HALF = CONV_WIDTH // 2
P_HEADS = 8
N_KEYS = 128
N_EXPERTS = N_KEYS * N_KEYS
P_DK = 256
P_TOPK = 16
P_CHUNK = 128

OFF_Q = 0
OFF_KV = Q_RANK
OFF_CONV = Q_RANK + KV_RANK + ROPE_DIM
OFF_GATE = OFF_CONV + 2 * CONV_CH
N_IN = OFF_GATE + 2 * D_MODEL


def rms_norm_2(x, g):
    xf = x.astype(jnp.float32)
    y = xf * lax.rsqrt(jnp.mean(xf * xf, axis=-1, keepdims=True) + EPS)
    return (y * g.astype(jnp.float32)).astype(x.dtype)

def layer_norm(x, g, b):
    xf = x.astype(jnp.float32)
    mu = jnp.mean(xf, axis=-1, keepdims=True)
    var = jnp.mean(jnp.square(xf - mu), axis=-1, keepdims=True)
    y = (xf - mu) * lax.rsqrt(var + EPS) * g.astype(jnp.float32) + b.astype(jnp.float32)
    return y.astype(x.dtype)

def modulate(h, shift, scale):
    return h * (1 + scale) + shift

def axial_rope_tables(n_tok):
    rows = n_tok // GRID_W
    r = jnp.repeat(jnp.arange(rows, dtype=jnp.int32), GRID_W)
    col = jnp.tile(jnp.arange(GRID_W, dtype=jnp.int32), rows)
    n_freq = ROPE_DIM // 4
    freq = ROPE_THETA ** (-jnp.arange(n_freq, dtype=jnp.float32) / n_freq)
    ang = jnp.stack([r[:, None] * freq, col[:, None] * freq], axis=1)
    return jnp.cos(ang), jnp.sin(ang)

def apply_rope(x, cos, sin):
    shp = x.shape
    xr = x.reshape(shp[:-1] + (2, 2, ROPE_DIM // 4)).astype(jnp.float32)
    extra = x.ndim - 3
    c = cos.reshape(cos.shape[:1] + (1,) * extra + cos.shape[1:])
    s = sin.reshape(sin.shape[:1] + (1,) * extra + sin.shape[1:])
    x1, x2 = xr[..., 0, :], xr[..., 1, :]
    out = jnp.stack([x1 * c - x2 * s, x2 * c + x1 * s], axis=-2)
    return out.reshape(shp).astype(x.dtype)

def mla_queries(cq, q_norm_g, w_uq):
    b, n, _ = cq.shape
    q = (rms_norm_2(cq, q_norm_g) @ w_uq).reshape(b, n, N_HEADS, NOPE_DIM + ROPE_DIM)
    return q[..., :NOPE_DIM], q[..., NOPE_DIM:]

def mla_keys(kvr, kv_norm_g, w_ukv):
    b, n, _ = kvr.shape
    c_kv = rms_norm_2(kvr[..., :KV_RANK], kv_norm_g)
    kv = (c_kv @ w_ukv).reshape(b, n, N_HEADS, NOPE_DIM + V_DIM)
    return kv[..., :NOPE_DIM], kvr[..., KV_RANK:], kv[..., NOPE_DIM:]

def attend(qn, qr, kn, kr, v):
    s = jnp.einsum('bqhd,bkhd->bhqk', qn, kn) + jnp.einsum('bqhd,bkd->bhqk', qr, kr)
    p = jax.nn.softmax(s.astype(jnp.float32) * ATTN_SCALE, axis=-1).astype(v.dtype)
    return jnp.einsum('bhqk,bkhd->bqhd', p, v)

def attend_blocked(qn, qr, kn, kr, v):
    b, n = qn.shape[:2]
    nb = n // Q_BLOCK
    blk = lambda t: jnp.moveaxis(t.reshape((b, nb, Q_BLOCK) + t.shape[2:]), 1, 0)
    out = lax.map(lambda qs: attend(qs[0], qs[1], kn, kr, v), (blk(qn), blk(qr)))
    return jnp.moveaxis(out, 0, 1).reshape(b, n, N_HEADS, V_DIM)

def conformer_conv(u, conv_w, conv_b, ln_g, ln_b, w_pw):
    a, g = jnp.split(u, 2, axis=-1)
    y = a * jax.nn.sigmoid(g)
    y = lax.conv_general_dilated(y, conv_w[:, None, :], window_strides=(1,),
                                 padding=[(CONV_HALF, CONV_HALF)],
                                 dimension_numbers=('NWC', 'WIO', 'NWC'),
                                 feature_group_count=CONV_CH) + conv_b
    y = jax.nn.silu(layer_norm(y, ln_g, ln_b))
    return y @ w_pw

def merge_branches(u, attn_heads, conv_w, conv_b, ln_g, ln_b, w_pw, w_o_mla, w_out):
    b, n = attn_heads.shape[:2]
    y_a = attn_heads.reshape(b, n, N_HEADS * V_DIM) @ w_o_mla
    y_c = conformer_conv(u[..., OFF_CONV:OFF_GATE], conv_w, conv_b, ln_g, ln_b, w_pw)
    g = jax.nn.sigmoid(u[..., OFF_GATE:])
    return (g[..., :D_MODEL] * y_a + g[..., D_MODEL:] * y_c) @ w_out

def peer_ffn(h, w_pq, sub_keys, u_tab, v_tab):
    shp = h.shape
    toks = h.reshape(-1, P_CHUNK, D_MODEL)

    def chunk(xc):
        q = (xc @ w_pq).reshape(P_CHUNK, P_HEADS, 2, P_DK // 2)
        s = jnp.einsum('thpd,hpkd->thpk', q, sub_keys)
        s_top, i_top = lax.top_k(s, P_TOPK)
        cand = s_top[..., 0, :, None] + s_top[..., 1, None, :]
        best, ci = lax.top_k(cand.reshape(P_CHUNK, P_HEADS, P_TOPK * P_TOPK), P_TOPK)
        e1 = jnp.take_along_axis(i_top[..., 0, :], ci // P_TOPK, axis=-1)
        e2 = jnp.take_along_axis(i_top[..., 1, :], ci % P_TOPK, axis=-1)
        expert = e1 * N_KEYS + e2
        gate = jax.nn.softmax(best.astype(jnp.float32), axis=-1).astype(xc.dtype)
        act = jax.nn.gelu(jnp.einsum('thkd,td->thk', u_tab[expert], xc), approximate=False)
        return jnp.einsum('thk,thkd->td', gate * act, v_tab[expert])

    return lax.map(chunk, toks).reshape(shp)

def second_inputs(seed: int = 0) -> dict:
    key = jax.random.key(seed)
    ks = jax.random.split(key, 30)
    nrm = lambda k, s, sc: jax.random.normal(k, s, jnp.float32) * sc
    D = D_MODEL
    return {
        "x": nrm(ks[0], (BATCH, SEQ, D), 1.0),
        "c": nrm(ks[1], (BATCH, D), 1.0),
        "ctx": nrm(ks[2], (BATCH, CTX_LEN, D), 1.0),
        "c_ctx": nrm(ks[3], (D,), 1.0),
        "w_mod": nrm(ks[4], (DEPTH, D, 6 * D), 0.5 * D ** -0.5),
        "b_mod": nrm(ks[5], (DEPTH, 6 * D), 0.01),
        "norm1_g": 1.0 + nrm(ks[6], (DEPTH, D), 0.02),
        "norm2_g": 1.0 + nrm(ks[7], (DEPTH, D), 0.02),
        "w_in": nrm(ks[8], (DEPTH, D, N_IN), D ** -0.5),
        "q_norm_g": 1.0 + nrm(ks[9], (DEPTH, Q_RANK), 0.02),
        "w_uq": nrm(ks[10], (DEPTH, Q_RANK, N_HEADS * (NOPE_DIM + ROPE_DIM)), Q_RANK ** -0.5),
        "kv_norm_g": 1.0 + nrm(ks[11], (DEPTH, KV_RANK), 0.02),
        "w_ukv": nrm(ks[12], (DEPTH, KV_RANK, N_HEADS * (NOPE_DIM + V_DIM)), KV_RANK ** -0.5),
        "w_o_mla": nrm(ks[13], (DEPTH, N_HEADS * V_DIM, D), (N_HEADS * V_DIM) ** -0.5),
        "conv_w": nrm(ks[14], (DEPTH, CONV_WIDTH, CONV_CH), CONV_WIDTH ** -0.5),
        "conv_b": nrm(ks[15], (DEPTH, CONV_CH), 0.01),
        "conv_ln_g": 1.0 + nrm(ks[16], (DEPTH, CONV_CH), 0.02),
        "conv_ln_b": nrm(ks[17], (DEPTH, CONV_CH), 0.01),
        "w_pw": nrm(ks[18], (DEPTH, CONV_CH, D), CONV_CH ** -0.5),
        "w_out": nrm(ks[19], (DEPTH, D, D), D ** -0.5),
        "w_pq": nrm(ks[20], (DEPTH, D, P_HEADS * P_DK), D ** -0.5),
        "sub_keys": nrm(ks[21], (DEPTH, P_HEADS, 2, N_KEYS, P_DK // 2), (P_DK // 2) ** -0.5),
        "u_experts": nrm(ks[22], (DEPTH, N_EXPERTS, D), D ** -0.5),
        "v_experts": nrm(ks[23], (DEPTH, N_EXPERTS, D), 1.0),
        "final_g": 1.0 + nrm(ks[24], (D,), 0.02),
    }

def second_block(x, c, ctx, c_ctx, w_mod, b_mod, norm1_g, norm2_g, w_in, q_norm_g, w_uq,
              kv_norm_g, w_ukv, w_o_mla, conv_w, conv_b, conv_ln_g, conv_ln_b, w_pw,
              w_out, w_pq, sub_keys, u_experts, v_experts, final_g):
    n_lat = x.shape[1]
    cos, sin = axial_rope_tables(n_lat)
    for l in range(DEPTH):
        last = l == DEPTH - 1
        mod_lat = (jax.nn.silu(c) @ w_mod[l] + b_mod[l])[:, None, :]
        mod_ctx = jax.nn.silu(c_ctx) @ w_mod[l] + b_mod[l]
        sh1, sc1, g1, sh2, sc2, g2 = jnp.split(mod_lat, 6, axis=-1)
        csh1, csc1, cg1, csh2, csc2, cg2 = jnp.split(mod_ctx, 6, axis=-1)

        h = modulate(rms_norm_2(x, norm1_g[l]), sh1, sc1)
        u = h @ w_in[l]
        qn, qr = mla_queries(u[..., OFF_Q:OFF_KV], q_norm_g[l], w_uq[l])
        qr = apply_rope(qr, cos, sin)
        kn_l, kr_l, v_l = mla_keys(u[..., OFF_KV:OFF_CONV], kv_norm_g[l], w_ukv[l])
        kr_l = apply_rope(kr_l, cos, sin)

        hc = modulate(rms_norm_2(ctx, norm1_g[l]), csh1, csc1)
        if last:
            uc = hc @ w_in[l][:, OFF_KV:OFF_CONV]
            kvr_c = uc
        else:
            uc = hc @ w_in[l]
            kvr_c = uc[..., OFF_KV:OFF_CONV]
        kn_c, kr_c, v_c = mla_keys(kvr_c, kv_norm_g[l], w_ukv[l])

        kn = jnp.concatenate([kn_l, kn_c], axis=1)
        kr = jnp.concatenate([kr_l, kr_c], axis=1)
        vv = jnp.concatenate([v_l, v_c], axis=1)
        attn_lat = attend_blocked(qn, qr, kn, kr, vv)
        x = x + g1 * merge_branches(u, attn_lat, conv_w[l], conv_b[l], conv_ln_g[l],
                                    conv_ln_b[l], w_pw[l], w_o_mla[l], w_out[l])
        if not last:
            qn_c, qr_c = mla_queries(uc[..., OFF_Q:OFF_KV], q_norm_g[l], w_uq[l])
            attn_c = attend(qn_c, qr_c, kn_c, kr_c, v_c)
            ctx = ctx + cg1 * merge_branches(uc, attn_c, conv_w[l], conv_b[l], conv_ln_g[l],
                                             conv_ln_b[l], w_pw[l], w_o_mla[l], w_out[l])

        h2 = modulate(rms_norm_2(x, norm2_g[l]), sh2, sc2)
        x = x + g2 * peer_ffn(h2, w_pq[l], sub_keys[l], u_experts[l], v_experts[l])
        if not last:
            hc2 = modulate(rms_norm_2(ctx, norm2_g[l]), csh2, csc2)
            ctx = ctx + cg2 * peer_ffn(hc2, w_pq[l], sub_keys[l], u_experts[l], v_experts[l])
    return rms_norm_2(x, final_g)


def setup_inputs(seed=0):
    out = dict(first_inputs(seed))
    for name, value in second_inputs(seed + 1).items():
        if name != "x":
            out[name + "_2"] = value
    return out


def reference(
    x, meta_tokens, attn_norm_g, w_in, fox_forget_b, ret_norm_g, w_out, ffn_norm_g, w_up,
    conv_w, conv_b, w_down, final_norm_g, c_2, ctx_2, c_ctx_2, w_mod_2, b_mod_2, norm1_g_2,
    norm2_g_2, w_in_2, q_norm_g_2, w_uq_2, kv_norm_g_2, w_ukv_2, w_o_mla_2, conv_w_2, conv_b_2,
    conv_ln_g_2, conv_ln_b_2, w_pw_2, w_out_2, w_pq_2, sub_keys_2, u_experts_2, v_experts_2,
    final_g_2,
):
    x = first_block(
        x, meta_tokens, attn_norm_g, w_in, fox_forget_b, ret_norm_g, w_out, ffn_norm_g, w_up,
        conv_w, conv_b, w_down, final_norm_g,
    )
    return second_block(
        x, c_2, ctx_2, c_ctx_2, w_mod_2, b_mod_2, norm1_g_2, norm2_g_2, w_in_2, q_norm_g_2,
        w_uq_2, kv_norm_g_2, w_ukv_2, w_o_mla_2, conv_w_2, conv_b_2, conv_ln_g_2, conv_ln_b_2,
        w_pw_2, w_out_2, w_pq_2, sub_keys_2, u_experts_2, v_experts_2, final_g_2,
    )


_drawn_inputs = setup_inputs


def setup_inputs(seed=0):
    import zlib

    import numpy as np

    out = dict(_drawn_inputs(seed))
    spreads = {}
    factors = {'ret_norm_g': 3.005,
     'conv_b': 2.776,
     'ctx_2': 3.897,
     'norm1_g_2': 6.185,
     'q_norm_g_2': 8.0,
     'kv_norm_g_2': 8.0,
     'conv_b_2': 42.561,
     'conv_ln_g_2': 27.794,
     'conv_ln_b_2': 51.421,
     'final_g_2': 8.187,
     'norm2_g_2': 4.949}
    for name, (base, spread) in spreads.items():
        noise = np.random.default_rng([zlib.crc32(name.encode()), seed]).standard_normal(out[name].shape)
        drawn = base * np.exp(spread * noise) if base else spread * noise
        out[name] = __import__('jax').numpy.asarray(drawn.astype(out[name].dtype))
    for name, factor in factors.items():
        out[name] = (out[name] * factor).astype(out[name].dtype)
    return out
```

```python
from contextlib import ExitStack

import numpy as np

import concourse.bass as bass
from concourse import mybir
from concourse.alu_op_type import AluOpType as ALU

ACT = mybir.ActivationFunctionType
F32 = mybir.dt.float32
BF16 = mybir.dt.bfloat16
U32 = mybir.dt.uint32
AX_X = mybir.AxisListType.X

P = 128
SEQ, D = 512, 1024
KC = D // P
NT = SEQ // P
META, PREFIX = 16, 128
NK = META + SEQ
HALF = NK // 2
EPS = 1e-6
NEG = -1e30
RH, RDK, RDV, CHUNK = 4, 64, 128, 64
FH, FDH = 8, 64
F = 2816
NF = F // P
CTX = 256
NKV = SEQ + CTX
AH, NOPE, ROPE, VD = 16, 64, 32, 64
QK = NOPE + ROPE
TAPS = 31
PH, TOPK, NKEY = 8, 16, 128
NEXP = NKEY * NKEY
UNIT = 4096
BANK = 512

COLUMNS = dict(attn_g=KC, ret_g=RH, ffn_g=KC, conv_w=3 * NF, conv_b=NF, norm1_g=KC, q_g=2, kv_g=1,
               dw_w=TAPS * KC, dw_b=KC, ln_g=KC, ln_b=KC, cond=2 * KC)


def column_places():
    at, places = 0, {}
    for name, n in COLUMNS.items():
        places[name] = (at, at + n)
        at += n
    return places, at


class Sync:

    def __init__(self, nc, ctx):
        self.nc, self.ctx = nc, ctx
        self.engines = {"pe": nc.tensor, "dve": nc.vector, "act": nc.scalar, "pool": nc.gpsimd, "sp": nc.sync}
        self.sems, self.count, self.last = {}, {}, {}
        self.seen = {e: {} for e in self.engines}

    def mark(self, ins, name, by=1):
        if name not in self.sems:
            self.sems[name] = self.ctx.enter_context(self.nc.semaphore(name))
            self.count[name] = 0
        ins.then_inc(self.sems[name], by)
        self.count[name] += by
        token = (name, self.count[name])
        if by == 1:
            self.last[name.split("_")[0]] = token
        return token

    def need(self, engine, *tokens):
        for t in tokens:
            if t is None:
                continue
            if isinstance(t, list):
                self.need(engine, *t)
                continue
            name, value = t
            if self.seen[engine].get(name, 0) < value:
                self.seen[engine][name] = value
                self.engines[engine].wait_ge(self.sems[name], value)

    def fence(self, engines=("pe", "dve", "act", "pool", "sp")):
        for e in engines:
            self.need(e, *[t for who, t in self.last.items()])


class Ring:

    def __init__(self, buffers):
        self.buffers, self.free, self.at = buffers, [[] for _ in buffers], 0

    def take(self):
        i = self.at % len(self.buffers)
        self.at += 1
        free, self.free[i] = self.free[i], []
        return i, self.buffers[i], free


class Psum:

    def __init__(self, tensor):
        self.tensor, self.free, self.at, self.held = tensor, [[] for _ in range(8)], 0, set()

    def take(self, n=1):
        if n == 2 and self.at % 2:
            self.at += 1
        b = self.at % 8
        self.at += n
        free = sum(self.free[b:b + n], [])
        for k in range(b, b + n):
            self.free[k] = []
            assert k not in self.held
            self.held.add(k)
        return b, (self.tensor[:, b, :] if n == 1 else self.tensor[:, b:b + 2, :]), free

    def release(self, b, *tokens, n=1):
        for k in range(b, b + n):
            self.free[k] += tokens
            self.held.discard(k)


def program(nc, A, out):
    ctx = ExitStack()
    with ctx:
        S = Sync(nc, ctx)
        mark, need = S.mark, S.need
        pe, dve, act, pool, sp = nc.tensor, nc.vector, nc.scalar, nc.gpsimd, nc.sync

        def sb(stack, name, shape, dt=F32):
            return stack.enter_context(nc.sbuf_tensor(name, shape, dt))

        psum = Psum(ctx.enter_context(nc.psum_tensor("psum", [P, 8, BANK], F32)))

        ident = sb(ctx, "ident", [P, P])
        ident16 = sb(ctx, "ident16", [P, P], BF16)
        ones = sb(ctx, "ones", [P, P])
        eps = sb(ctx, "eps", [P, 1])
        places, n_columns = column_places()
        cols = sb(ctx, "cols", [P, n_columns])
        x = sb(ctx, "x", [P, NT, D])
        stat = sb(ctx, "stat", [P, 3, 8])

        def col(name, i=0, n=1):
            a = places[name][0] + i
            return cols[:, a:a + n]

        t_x = [mark(sp.dma_start(x[:, i, :], A["x"][i * P:(i + 1) * P, :]), f"ld_x{i}", 16) for i in range(NT)]
        t_const = [mark(act.dma_start(ident[:], A["ident"]), "ld_const", 16),
                   mark(act.dma_start(cols[:], A["cols"]), "ld_const", 16)][-1]
        t_ones = [mark(pool.memset(ones[:], 1.0), "pool_const"), mark(pool.memset(eps[:], EPS), "pool_const")][-1]
        need("dve", t_const)
        t_ident16 = mark(dve.tensor_copy(ident16[:], ident[:]), "dve_const")

        wring = Ring([sb(ctx, f"weights{i}", [P, UNIT]) for i in range(3)])

        def weights(name, unit, k, n):
            i, buffer, free = wring.take()
            need("sp", *free)
            view = buffer[:, 0:k * n]
            arrived = mark(sp.dma_start(view, A[name][unit][:, 0:k * n]), f"ld_weights{i}", 16)
            return view.rearrange("p (k n) -> p k n", k=k), arrived, wring.free[i]

        def chain(out_ap, pairs, name, start=True, stop=True):
            for k, (lhsT, rhs) in enumerate(pairs):
                last = pe.matmul(out_ap, lhsT, rhs, start=start and k == 0, stop=stop and k == len(pairs) - 1)
            return mark(last, name)

        def token_rstd(src, n, j, scratch, arrived, name):
            need("act", arrived, t_const, t_ones)
            t = mark(act.activation(scratch[0:n, :], src, ACT.Square, accum_out=stat[0:n, 0, j:j + 1]), f"act_{name}")
            need("act", t)
            t = mark(act.activation(stat[0:n, 1, j:j + 1], stat[0:n, 0, j:j + 1], ACT.Sqrt, bias=eps[0:n, :],
                                    scale=1.0 / D), f"act_{name}")
            need("dve", t)
            return mark(dve.reciprocal(stat[0:n, 2, j:j + 1], stat[0:n, 1, j:j + 1]), f"dve_{name}")

        def transposed(src, n_tiles, dst, scale, shift, name, ready, at=0):
            done = []
            for c in range(KC):
                b, bank, free = psum.take()
                need("pe", *free, t_const)
                for i in range(n_tiles):
                    need("pe", ready[i])
                    last = pe.transpose(bank[:, i * P:(i + 1) * P], src[:, i, c * P:(c + 1) * P], ident[:])
                t = mark(last, f"pe_{name}")
                o = dst[:, c, at:at + n_tiles * P]
                engine = "act" if c % 2 else "dve"
                need(engine, t)
                if engine == "act":
                    t = mark(act.activation(o, bank[:, 0:n_tiles * P], ACT.Identity, scale=scale[c],
                                            bias=shift[c] if shift else 0.0), f"act_{name}")
                elif shift:
                    t = mark(dve.tensor_scalar(o, bank[:, 0:n_tiles * P], scale[c], shift[c], ALU.mult, ALU.add), f"dve_{name}")
                else:
                    t = mark(dve.tensor_scalar(o, bank[:, 0:n_tiles * P], scale[c], None, ALU.mult), f"dve_{name}")
                psum.release(b, t)
                done.append(t)
            return done

        def meta_transposed(src, dst, gain, name, ready):
            b, bank, free = psum.take()
            need("pe", *free, ready)
            for c in range(KC):
                last = pe.transpose(bank[:, c * META:(c + 1) * META], src[:, c * P:(c + 1) * P], ident[0:META, 0:META])
            t = mark(last, f"pe_{name}")
            need("dve", t)
            t = mark(dve.tensor_tensor(dst[:, :, 0:META], bank[:, 0:KC * META].rearrange("p (c m) -> p c m", c=KC),
                                       gain.unsqueeze(2).to_broadcast([P, KC, META]), ALU.mult), f"dve_{name}")
            psum.release(b, t)
            return t

        def halves(ap):
            return ap.rearrange("p (a n) -> p a n", a=2)

        def project_halves(w, k0, n, src, name, ready, m=P):
            b, pair, free = psum.take(2)
            need("pe", *free, *ready)
            for a in range(2):
                t = chain(pair[0:m, a, 0:HALF], [(w[:, c, k0:k0 + m], src[:, c, a * HALF:(a + 1) * HALF])
                                                 for c in range(KC)], name)
            return b, pair[0:m, :, 0:HALF], t

        block1 = ctx.enter_context(ExitStack())
        mixer = ctx.enter_context(ExitStack())
        xm = sb(block1, "xm", [META, D])
        xnT = sb(mixer, "xnT", [P, KC, NK])
        mixedT = sb(mixer, "mixedT", [P, KC, NK])
        rv = sb(mixer, "rv", [P, NT + 1, RH * RDV])
        fv = sb(mixer, "fv", [P, NT + 1, FH * FDH])
        rqk = sb(mixer, "rqk", [P, 4, NK])
        fqk = sb(mixer, "fqk", [P, 8, NK])
        silu_rg = sb(mixer, "silu_rg", [P, RH, NK])
        t_xm = mark(sp.dma_start(xm[:], A["meta"]), "ld_meta", 16)

        first = ctx.enter_context(ExitStack())
        xn = sb(first, "xn", [P, NT, D])
        xnm = sb(first, "xnm", [META, D])
        scratch = sb(first, "scratch", [P, D])

        def normalise(name, t_src, t_src_m, meta=META):
            ready = []
            for i in range(NT):
                t = token_rstd(x[:, i, :], P, i, scratch, t_src[i], name)
                need("dve", t)
                ready.append(mark(dve.tensor_scalar(xn[:, i, :], x[:, i, :], stat[:, 2, i:i + 1], None, ALU.mult), f"dve_{name}"))
            t = token_rstd(xm[:], META, 4, scratch, t_src_m, name)
            need("dve", t)
            ready_m = mark(dve.tensor_scalar(xnm[:], xm[:], stat[0:META, 2, 4:5], None, ALU.mult), f"dve_{name}")
            return ready, ready_m

        ready, ready_m = normalise("norm1", t_x, t_xm)
        t_xnT = [meta_transposed(xnm[:], xnT, col("attn_g", 0, KC), "norm1", ready_m)]
        t_xnT += transposed(xn, NT, xnT, [col("attn_g", c) for c in range(KC)], None, "norm1", ready, META)
        S.fence()
        first.close()

        second = ctx.enter_context(ExitStack())
        raw = Ring([sb(second, f"raw{i}", [P, NK]) for i in range(2)])
        turned = Ring([sb(second, f"turned{i}", [P, NK]) for i in range(2)])
        tables = Ring([sb(second, f"rope{i}", [P, 2, NK]) for i in range(2)])
        swap = sb(second, "swap", [P, P])
        forget = sb(second, "forget", [FH, 4, NK])
        wff = sb(second, "wff", [P, KC, FH])
        fb = sb(second, "fb", [FH, 1])
        sel = sb(second, "sel", [FH, FH, P])
        t_small = [mark(act.dma_start(d, A[n]), "ld_mixer", 16) for d, n in
                   ((swap[:], "swap1"), (wff[:], "w_ff"), (fb[:], "fox_b"), (sel[:], "sel"))][-1]

        t_v = {}
        for unit, (dst, key) in enumerate(((rv, "rv"), (fv, "fv"))):
            w, arrived, free_w = weights("w_in_v", unit, KC, 512)
            need("pe", arrived, *t_xnT)
            for i in range(NT + 1):
                n, at = (P, META + i * P) if i < NT else (META, 0)
                b, bank, free = psum.take()
                need("pe", *free)
                t = chain(bank[0:n, :], [(xnT[:, c, at:at + n], w[:, c, :]) for c in range(KC)], "pe_values")
                need("act", t)
                t_v[key, i] = mark(act.activation(dst[0:n, i, :], bank[0:n, :], ACT.Copy), "act_values")
                psum.release(b, t_v[key, i])
            free_w.append(t)

        need("pe", t_small)
        b, pair, t = project_halves(wff, 0, FH, xnT, "pe_forget", t_xnT, FH)
        need("dve", t, t_small)
        z, e, m0, run = (forget[:, k, :] for k in range(4))
        t = mark(dve.tensor_scalar(halves(z), pair, fb[:, 0:1], None, ALU.add), "dve_forget")
        psum.release(b, t, n=2)
        need("dve", t)
        need("act", t)
        t2 = mark(act.activation(e, z, ACT.Abs), "act_forget")
        need("act", t2)
        t = mark(act.activation(e, e, ACT.Exp, scale=-1.0), "act_forget")
        need("act", t, t_ones)
        t = mark(act.activation(e, e, ACT.Ln, bias=ones[0:FH, 0:1]), "act_forget")
        t2 = mark(dve.tensor_scalar(m0, z, 0.0, None, ALU.min), "dve_forget")
        need("dve", t, t2)
        t = mark(dve.tensor_tensor(z, m0, e, ALU.subtract), "dve_forget")
        need("dve", t)
        t2 = mark(dve.memset(m0, 1.0), "dve_forget")
        need("dve", t, t2)
        t_run = mark(dve.tensor_tensor_scan(run, m0, z, 0.0, ALU.mult, ALU.add), "dve_forget")

        t_rqk = []
        w, arrived, free_w = weights("w_in_t", 0, KC, 512)
        for j in range(4):
            need("pe", arrived)
            b, pair, t = project_halves(w, j * P, P, xnT, "pe_rqk", [])
            r, rbuf, rfree = raw.take()
            need("act", t, *rfree)
            t_raw = mark(act.activation(halves(rbuf[:]), pair, ACT.Copy), "act_rqk")
            psum.release(b, t_raw, n=2)
            ti, table, tfree = tables.take()
            need("sp", *tfree)
            t_table = mark(sp.dma_start(table[:], A["rope1"][j]), f"ld_rope{ti}", 16)
            b, pair, free = psum.take(2)
            need("pe", *free, t_raw, t_small)
            for a in range(2):
                t = chain(pair[:, a, 0:HALF], [(swap[:], rbuf[:, a * HALF:(a + 1) * HALF])], "pe_rqk")
            need("dve", t_raw, t_table)
            u, ubuf, ufree = turned.take()
            need("dve", *ufree)
            t1 = mark(dve.tensor_tensor(rqk[:, j, :], rbuf[:], table[:, 0, :], ALU.mult), "dve_rqk")
            need("dve", t)
            t2 = mark(dve.tensor_tensor(halves(ubuf[:]), pair[:, :, 0:HALF], halves(table[:, 1, :]), ALU.mult), "dve_rqk")
            psum.release(b, t2, n=2)
            tables.free[ti] += [t1, t2]
            raw.free[r] += [t1, t]
            need("dve", t1, t2)
            t3 = mark(dve.tensor_tensor(rqk[:, j, :], rqk[:, j, :], ubuf[:], ALU.add), "dve_rqk")
            turned.free[u].append(t3)
            t_rqk.append(t3)
        free_w.append(t)

        w, arrived, free_w = weights("w_in_t", 1, KC, 512)
        t_rg = []
        for j in range(RH):
            need("pe", arrived)
            b, pair, t = project_halves(w, j * P, P, xnT, "pe_rg", [])
            need("act", t)
            t_rg.append(mark(act.activation(halves(silu_rg[:, j, :]), pair, ACT.Silu), "act_rg"))
            psum.release(b, t_rg[-1], n=2)
        free_w.append(t)

        t_fqk = []
        for unit in range(2):
            w, arrived, free_w = weights("w_in_t", 2 + unit, KC, 512)
            for j in range(4):
                need("pe", arrived)
                b, pair, t = project_halves(w, j * P, P, xnT, "pe_fqk", [])
                need("act", t)
                t_fqk.append(mark(act.activation(halves(fqk[:, 4 * unit + j, :]), pair, ACT.Copy,
                                                 scale=(FDH ** -0.5 if unit == 0 else 1.0)), "act_fqk"))
                psum.release(b, t_fqk[-1], n=2)
            free_w.append(t)

        diag = sb(second, "diag", [P, RH, P])
        causal16 = sb(second, "causal16", [P, P], BF16)
        causal = sb(second, "causal", [P, P])
        t_diag = [mark(act.dma_start(d, A[n]), "ld_diag", 16) for d, n in ((diag[:], "ret_diag"), (causal[:], "causal"))][-1]
        need("dve", t_diag)
        t_causal = mark(dve.tensor_copy(causal16[:], causal[:]), "dve_mask")
        scoresT = Ring([sb(second, f"scoresT{i}", [P, NT + 1, NK]) for i in range(1)])
        wide = Ring([sb(second, f"wide{i}", [P, NK]) for i in range(2)])

        def tiles():
            return [(NT, META, 0)] + [(j, P, META + j * P) for j in range(NT)]

        t_mixed = []
        for h in range(RH):
            rows = slice((h % 2) * RDK, (h % 2) * RDK + RDK)
            q, k = rqk[rows, h // 2, :], rqk[rows, 2 + h // 2, :]
            si, sT, sfree = scoresT.take()
            t_scores = []
            for j, n, at in tiles():
                b, pair, free = psum.take(2)
                need("pe", *free, *t_rqk)
                parts = []
                if j == NT:
                    for a in range(2):
                        t = chain(pair[0:n, a, 0:HALF], [(k[:, at:at + n], q[:, a * HALF:(a + 1) * HALF])], "pe_ret")
                    src, dst = pair[0:n, :, 0:HALF], halves(sT[0:n, j, :])
                else:
                    t = chain(pair[:, 0, 0:NK - at], [(k[:, at:at + n], q[:, at:NK])], "pe_ret")
                    src, dst = pair[:, 0, 0:NK - at], sT[:, j, at:NK]
                need("act", t, *sfree)
                t_copy = mark(act.activation(dst, src, ACT.Copy), "act_ret")
                need("dve", t_copy, t_diag)
                parts.append(mark(dve.tensor_tensor(sT[0:n, j, at:at + n], sT[0:n, j, at:at + n], diag[0:n, h, 0:n], ALU.mult), "dve_ret"))
                psum.release(b, t_copy, n=2)
                t_scores.append(parts)
            b, pair, free = psum.take(2)
            need("pe", *free)
            for (j, n, at), parts in list(zip(tiles(), t_scores))[1:] + [(tiles()[0], t_scores[0])]:
                need("pe", t_v["rv", j], *parts)
                v = rv[0:n, j, h * RDV:(h + 1) * RDV]
                if j == NT:
                    pe.matmul(pair[:, 1, 0:META], v, sT[0:n, j, 0:META], start=True, stop=True)
                    last = pe.matmul(pair[:, 0, 0:SEQ], v, sT[0:n, j, META:NK], start=False, stop=True)
                else:
                    pe.matmul(pair[:, 0, at - META:SEQ], v, sT[:, j, at:NK], start=j == 0, stop=False)
            t_o = mark(last, "pe_ret")
            scoresT.free[si].append(t_o)
            o = sb_o = wide.take()
            wi, obuf, ofree = o
            need("act", t_o, *ofree)
            mark(act.activation(obuf[:, META:NK], pair[:, 0, 0:SEQ], ACT.Copy), "act_ret")
            t_oc = mark(act.activation(obuf[:, 0:META], pair[:, 1, 0:META], ACT.Copy), "act_ret")
            psum.release(b, t_oc, n=2)
            r, sq, rfree = raw.take()
            need("act", t_oc, *rfree)
            t_sq = mark(act.activation(sq[:], obuf[:], ACT.Square), "act_ret")
            b, pair, free = psum.take(2)
            need("pe", *free, t_sq, t_ones)
            for a in range(2):
                t = chain(pair[:, a, 0:HALF], [(ones[:], sq[:, a * HALF:(a + 1) * HALF])], "pe_ret")
            u, root, ufree = turned.take()
            need("act", t, *ufree)
            t_root = mark(act.activation(halves(root[:]), pair[:, :, 0:HALF], ACT.Sqrt, bias=eps[:, :], scale=1.0 / RDV), "act_ret")
            psum.release(b, t_root, n=2)
            raw.free[r].append(t)
            need("dve", t_root)
            t = mark(dve.reciprocal(root[:], root[:]), "dve_ret")
            need("dve", t, t_oc)
            t = mark(dve.tensor_tensor(obuf[:], obuf[:], root[:], ALU.mult), "dve_ret")
            turned.free[u].append(t)
            need("dve", t, t_rg[h])
            t = mark(dve.scalar_tensor_tensor(mixedT[:, h, :], obuf[:], col("ret_g", h), silu_rg[:, h, :],
                                              ALU.mult, ALU.mult), "dve_ret")
            wide.free[wi].append(t)
            t_mixed.append(t)

        S.fence(("dve", "act", "pe"))
        third = ctx.enter_context(ExitStack())
        bias = Ring([raw.buffers[0], raw.buffers[1]])
        logits = Ring([wide.buffers[0], wide.buffers[1], turned.buffers[0], turned.buffers[1]])
        negmax = sb(third, "negmax", [P, 4, 4])
        pT = Ring([xnT[:, 0:NT + 1, :], scoresT.buffers[0]])
        small = Ring([negmax[:, i, :] for i in range(4)])
        for h in range(FH):
            rows = slice((h % 2) * FDH, (h % 2) * FDH + FDH)
            q, k = fqk[rows, h // 2, :], fqk[rows, 4 + h // 2, :]
            b, pair, free = psum.take(2)
            need("pe", *free, t_run, t_small)
            for a in range(2):
                t = chain(pair[:, a, 0:HALF], [(sel[:, h, :], run[:, a * HALF:(a + 1) * HALF])], "pe_bias")
            bi, negc, bfree = bias.take()
            need("act", t, *bfree)
            t_negc = mark(act.activation(halves(negc[:]), pair[:, :, 0:HALF], ACT.Copy, scale=-1.0), "act_fox")
            psum.release(b, t_negc, n=2)
            pi, pt, pfree = pT.take()
            t_pt = []
            for i, n, at in tiles():
                b, pair, free = psum.take(2)
                need("pe", *free, *t_fqk, t_causal)
                width = META if i == NT else at + P
                if i == NT:
                    pe.matmul(pair[0:n, 0, 0:n], q[:, 0:n], k[:, 0:n], start=True, stop=False)
                    last = pe.matmul(pair[0:n, 0, 0:n], ident16[0:n, 0:n], causal16[0:n, 0:n], start=False, stop=True)
                    view, shape = pair[0:n, 0, 0:n], (lambda ap: ap)
                elif width <= BANK:
                    pe.matmul(pair[:, 0, 0:width], q[:, at:at + n], k[:, 0:width], start=True, stop=True)
                    last = pe.matmul(pair[:, 0, at:width], ident16[:], causal16[:], start=False, stop=True, skip_group_check=True)
                    view, shape = pair[:, 0, 0:width], (lambda ap: ap)
                else:
                    pe.matmul(pair[:, 0, 0:HALF], q[:, at:at + n], k[:, 0:HALF], start=True, stop=True)
                    pe.matmul(pair[:, 1, 0:HALF], q[:, at:at + n], k[:, HALF:NK], start=True, stop=True)
                    last = pe.matmul(pair[:, 1, at - HALF:HALF], ident16[:], causal16[:], start=False, stop=True, skip_group_check=True)
                    view, shape = pair[:, :, 0:HALF], halves
                t = mark(last, "pe_fox")
                li, L, lfree = logits.take()
                ni, nm, nfree = small.take()
                need("dve", t, t_negc, *lfree, *nfree)
                t_max = mark(dve.tensor_tensor_reduce(shape(L[0:n, 0:width]), view, shape(negc[0:n, 0:width]), 1.0, NEG * 1e8,
                                                      ALU.add, ALU.max, nm[0:n, 0:1]), "dve_fox")
                psum.release(b, t_max, n=2)
                if i == NT - 1:
                    bias.free[bi].append(t_max)
                need("dve", t_max)
                t = mark(dve.tensor_scalar(nm[0:n, 1:2], nm[0:n, 0:1], -1.0, None, ALU.mult), "dve_fox")
                need("act", t, t_max)
                t = mark(act.activation(L[0:n, 0:width], L[0:n, 0:width], ACT.Exp, bias=nm[0:n, 1:2],
                                        accum_out=nm[0:n, 2:3]), "act_fox")
                need("dve", t)
                t = mark(dve.reciprocal(nm[0:n, 3:4], nm[0:n, 2:3]), "dve_fox")
                need("dve", t)
                t_p = mark(dve.tensor_scalar(L[0:n, 0:width], L[0:n, 0:width], nm[0:n, 3:4], None, ALU.mult), "dve_fox")
                small.free[ni].append(t_p)
                if i == NT:
                    b, bank, free = psum.take()
                    need("pe", *free, t_p)
                    t = mark(pe.transpose(bank[0:n, 0:n], L[0:n, 0:n], ident[0:n, 0:n]), "pe_fox")
                    need("act", t, *pfree)
                    t_pt.append(mark(act.activation(pt[0:n, NT, 0:n], bank[0:n, 0:n], ACT.Copy), "act_fox"))
                    psum.release(b, t_pt[-1])
                    logits.free[li].append(t)
                else:
                    b, pair, free = psum.take(2)
                    need("pe", *free, t_p)
                    t_m = mark(pe.transpose(pair[0:META, 1, 0:P], L[:, 0:META], ident[:]), "pe_fox")
                    bank = pair[:, 0, :]
                    for j in range(i + 1):
                        last = pe.transpose(bank[:, j * P:(j + 1) * P], L[:, META + j * P:META + (j + 1) * P], ident[:])
                    t = mark(last, "pe_fox")
                    need("dve", t_m, *pfree)
                    t_pt.append(mark(dve.tensor_copy(pt[0:META, NT, at:at + P], pair[0:META, 1, 0:P]), "dve_fox"))
                    psum.release(b + 1, t_pt[-1])
                    logits.free[li].append(t)
                    need("act", t, *pfree)
                    t_pt.append(mark(act.activation(pt[:, 0:i + 1, at:at + P],
                                                    bank[:, 0:(i + 1) * P].rearrange("p (j t) -> p j t", t=P), ACT.Copy), "act_fox"))
                    psum.release(b, t_pt[-1])
            b, pair, free = psum.take(2)
            need("pe", *free, *t_pt)
            for j, n, at in tiles()[1:] + tiles()[:1]:
                need("pe", t_v["fv", j])
                v = fv[0:n, j, h * FDH:(h + 1) * FDH]
                if j == NT:
                    pe.matmul(pair[rows, 1, 0:META], v, pt[0:n, j, 0:META], start=True, stop=True)
                    last = pe.matmul(pair[rows, 0, 0:SEQ], v, pt[0:n, j, META:NK], start=False, stop=True)
                else:
                    pe.matmul(pair[rows, 0, at - META:SEQ], v, pt[:, j, at:NK], start=j == 0, stop=False)
            t = mark(last, "pe_fox")
            pT.free[pi].append(t)
            need("dve", t)
            mark(dve.tensor_copy(mixedT[rows, 4 + h // 2, META:NK], pair[rows, 0, 0:SEQ]), "dve_fox")
            t_mixed.append(mark(dve.tensor_copy(mixedT[rows, 4 + h // 2, 0:META], pair[rows, 1, 0:META]), "dve_fox"))
            psum.release(b, t_mixed[-1], n=2)

        t_x2 = [None] * (NT + 1)
        for half in range(2):
            w, arrived, free_w = weights("w_out", half, KC, 512)
            need("pe", arrived, *t_mixed)
            for i, n, at in tiles():
                b, bank, free = psum.take()
                need("pe", *free)
                t = chain(bank[0:n, :], [(mixedT[:, c, at:at + n], w[:, c, :]) for c in range(KC)], "pe_out")
                need("dve", t)
                dst = (xm[:, half * 512:(half + 1) * 512] if i == NT else x[:, i, half * 512:(half + 1) * 512])
                t_x2[i] = mark(dve.tensor_tensor(dst, dst, bank[0:n, :], ALU.add), "dve_out")
                psum.release(b, t_x2[i])
            free_w.append(t)
        S.fence()
        third.close()
        second.close()
        mixer.close()

        ffn = ctx.enter_context(ExitStack())
        LEAD = 2
        NA = LEAD + SEQ
        gT = sb(ffn, "gT", [P, NF, SEQ])
        xnT = sb(ffn, "xnT2", [P, KC, NK])
        xn = sb(ffn, "xn2", [P, NT, D])
        xnm = sb(ffn, "xnm2", [META, D])
        scratch = sb(ffn, "scratch2", [P, D])
        branch = Ring([sb(ffn, f"branch{i}", [P, NA]) for i in range(3)])
        acc = Ring([sb(ffn, f"acc{i}", [P, SEQ]) for i in range(3)])
        ready, ready_m = normalise("norm2", t_x2, t_x2[NT])
        t_xnT = [meta_transposed(xnm[:], xnT, col("ffn_g", 0, KC), "norm2", ready_m)]
        t_xnT += transposed(xn, NT, xnT, [col("ffn_g", c) for c in range(KC)], None, "norm2", ready, META)
        NAH = NA // 2
        for u in range(NF // 2):
            w, arrived, free_w = weights("w_up", u, KC, 512)
            need("pe", arrived, *t_xnT)
            for v in range(2):
                f = 2 * u + v
                b, pair, free = psum.take(2)
                need("pe", *free)
                for a in range(2):
                    at = META - LEAD + a * NAH
                    t = chain(pair[:, a, 0:NAH], [(w[:, c, v * P:(v + 1) * P], xnT[:, c, at:at + NAH]) for c in range(KC)], "pe_up")
                bi, abuf, bfree = branch.take()
                need("act", t, *bfree)
                t_a = mark(act.activation(abuf[:].rearrange("p (a n) -> p a n", a=2), pair[:, :, 0:NAH], ACT.Copy), "act_up")
                psum.release(b, t_a, n=2)
                ai, cbuf, afree = acc.take()
                need("dve", t_a, *afree)
                t = mark(dve.tensor_scalar(cbuf[:], abuf[:, 0:SEQ], col("conv_w", f), col("conv_b", f), ALU.mult, ALU.add), "dve_up")
                for j in range(1, 3):
                    need("dve", t)
                    t = mark(dve.scalar_tensor_tensor(cbuf[:], abuf[:, j:j + SEQ], col("conv_w", j * NF + f), cbuf[:],
                                                      ALU.mult, ALU.add), "dve_up")
                branch.free[bi].append(t)
                need("act", t)
                t_s = mark(act.activation(cbuf[:], cbuf[:], ACT.Silu), "act_up")
                b, bank, free = psum.take()
                need("pe", *free)
                t = chain(bank[:, :], [(w[:, c, 256 + v * P:256 + (v + 1) * P], xnT[:, c, META:NK]) for c in range(KC)], "pe_up")
                need("dve", t, t_s)
                t_g = mark(dve.tensor_tensor(gT[:, f, :], bank[:, :], cbuf[:], ALU.mult), "dve_up")
                psum.release(b, t_g)
                acc.free[ai].append(t_g)
            free_w.append(t)
        t_x3 = [None] * NT
        splits = [(0, 8), (8, 16), (16, NF)]
        for half in range(2):
            banks = [psum.take() for _ in range(NT)]
            for s, (f0, f1) in enumerate(splits):
                w, arrived, free_w = weights("w_down", half * len(splits) + s, f1 - f0, 512)
                need("pe", arrived, t_g)
                for i in range(NT):
                    need("pe", *banks[i][2])
                    t = chain(banks[i][1][:, :], [(gT[:, f, i * P:(i + 1) * P], w[:, f - f0, :]) for f in range(f0, f1)],
                              "pe_down", start=s == 0, stop=s == len(splits) - 1)
                    if s == len(splits) - 1:
                        need("dve", t)
                        dst = x[:, i, half * 512:(half + 1) * 512]
                        t_x3[i] = mark(dve.tensor_tensor(dst, dst, banks[i][1][:, :], ALU.add), "dve_down")
                        psum.release(banks[i][0], t_x3[i])
                free_w.append(t)
        S.fence()
        ffn.close()
        block1.close()

        block2 = ctx.enter_context(ExitStack())
        merged = sb(block2, "merged", [P, KC, SEQ])
        sig_a = sb(block2, "sig_a", [P, KC, SEQ])
        latent = sb(block2, "latent", [P, 2 * SEQ + 2 * NKV])
        cq = latent[:, 0:2 * SEQ].rearrange("p (k n) -> p k n", k=2)
        ckv = latent[:, 2 * SEQ:2 * SEQ + NKV]
        kr = latent[:, 2 * SEQ + NKV:]
        silu_c = sb(block2, "silu_c", [P, KC, 2])
        modrow = Ring([sb(block2, f"modrow{i}", [2, 512]) for i in range(1)])
        modbias = Ring([sb(block2, f"modbias{i}", [2, 512]) for i in range(1)])
        swap2 = sb(block2, "swap2", [P, P])
        rope2 = sb(block2, "rope2", [P, 2, SEQ])
        t_rope2 = [mark(act.dma_start(d, A[n]), "ld_rope2", 16) for d, n in ((swap2[:], "swap2"), (rope2[:], "rope2"))][-1]

        pre = ctx.enter_context(ExitStack())
        hT = sb(pre, "hT", [P, KC, SEQ])
        hcT = sb(pre, "hcT", [P, KC, CTX])
        modc = sb(pre, "modc", [P, 16, 2])
        gain1 = sb(pre, "gain1", [P, 2, KC])
        norm = ctx.enter_context(ExitStack())
        xn = sb(norm, "xn3", [P, NT, D])
        ctxn = sb(norm, "ctxn", [P, 2, D])
        scratch = sb(norm, "scratch3", [P, D])
        final1 = sb(norm, "final1", [P, D])
        t_ctx = mark(act.dma_start(ctxn[:], A["ctx"]), "ld_ctx", 16)
        t_final1 = mark(act.dma_start(final1[:], A["final1"]), "ld_final1", 16)

        t_silu_c = mark(act.activation(silu_c[:].rearrange("p k t -> p (k t)"), col("cond", 0, 2 * KC), ACT.Silu), "act_mod")

        def mod_unit(u):
            bi, brow, bfree = modbias.take()
            need("act", *bfree)
            t_b = mark(act.dma_start(brow[:], A["b_mod"][u]), f"ld_modbias{bi}", 16)
            w, arrived, free_w = weights("w_mod", u, KC, 512)
            b, bank, free = psum.take()
            need("pe", *free, arrived, t_silu_c)
            t = chain(bank[0:2, :], [(silu_c[:, c, :], w[:, c, :]) for c in range(KC)], "pe_mod")
            free_w.append(t)
            ri, row, rfree = modrow.take()
            need("dve", t, t_b, *rfree)
            t = mark(dve.tensor_tensor(row[:], bank[0:2, :], brow[:], ALU.add), "dve_mod")
            psum.release(b, t)
            modbias.free[bi].append(t)
            return ri, row, t

        for u in range(4):
            ri, row, t_row = mod_unit(u)
            b, bank, free = psum.take()
            need("pe", *free, t_row)
            for j in range(4):
                last = pe.transpose(bank[:, 2 * j:2 * j + 2], row[:, j * P:(j + 1) * P], ident[0:2, 0:2])
            t = mark(last, "pe_mod")
            modrow.free[ri].append(t)
            need("dve", t)
            t_modc = mark(dve.tensor_copy(modc[:, 4 * u:4 * u + 4, :].rearrange("p k t -> p (k t)"), bank[:, 0:8]), "dve_mod")
            psum.release(b, t_modc)
        need("dve", t_modc)
        for r in range(2):
            t_gain = mark(dve.scalar_tensor_tensor(gain1[:, r, :], modc[:, 8:16, r], 1.0, col("norm1_g", 0, KC),
                                                   ALU.add, ALU.mult), "dve_mod")

        ready = []
        for i in range(NT):
            t = token_rstd(x[:, i, :], P, i, scratch, t_x3[i], "norm3")
            need("dve", t, t_final1)
            t = mark(dve.scalar_tensor_tensor(x[:, i, :], x[:, i, :], stat[:, 2, i:i + 1], final1[:], ALU.mult, ALU.mult), "dve_norm3")
            t = token_rstd(x[:, i, :], P, i, scratch, t, "norm3")
            need("dve", t)
            ready.append(mark(dve.tensor_scalar(xn[:, i, :], x[:, i, :], stat[:, 2, i:i + 1], None, ALU.mult), "dve_norm3"))
        need("dve", t_ctx)
        ready_c = []
        for i in range(2):
            t = token_rstd(ctxn[:, i, :], P, 5 + i, scratch, t_ctx, "norm3")
            need("dve", t)
            ready_c.append(mark(dve.tensor_scalar(ctxn[:, i, :], ctxn[:, i, :], stat[:, 2, 5 + i:6 + i], None, ALU.mult), "dve_norm3"))
        need("act", t_gain)
        need("dve", t_gain)
        t_hT = transposed(xn, NT, hT, [gain1[:, 0, c:c + 1] for c in range(KC)], [modc[:, c, 0:1] for c in range(KC)], "norm3", ready)
        t_hcT = transposed(ctxn, 2, hcT, [gain1[:, 1, c:c + 1] for c in range(KC)], [modc[:, c, 1:2] for c in range(KC)], "norm3", ready_c)
        S.fence()
        norm.close()

        conv = ctx.enter_context(ExitStack())
        sig_c = sb(conv, "sig_c", [P, KC, SEQ])
        EDGE = TAPS // 2
        padded = sb(conv, "padded", [P, KC, SEQ + 2 * EDGE])
        sg = Ring([sb(conv, f"sg{i}", [P, SEQ]) for i in range(3)])
        mark(pool.memset(padded[:, :, 0:EDGE], 0.0), "pool_pad")
        t_pad = mark(pool.memset(padded[:, :, EDGE + SEQ:], 0.0), "pool_pad")
        need("dve", t_pad)
        t_conv = [None] * KC
        for u in range(4):
            w, arrived, free_w = weights("w_in2", 1 + u, KC, 512)
            need("pe", arrived, *t_hT)
            for v in range(2):
                k = 2 * u + v
                b, bank, free = psum.take()
                need("pe", *free)
                t = chain(bank[:, :], [(w[:, c, 256 + v * P:256 + (v + 1) * P], hT[:, c, :]) for c in range(KC)], "pe_glu")
                gi, gbuf, gfree = sg.take()
                need("act", t, *gfree)
                t_sg = mark(act.activation(gbuf[:], bank[:, :], ACT.Sigmoid), "act_glu")
                psum.release(b, t_sg)
                b, bank, free = psum.take()
                need("pe", *free)
                t = chain(bank[:, :], [(w[:, c, v * P:(v + 1) * P], hT[:, c, :]) for c in range(KC)], "pe_glu")
                need("dve", t, t_sg)
                t_y = mark(dve.tensor_tensor(padded[:, k, EDGE:EDGE + SEQ], bank[:, :], gbuf[:], ALU.mult), "dve_glu")
                psum.release(b, t_y)
                sg.free[gi].append(t_y)
            free_w.append(t)
            need("dve", t_y)
            pair_t = {}
            for j in range(TAPS):
                for k in (2 * u, 2 * u + 1):
                    src = padded[:, k, j:j + SEQ]
                    if j == 0:
                        pair_t[k] = mark(dve.tensor_scalar(merged[:, k, :], src, col("dw_w", k), col("dw_b", k), ALU.mult, ALU.add), "dve_conv")
                    else:
                        need("dve", pair_t[k])
                        pair_t[k] = mark(dve.scalar_tensor_tensor(merged[:, k, :], src, col("dw_w", j * KC + k), merged[:, k, :],
                                                                  ALU.mult, ALU.add), "dve_conv")
                    t_conv[k] = pair_t[k]

        w, arrived, free_w = weights("w_in2", 0, KC, 416)
        need("pe", arrived, *t_hcT)
        lat = {}
        for j in range(3):
            b, bank, free = psum.take()
            need("pe", *free)
            t = chain(bank[:, :], [(w[:, c, j * P:(j + 1) * P], hT[:, c, :]) for c in range(KC)], "pe_ckv")
            dst = cq[:, j, :] if j < 2 else ckv[:, 0:SEQ]
            need("act", t)
            lat[j] = mark(act.activation(dst, bank[:, :], ACT.Copy), "act_ckv")
            psum.release(b, lat[j])
        b, bank, free = psum.take()
        need("pe", *free)
        t = chain(bank[:, 0:CTX], [(w[:, c, 2 * P:3 * P], hcT[:, c, :]) for c in range(KC)], "pe_ckv")
        need("act", t)
        t_ckv = mark(act.activation(ckv[:, SEQ:NKV], bank[:, 0:CTX], ACT.Copy), "act_ckv")
        psum.release(b, t_ckv)
        R = slice(NOPE, QK)
        for src, n, at in ((hT, SEQ, 0), (hcT, CTX, SEQ)):
            b, bank, free = psum.take()
            need("pe", *free)
            t = chain(bank[R, 0:n], [(w[:, c, 3 * P:3 * P + ROPE], src[:, c, :]) for c in range(KC)], "pe_ckv")
            need("act", t)
            t_kr = mark(act.activation(kr[R, at:at + n], bank[R, 0:n], ACT.Copy), "act_ckv")
            psum.release(b, t_kr)
        free_w.append(t)
        b, bank, free = psum.take()
        need("pe", *free, t_kr, t_rope2)
        t = chain(bank[R, :], [(swap2[R, R], kr[R, 0:SEQ])], "pe_ckv")
        gi, gbuf, gfree = sg.take()
        need("dve", t, t_kr, t_rope2, *gfree)
        t1 = mark(dve.tensor_tensor(gbuf[R, :], bank[R, :], rope2[R, 1, :], ALU.mult), "dve_ckv")
        psum.release(b, t1)
        t2 = mark(dve.tensor_tensor(kr[R, 0:SEQ], kr[R, 0:SEQ], rope2[R, 0, :], ALU.mult), "dve_ckv")
        need("dve", t1, t2)
        t_kr = mark(dve.tensor_tensor(kr[R, 0:SEQ], kr[R, 0:SEQ], gbuf[R, :], ALU.add), "dve_ckv")
        sg.free[gi].append(t_kr)

        def feature_norm(views, n, rank, gains, name, ready):
            b, bank, free = psum.take()
            need("pe", *free, t_ones)
            for k, view in enumerate(views):
                gi, sq, gfree = sg.take()
                need("act", *gfree, *ready)
                t = mark(act.activation(sq[:, 0:n], view, ACT.Square), f"act_{name}")
                need("pe", t)
                t = mark(pe.matmul(bank[:, 0:n], ones[:], sq[:, 0:n], start=k == 0, stop=k == len(views) - 1), f"pe_{name}")
                sg.free[gi].append(t)
            gi, root, gfree = sg.take()
            need("act", t, *gfree)
            t = mark(act.activation(root[:, 0:n], bank[:, 0:n], ACT.Sqrt, bias=eps[:, :], scale=1.0 / rank), f"act_{name}")
            psum.release(b, t)
            need("dve", t, *ready)
            t = mark(dve.reciprocal(root[:, 0:n], root[:, 0:n]), f"dve_{name}")
            need("dve", t)
            for view, g in zip(views, gains):
                t = mark(dve.scalar_tensor_tensor(view, view, g, root[:, 0:n], ALU.mult, ALU.mult), f"dve_{name}")
            sg.free[gi].append(t)
            return t

        t_cq = feature_norm([cq[:, 0, :], cq[:, 1, :]], SEQ, 256, [col("q_g", 0), col("q_g", 1)], "cnorm", [lat[0], lat[1]])
        t_ckv1 = feature_norm([ckv[:, 0:SEQ]], SEQ, 128, [col("kv_g")], "cnorm", [lat[2]])
        t_ckv2 = feature_norm([ckv[:, SEQ:NKV]], CTX, 128, [col("kv_g")], "cnorm", [t_ckv])

        t_gate = {}
        for u in range(4):
            w, arrived, free_w = weights("w_in2", 5 + u, KC, 512)
            need("pe", arrived)
            for v in range(4):
                k = 4 * u + v
                b, bank, free = psum.take()
                need("pe", *free)
                t = chain(bank[:, :], [(w[:, c, v * P:(v + 1) * P], hT[:, c, :]) for c in range(KC)], "pe_gate")
                need("act", t)
                dst = sig_a[:, k, :] if k < KC else sig_c[:, k - KC, :]
                t_gate[k] = mark(act.activation(dst, bank[:, :], ACT.Sigmoid), "act_gate")
                psum.release(b, t_gate[k])
            free_w.append(t)

        b, bank, free = psum.take()
        need("pe", *free, *t_conv)
        t = chain(bank[:, :], [(ones[:], merged[:, k, :]) for k in range(KC)], "pe_ln")
        mi, mean, mfree = sg.take()
        need("act", t, *mfree)
        t_mean = mark(act.activation(mean[:], bank[:, :], ACT.Copy, scale=1.0 / D), "act_ln")
        psum.release(b, t_mean)
        b, bank, free = psum.take()
        need("pe", *free)
        t_cent = []
        for k in range(KC):
            need("dve", t_mean, t_conv[k])
            t_cent.append(mark(dve.tensor_tensor(merged[:, k, :], merged[:, k, :], mean[:], ALU.subtract), "dve_ln"))
        sg.free[mi].append(t_cent[-1])
        for k in range(KC):
            gi, sq, gfree = sg.take()
            need("act", *gfree, t_cent[k])
            t = mark(act.activation(sq[:], merged[:, k, :], ACT.Square), "act_ln")
            need("pe", t)
            t = mark(pe.matmul(bank[:, :], ones[:], sq[:], start=k == 0, stop=k == KC - 1), "pe_ln")
            sg.free[gi].append(t)
        gi, root, gfree = sg.take()
        need("act", t, *gfree)
        t = mark(act.activation(root[:], bank[:, :], ACT.Sqrt, bias=eps[:, :], scale=1.0 / D), "act_ln")
        psum.release(b, t)
        need("dve", t)
        t = mark(dve.reciprocal(root[:], root[:]), "dve_ln")
        need("dve", t)
        t_sw = []
        for k in range(KC):
            t = mark(dve.tensor_tensor(padded[:, k, 0:SEQ], merged[:, k, :], root[:], ALU.mult), "dve_ln")
            need("act", t)
            t_sw.append(mark(act.activation(padded[:, k, 0:SEQ], padded[:, k, 0:SEQ], ACT.Silu, scale=col("ln_g", k),
                                            bias=col("ln_b", k)), "act_ln"))
        for u in range(2):
            w, arrived, free_w = weights("w_pw", u, KC, 512)
            need("pe", arrived, *t_sw)
            for v in range(4):
                k = 4 * u + v
                b, bank, free = psum.take()
                need("pe", *free)
                t = chain(bank[:, :], [(w[:, c, v * P:(v + 1) * P], padded[:, c, 0:SEQ]) for c in range(KC)], "pe_pw")
                need("dve", t, t_gate[KC + k])
                t_m = mark(dve.tensor_tensor(merged[:, k, :], bank[:, :], sig_c[:, k, :], ALU.mult), "dve_pw")
                psum.release(b, t_m)
            free_w.append(t)
        S.fence()
        conv.close()
        pre.close()

        attn = ctx.enter_context(ExitStack())
        values = sb(attn, "values", [P, NKV // P, AH * VD])
        headsT = sb(attn, "headsT", [P, KC, SEQ])
        Qs = Ring([sb(attn, f"Qs{i}", [P, 4, SEQ]) for i in range(2)])
        Ks = Ring([sb(attn, f"Ks{i}", [P, 2, NKV]) for i in range(2)])
        probs = Ring([sb(attn, f"probs{i}", [P, NKV]) for i in range(2)])
        turn = Ring([sb(attn, f"turn{i}", [P, SEQ]) for i in range(2)])
        mstat = sb(attn, "mstat", [P, 4, 4])
        ms = Ring([mstat[:, i, :] for i in range(4)])
        wq, t_wq, free_wq = weights("w_uq", 0, 2, 1536)
        wkv, t_wkv, free_wkv = weights("w_ukv", 0, 1, 2048)
        lent, lent_buffer, lent_free = wring.take()
        probsT = Ring([sb(attn, "probsT0", [P, NKV // P, SEQ]),
                       lent_buffer[:, 0:NKV // P * SEQ].rearrange("p (j t) -> p j t", t=SEQ)])
        probsT.free[1] += lent_free
        t_under = []
        for buffer in Ks.buffers:
            for s in range(2):
                t_under.append(mark(pool.tensor_copy(buffer[R, s, :], kr[R, :]), "pool_kr"))
        need("pe", t_wkv, t_ckv1, t_ckv2)
        t_values = []
        for j in range(NKV // P):
            for half in range(2):
                b, bank, free = psum.take()
                need("pe", *free)
                t = chain(bank[:, :], [(ckv[:, j * P:(j + 1) * P], wkv[:, 0, 1024 + half * 512:1024 + (half + 1) * 512])], "pe_values2")
                need("act", t)
                t_values.append(mark(act.activation(values[:, j, half * 512:(half + 1) * 512], bank[:, :], ACT.Copy), "act_values2"))
                psum.release(b, t_values[-1])
        t_heads = []
        KH = NKV // 2

        def queries(g):
            qi, Q, qfree = Qs.take()
            need("pe", t_wq, t_cq)
            done = []
            for v in range(2):
                b, bank, free = psum.take()
                need("pe", *free)
                t = chain(bank[:, :], [(wq[:, c, (2 * g + v) * P:(2 * g + v + 1) * P], cq[:, c, :]) for c in range(2)], "pe_q")
                need("act", t, *qfree)
                mark(act.activation(Q[0:NOPE, 2 * v, :], bank[0:NOPE, :], ACT.Copy), "act_q")
                t = mark(act.activation(Q[0:NOPE, 2 * v + 1, :], bank[NOPE:P, :], ACT.Copy), "act_q")
                psum.release(b, t)
                done.append(t)
            b, bank, free = psum.take()
            need("pe", *free)
            t = chain(bank[:, :], [(wq[:, c, AH * NOPE + g * P:AH * NOPE + (g + 1) * P], cq[:, c, :]) for c in range(2)], "pe_q")
            ti, plain, tfree = turn.take()
            need("act", t, *tfree)
            t_plain = mark(act.activation(plain[:], bank[:, :], ACT.Copy), "act_q")
            psum.release(b, t_plain)
            b, bank, free = psum.take()
            need("pe", *free, t_plain)
            t = chain(bank[:, :], [(swap2[:], plain[:])], "pe_q")
            ui, cross, ufree = turn.take()
            need("dve", t, *ufree)
            t1 = mark(dve.tensor_tensor(cross[:], bank[:, :], rope2[:, 1, :], ALU.mult), "dve_q")
            psum.release(b, t1)
            t2 = mark(dve.tensor_tensor(plain[:], plain[:], rope2[:, 0, :], ALU.mult), "dve_q")
            need("dve", t1, t2, *qfree)
            for j in range(4):
                t = mark(dve.tensor_tensor(Q[R, j, :], plain[j * ROPE:(j + 1) * ROPE, :], cross[j * ROPE:(j + 1) * ROPE, :], ALU.add), "dve_q")
            done.append(t)
            turn.free[ti].append(t)
            turn.free[ui].append(t)
            return qi, Q, done

        def keys(p):
            ki, K, kfree = Ks.take()
            b, pair, free = psum.take(2)
            need("pe", *free)
            for a in range(2):
                t = chain(pair[:, a, 0:KH], [(wkv[:, 0, p * P:(p + 1) * P], ckv[:, a * KH:(a + 1) * KH])], "pe_k")
            need("act", t, *kfree)
            mark(act.activation(K[0:NOPE, 0, :].rearrange("p (a n) -> p a n", a=2), pair[0:NOPE, :, 0:KH], ACT.Copy), "act_k")
            t = mark(act.activation(K[0:NOPE, 1, :].rearrange("p (a n) -> p a n", a=2), pair[NOPE:P, :, 0:KH], ACT.Copy), "act_k")
            psum.release(b, t, n=2)
            return ki, K, t

        scale2 = QK ** -0.5
        for h in range(AH):
            if h % 4 == 0:
                qi, Q, t_Q = queries(h // 4)
            if h % 2 == 0:
                ki, K, t_K = keys(h // 2)
            pi, pt, pfree = probsT.take()
            t_pt = []
            for i in range(NT):
                b, pair, free = psum.take(2)
                need("pe", *free, *t_Q, t_K, *t_under)
                for a in range(2):
                    last = pe.matmul(pair[:, a, 0:KH], Q[0:QK, h % 4, i * P:(i + 1) * P], K[0:QK, h % 2, a * KH:(a + 1) * KH],
                                     start=True, stop=True)
                t_s = mark(last, "pe_scores2")
                mi, st, mfree = ms.take()
                need("dve", t_s, *mfree)
                t = mark(dve.tensor_reduce(st[:, 0:1], pair[:, :, 0:KH], mybir.AxisListType.XY, ALU.max), "dve_attn2")
                need("dve", t)
                t = mark(dve.tensor_scalar(st[:, 1:2], st[:, 0:1], -scale2, None, ALU.mult), "dve_attn2")
                li, L, lfree = probs.take()
                need("act", t, t_s, *lfree)
                t = mark(act.activation(L[:].rearrange("p (a n) -> p a n", a=2), pair[:, :, 0:KH], ACT.Exp, bias=st[:, 1:2],
                                        scale=scale2, accum_out=st[:, 2:3]), "act_attn2")
                psum.release(b, t, n=2)
                need("dve", t)
                t = mark(dve.reciprocal(st[:, 3:4], st[:, 2:3]), "dve_attn2")
                need("dve", t)
                t_p = mark(dve.tensor_scalar(L[:], L[:], st[:, 3:4], None, ALU.mult), "dve_attn2")
                ms.free[mi].append(t_p)
                b, pair, free = psum.take(2)
                need("pe", *free, t_p)
                for j in range(NKV // P):
                    last = pe.transpose(pair[:, j // 3, (j % 3) * P:(j % 3 + 1) * P], L[:, j * P:(j + 1) * P], ident[:])
                t = mark(last, "pe_attn2")
                probs.free[li].append(t)
                need("act", t, *pfree)
                t = mark(act.activation(pt[:, :, i * P:(i + 1) * P].rearrange("p (a j) t -> p a j t", a=2),
                                        pair[:, :, 0:KH].rearrange("p a (j t) -> p a j t", t=P), ACT.Copy), "act_attn2")
                psum.release(b, t, n=2)
                t_pt.append(t)
            rows = slice((h % 2) * VD, (h % 2) * VD + VD)
            b, bank, free = psum.take()
            need("pe", *free, *t_pt, *t_values)
            t = chain(bank[rows, :], [(values[:, j, h * VD:(h + 1) * VD], pt[:, j, :]) for j in range(NKV // P)], "pe_attn2")
            probsT.free[pi].append(t)
            if h % 4 == 3:
                Qs.free[qi].append(t)
            if h % 2 == 1:
                Ks.free[ki].append(t)
            need("dve", t)
            t_heads.append(mark(dve.tensor_copy(headsT[rows, h // 2, :], bank[rows, :]), "dve_heads"))
            psum.release(b, t_heads[-1])
        free_wq.append(t)
        free_wkv.append(t)
        wring.free[lent].append(t)

        for u in range(2):
            w, arrived, free_w = weights("w_o_mla", u, KC, 512)
            need("pe", arrived, *t_heads)
            for v in range(4):
                k = 4 * u + v
                b, bank, free = psum.take()
                need("pe", *free)
                t = chain(bank[:, :], [(w[:, c, v * P:(v + 1) * P], headsT[:, c, :]) for c in range(KC)], "pe_o")
                need("dve", t, t_gate[k])
                t1 = mark(dve.tensor_tensor(sig_a[:, k, :], bank[:, :], sig_a[:, k, :], ALU.mult), "dve_o")
                psum.release(b, t1)
                need("dve", t1, t_m)
                t_merged = mark(dve.tensor_tensor(merged[:, k, :], merged[:, k, :], sig_a[:, k, :], ALU.add), "dve_o")
            free_w.append(t)
        S.fence()
        attn.close()

        rest = ctx.enter_context(ExitStack())
        mod_rows = sb(rest, "mod_rows", [P, 4, D])
        rows_ = {name: mod_rows[:, k, :] for k, name in enumerate(("g1", "sh2", "sc2", "g2"))}
        h2 = sb(rest, "h2", [P, NT, D])
        final2 = sb(rest, "final2", [P, D])
        qT = sb(rest, "qT", [P, 2 * PH, SEQ])
        subkeys = sb(rest, "subkeys", [P, 2 * PH, NKEY])
        t_norm2 = mark(act.dma_start(final2[:], A["norm2_g"]), "ld_norm2", 16)
        t_sub = mark(act.dma_start(subkeys[:], A["sub_keys"]), "ld_sub", 16)
        for u in range(4, 12):
            ri, row, t_row = mod_unit(u)
            b, bank, free = psum.take()
            need("pe", *free, t_row)
            t = chain(bank[:, :], [(ones[0:1, :], row[0:1, :])], "pe_mod")
            modrow.free[ri].append(t)
            need("act", t)
            name = ("g1", "sh2", "sc2", "g2")[(u - 4) // 2]
            t_rows = mark(act.activation(rows_[name][:, (u % 2) * 512:(u % 2 + 1) * 512], bank[:, :], ACT.Copy), "act_mod")
            psum.release(b, t_rows)
        need("dve", t_rows, t_norm2)
        t_gain2 = mark(dve.scalar_tensor_tensor(rows_["sc2"], rows_["sc2"], 1.0, final2[:], ALU.add, ALU.mult), "dve_mod2")
        need("act", t_gain2)
        t_final2 = mark(act.dma_start(final2[:], A["final_g"]), "ld_final2", 16)
        t_x4 = [[] for _ in range(NT)]
        for half in range(2):
            cut = slice(half * 512, (half + 1) * 512)
            w, arrived, free_w = weights("w_out2", half, KC, 512)
            need("pe", arrived, t_merged)
            for i in range(NT):
                b, bank, free = psum.take()
                need("pe", *free)
                t = chain(bank[:, :], [(merged[:, c, i * P:(i + 1) * P], w[:, c, :]) for c in range(KC)], "pe_out2")
                need("dve", t, t_rows)
                t1 = mark(dve.tensor_tensor(h2[:, i, cut], bank[:, :], rows_["g1"][:, cut], ALU.mult), "dve_out2")
                psum.release(b, t1)
                need("dve", t1)
                t_x4[i].append(mark(dve.tensor_tensor(x[:, i, cut], x[:, i, cut], h2[:, i, cut], ALU.add), "dve_out2"))
            free_w.append(t)
        S.fence()
        scratch, h2T = sig_a[:, 0:2, :].rearrange("p a n -> p (a n)"), merged
        ready = []
        for i in range(NT):
            t = token_rstd(x[:, i, :], P, i, scratch, t_x4[i], "norm4")
            need("dve", t, t_gain2)
            t = mark(dve.scalar_tensor_tensor(h2[:, i, :], x[:, i, :], stat[:, 2, i:i + 1], rows_["sc2"], ALU.mult, ALU.mult), "dve_norm4")
            need("dve", t)
            ready.append(mark(dve.tensor_tensor(h2[:, i, :], h2[:, i, :], rows_["sh2"], ALU.add), "dve_norm4"))
        t_h2T = transposed(h2, NT, h2T, [ones[:, 0:1]] * KC, None, "norm4", ready)
        t_qT = []
        for u in range(4):
            w, arrived, free_w = weights("w_pq", u, KC, 512)
            need("pe", arrived, *t_h2T)
            for v in range(4):
                b, bank, free = psum.take()
                need("pe", *free)
                t = chain(bank[:, :], [(w[:, c, v * P:(v + 1) * P], h2T[:, c, :]) for c in range(KC)], "pe_pq")
                need("act", t)
                t_qT.append(mark(act.activation(qT[:, 4 * u + v, :], bank[:, :], ACT.Copy), "act_pq"))
                psum.release(b, t_qT[-1])
            free_w.append(t)
        S.fence()
        peer = ctx.enter_context(ExitStack())
        GROUP = 4
        scores = mod_rows[:, 0:2, :].rearrange("p a (r k) -> p (a r) k", k=NKEY)
        left = latent[:, 0:2 * PH * NKEY].rearrange("p (r k) -> p r k", k=NKEY)
        top = sb(peer, "top", [P, 2 * PH, TOPK])
        topi = sb(peer, "topi", [P, 2 * PH, TOPK], U32)
        topf = sb(peer, "topf", [P, 2 * PH, TOPK])
        best = sb(peer, "best", [P, PH, TOPK])
        besti = sb(peer, "besti", [P, PH, TOPK], U32)
        part = sb(peer, "part", [P, 2, PH, TOPK], U32)
        partf = sb(peer, "partf", [P, 2, PH, TOPK])
        picked = sb(peer, "picked", [P, 2, PH, TOPK])
        expert = [sb(peer, f"expert{i}", [P, PH * TOPK], U32) for i in range(2)]
        gate = [sb(peer, f"gate{i}", [P, PH, TOPK]) for i in range(2)]
        gsum = sb(peer, "gsum", [P, 2, PH])
        count = sb(peer, "count", [P, TOPK])
        hidden = [sb(peer, f"hidden{i}", [P, PH * TOPK]) for i in range(2)]
        coef = [sb(peer, f"coef{i}", [P, PH * TOPK]) for i in range(2)]
        diags = Ring([mod_rows[:, 2, a:a + P] for a in range(0, D, P)])
        slots = Ring([b[:, a:a + 2 * D] for b in wring.buffers for a in (0, 2 * D)]
                     + [b[:, a:a + 4, :].rearrange("p a n -> p (a n)") for b in (merged, sig_a) for a in (0, 4)])
        t_count = mark(act.dma_start(count[:], A["count16"]), "ld_count", 16)
        cand = left.rearrange("p r k -> p (r k)").rearrange("p (h a b) -> p h a b", h=PH, a=TOPK)
        rest2 = scores.rearrange("p r k -> p (r k)").rearrange("p (h n) -> p h n", h=PH)
        cand_rows = left.rearrange("p r k -> p (r k)").rearrange("p (h n) -> p h n", h=PH)
        LOW = -3.0e38

        def top16(n, row, spare, values_, index, ready):
            need("dve", *ready)
            def each(step):
                return [mark(step(r), "dve_top") for r in range(n)]
            a = each(lambda r: dve.max(values_[:, r, 0:8], row(r)))
            for r in range(n):
                need("dve", a[r])
                mark(dve.max_index(index[:, r, 0:8], values_[:, r, 0:8], row(r)), "dve_top")
            b_ = each(lambda r: dve.match_replace(spare(r), values_[:, r, 0:8], row(r), LOW))
            need("dve", *b_)
            c_ = each(lambda r: dve.max(values_[:, r, 8:16], spare(r)))
            need("dve", *c_)
            return each(lambda r: dve.max_index(index[:, r, 8:16], values_[:, r, 8:16], spare(r)))

        scores_read = []

        def route(i):
            t_sc = []
            for u in range(4):
                b, bank, free = psum.take()
                need("pe", *free, t_sub, *t_qT)
                for v in range(4):
                    r = 4 * u + v
                    last = pe.matmul(bank[:, v * P:(v + 1) * P], qT[:, r, i * P:(i + 1) * P], subkeys[:, r, :], start=True, stop=True)
                t = mark(last, "pe_route")
                need("act", t, *scores_read)
                t_sc.append(mark(act.activation(scores[:, 4 * u:4 * u + 4, :].rearrange("p r k -> p (r k)"), bank[:, :], ACT.Copy), "act_route"))
                psum.release(b, t_sc[-1])
            t = top16(2 * PH, lambda r: scores[:, r, :], lambda r: left[:, r, :], top, topi, t_sc)
            need("dve", *t)
            by_head = top[:].rearrange("p (h a) k -> p h a k", a=2)
            t = mark(dve.tensor_tensor(cand, by_head[:, :, 0, :].unsqueeze(3).to_broadcast([P, PH, TOPK, TOPK]),
                                       by_head[:, :, 1, :].unsqueeze(2).to_broadcast([P, PH, TOPK, TOPK]), ALU.add), "dve_route")
            t = top16(PH, lambda r: cand_rows[:, r, :], lambda r: rest2[:, r, :], best, besti, [t])
            need("dve", *t)
            g, e = gate[i % 2], expert[i % 2]
            flat = lambda ap: ap.rearrange("p h k -> p (h k)")
            t1 = mark(dve.tensor_scalar(flat(part[:, 0]), flat(besti[:]), 4, None, ALU.logical_shift_right), "dve_route")
            t2 = mark(dve.tensor_scalar(flat(part[:, 1]), flat(besti[:]), 15, None, ALU.bitwise_and), "dve_route")
            need("dve", t1, t2)
            t1 = mark(dve.tensor_copy(partf[:].rearrange("p a h k -> p (a h k)"), part[:].rearrange("p a h k -> p (a h k)")), "dve_route")
            t2 = mark(dve.tensor_copy(flat(topf[:]), flat(topi[:])), "dve_route")
            need("dve", t1, t2, t_count)
            topf_h = topf[:].rearrange("p (h a) k -> p h a k", a=2)
            for a in range(2):
                hot = cand
                t = mark(dve.tensor_tensor(hot, partf[:, a].unsqueeze(3).to_broadcast([P, PH, TOPK, TOPK]),
                                           count[:].unsqueeze(1).unsqueeze(1).to_broadcast([P, PH, TOPK, TOPK]), ALU.is_equal), "dve_route")
                need("dve", t)
                t = mark(dve.tensor_tensor(hot, hot, topf_h[:, :, a, :].unsqueeze(2).to_broadcast([P, PH, TOPK, TOPK]), ALU.mult), "dve_route")
                need("dve", t)
                t = mark(dve.tensor_reduce(picked[:, a], hot, AX_X, ALU.add), "dve_route")
                need("dve", t)
            t_e = mark(dve.scalar_tensor_tensor(e[:], flat(picked[:, 0]), float(NKEY), flat(picked[:, 1]), ALU.mult, ALU.add), "dve_route")
            t = mark(dve.tensor_tensor(g[:], best[:], best[:, :, 0:1].to_broadcast([P, PH, TOPK]), ALU.subtract), "dve_route")
            need("act", t)
            t = mark(act.activation(flat(g[:]), flat(g[:]), ACT.Exp), "act_route")
            need("dve", t)
            t = mark(dve.tensor_reduce(gsum[:, 0, :], g[:], AX_X, ALU.add), "dve_route")
            need("dve", t)
            t = mark(dve.reciprocal(gsum[:, 1, :], gsum[:, 0, :]), "dve_route")
            need("dve", t)
            t_g = mark(dve.tensor_tensor(g[:], g[:], gsum[:, 1, :].unsqueeze(2).to_broadcast([P, PH, TOPK]), ALU.mult), "dve_route")
            scores_read[:] = [t_g]
            return t_e, t_g

        routed = {0: route(0)}
        coef_read = [[], []]
        t_store = []
        for i in range(NT):
            t_e, t_g = routed[i]
            e, g, hid, cf = expert[i % 2], gate[i % 2], hidden[i % 2], coef[i % 2]
            ob, opair, ofree = psum.take(2)
            need("pe", *ofree)
            gathered = {}

            def gather(j):
                s, slot, free = slots.take()
                need("pool", t_e, *free)
                t = mark(pool.indirect_dma_start(slot, None, A["experts"], bass.IndirectOffsetOnAxis(ap=e[:, j:j + 1], axis=0)),
                         f"ld_slot{s}", 16)
                gathered[j] = (s, slot, t)

            for j0 in range(0, PH * TOPK, GROUP):
                for j in range(j0, j0 + GROUP):
                    gather(j)
                if j0 == 0:
                    need("dve", *coef_read[i % 2])
                for j in range(j0, j0 + GROUP):
                    s, slot, t = gathered[j]
                    need("dve", t)
                    t = mark(dve.tensor_tensor_reduce(slot[:, 0:D], slot[:, 0:D], h2[:, i, :], 1.0, 0.0, ALU.mult, ALU.add,
                                                      hid[:, j:j + 1]), "dve_hidden")
                need("act", t)
                t = mark(act.activation(cf[:, j0:j0 + GROUP], hid[:, j0:j0 + GROUP], ACT.Gelu), "act_gelu")
                need("dve", t, t_g)
                t = mark(dve.tensor_tensor(cf[:, j0:j0 + GROUP], cf[:, j0:j0 + GROUP], g[:].rearrange("p h k -> p (h k)")[:, j0:j0 + GROUP],
                                           ALU.mult), "dve_coef")
                need("act", t)
                for j in range(j0, j0 + GROUP):
                    s, slot, _ = gathered[j]
                    di, dg, dfree = diags.take()
                    need("act", *dfree)
                    t = mark(act.activation(dg, ident[:], ACT.Copy, scale=cf[:, j:j + 1]), "act_diag")
                    need("pe", t, gathered[j][2])
                    for half in range(2):
                        last = pe.matmul(opair[:, half, :], dg, slot[:, D + half * 512:D + (half + 1) * 512],
                                         start=j == 0, stop=j == PH * TOPK - 1)
                    t_acc = mark(last, "pe_peer")
                    slots.free[s].append(t_acc)
                    diags.free[di].append(t_acc)
                if j0 == 32 and i + 1 < NT:
                    routed[i + 1] = route(i + 1)
            coef_read[i % 2] = [t_acc]
            y = h2[:, i, :]
            need("dve", t_acc)
            t = mark(dve.tensor_tensor(y.rearrange("p (a n) -> p a n", a=2), opair, rows_["g2"].rearrange("p (a n) -> p a n", a=2), ALU.mult), "dve_last")
            psum.release(ob, t, n=2)
            need("dve", t)
            t = mark(dve.tensor_tensor(x[:, i, :], x[:, i, :], y, ALU.add), "dve_last")
            need("dve", t)
            t = token_rstd(x[:, i, :], P, i, y, t, "last")
            need("dve", t, t_final2)
            t = mark(dve.scalar_tensor_tensor(y, x[:, i, :], stat[:, 2, i:i + 1], final2[:], ALU.mult, ALU.mult), "dve_last")
            need("sp", t)
            t_store.append(mark(sp.dma_start(out[i * P:(i + 1) * P, :], y), "st_out", 16))
        need("sp", t_store[-1])
        peer.close()
        rest.close()
        block2.close()


def constants():
    c = {"ident": np.eye(P, dtype=np.float32)}
    n = np.arange(P)
    pos = (np.arange(NK) + PREFIX - META).astype(np.float64)
    half = RDK // 2
    inv = (1.0 / (np.float32(10000.0) ** (np.arange(half, dtype=np.float32) / np.float32(half)))).astype(np.float32)
    ang = (pos.astype(np.float32)[None, :] * inv[:, None]).astype(np.float32).astype(np.float64)
    cos, sin = np.cos(ang), np.sin(ang)
    log_g = np.log1p(-np.exp2(-5.0 - np.arange(RH)))
    rope1 = np.zeros((4, P, 2, NK))
    mid = pos.mean()
    for j in range(4):
        for s in range(2):
            h = 2 * (j % 2) + s
            decay = np.exp((pos - mid) * log_g[h]) if j < 2 else RDK ** -0.5 * np.exp((mid - pos) * log_g[h])
            for k in range(RDK):
                r = s * RDK + k
                rope1[j, r, 0] = cos[k % half] * decay
                rope1[j, r, 1] = (-sin[k] if k < half else sin[k - half]) * decay
    c["rope1"] = rope1.astype(np.float32)
    swap = np.zeros((P, P), np.float32)
    for b in range(P):
        swap[b + half if b % RDK < half else b - half, b] = 1
    c["swap1"] = swap
    d = n[:, None] - n[None, :]
    same = (n[:, None] // CHUNK) == (n[None, :] // CHUNK)
    c["ret_diag"] = np.stack([np.where(d <= 0, 1.0, np.where(same, np.exp(2.0 * d * log_g[h]), 0.0)) for h in range(RH)],
                             axis=1).astype(np.float32)
    c["causal"] = np.where(d >= 0, 0.0, NEG).astype(np.float32)
    c["sel"] = np.repeat(np.eye(FH, dtype=np.float32)[:, :, None], P, axis=2)
    nf = ROPE // 4
    freq = (np.float32(10000.0) ** (-np.arange(nf, dtype=np.float32) / np.float32(nf))).astype(np.float32)
    t = np.arange(SEQ)
    angle = np.stack([(t // 64)[:, None].astype(np.float32) * freq, (t % 64)[:, None].astype(np.float32) * freq], axis=1)
    angle = angle.astype(np.float32).astype(np.float64)
    rope2 = np.zeros((P, 2, SEQ))
    swap2 = np.zeros((P, P), np.float32)
    for r in range(P):
        a, b, f = (r % ROPE) // 16, (r % 16) // nf, r % nf
        rope2[r, 0] = np.cos(angle[:, a, f])
        rope2[r, 1] = np.sin(angle[:, a, f]) * (-1 if b == 0 else 1)
        swap2[r + nf if b == 0 else r - nf, r] = 1
    c["rope2"] = rope2.astype(np.float32)
    c["swap2"] = swap2
    c["count16"] = np.repeat(np.arange(TOPK, dtype=np.float32)[None], P, axis=0)
    return c


def units(w, pieces, k=KC):
    w3 = w.reshape(k, P, -1).transpose(1, 0, 2)
    out = np.zeros((len(pieces), P, UNIT), w.dtype)
    for u, ranges in enumerate(pieces):
        block = np.concatenate([w3[:, :, a:b] for a, b in ranges], axis=2)
        out[u, :, 0:block.shape[1] * block.shape[2]] = block.reshape(P, -1)
    return out


def plain(n):
    return [[(a, a + 512)] for a in range(0, n, 512)]


def arrange(i):
    f = {k: np.ascontiguousarray(v) for k, v in i.items()}
    a = dict(constants())
    a["x"] = f["x"][0]
    a["meta"] = f["meta_tokens"]
    w = f["w_in"][0]
    a["w_in_v"] = units(w, [[(512, 1024)], [(2560, 3072)]])
    a["w_in_t"] = units(w, [[(0, 512)], [(1024, 1536)], [(1536, 2048)], [(2048, 2560)]])
    a["w_ff"] = w[:, 3072:3080].reshape(KC, P, FH).transpose(1, 0, 2)
    a["fox_b"] = f["fox_forget_b"].reshape(FH, 1)
    a["w_out"] = units(f["w_out"][0], plain(D))
    a["w_up"] = units(f["w_up"][0], [[(256 * u, 256 * u + 256), (F + 256 * u, F + 256 * u + 256)] for u in range(NF // 2)])
    wd = f["w_down"][0]
    down = []
    for half in range(2):
        for f0, f1 in ((0, 8), (8, 16), (16, NF)):
            down.append(units(wd[f0 * P:f1 * P], [[(half * 512, half * 512 + 512)]], f1 - f0))
    a["w_down"] = np.concatenate(down)
    col = lambda v: v.reshape(-1, P).T
    cols = dict(attn_g=col(f["attn_norm_g"][0]), ret_g=col(f["ret_norm_g"][0]), ffn_g=col(f["ffn_norm_g"][0]),
                conv_w=col(f["conv_w"][0].reshape(-1)), conv_b=col(f["conv_b"][0]), norm1_g=col(f["norm1_g_2"][0]),
                q_g=col(f["q_norm_g_2"][0]), kv_g=col(f["kv_norm_g_2"][0]), dw_w=col(f["conv_w_2"][0].reshape(-1)),
                dw_b=col(f["conv_b_2"][0]), ln_g=col(f["conv_ln_g_2"][0]), ln_b=col(f["conv_ln_b_2"][0]),
                cond=np.stack([col(f["c_2"][0]), col(f["c_ctx_2"])], axis=2).reshape(P, -1))
    a["cols"] = np.concatenate([cols[k] for k in COLUMNS], axis=1)
    a["ctx"] = f["ctx_2"][0].reshape(2, P, D).transpose(1, 0, 2)
    rows = lambda v: np.repeat(v.reshape(1, D), P, axis=0)
    a["final1"], a["norm2_g"], a["final_g"] = rows(f["final_norm_g"]), rows(f["norm2_g_2"]), rows(f["final_g_2"])
    a["w_mod"] = units(f["w_mod_2"][0], plain(6 * D))
    a["b_mod"] = np.repeat(f["b_mod_2"][0].reshape(12, 1, 512), 2, axis=1)
    w = f["w_in_2"][0]
    conv0, gate0 = 416, 416 + 2 * D
    a["w_in2"] = units(w, [[(0, 416)]] + [[(conv0 + 256 * u, conv0 + 256 * u + 256),
                                          (conv0 + D + 256 * u, conv0 + D + 256 * u + 256)] for u in range(4)]
                       + [[(gate0 + 512 * u, gate0 + 512 * u + 512)] for u in range(4)])
    uq = f["w_uq_2"][0].reshape(256, AH, QK)
    uq = np.concatenate([uq[:, :, 0:NOPE].reshape(256, -1), uq[:, :, NOPE:].reshape(256, -1)], axis=1)
    a["w_uq"] = units(uq, [[(0, 1536)]], 2)
    ukv = f["w_ukv_2"][0].reshape(P, AH, NOPE + VD)
    ukv = np.concatenate([ukv[:, :, 0:NOPE].reshape(P, -1), ukv[:, :, NOPE:].reshape(P, -1)], axis=1)
    a["w_ukv"] = units(ukv, [[(0, 2048)]], 1)
    a["w_o_mla"] = units(f["w_o_mla_2"][0], plain(D))
    a["w_pw"] = units(f["w_pw_2"][0], plain(D))
    a["w_out2"] = units(f["w_out_2"][0], plain(D))
    a["w_pq"] = units(f["w_pq_2"][0], plain(2048))
    a["sub_keys"] = f["sub_keys_2"][0].reshape(2 * PH, NKEY, P).transpose(2, 0, 1)
    a["experts"] = np.concatenate([f["u_experts_2"][0], f["v_experts_2"][0]], axis=1)
    return {k: np.ascontiguousarray(v) for k, v in a.items()}


def kernel(**inputs):
    import concourse.bacc as bacc
    from concourse.bass_utils import run_bass_kernel_spmd

    nc = bacc.Bacc("TRN2", target_bir_lowering=False, num_devices=1)
    arrays = arrange(inputs)
    A = {name: nc.dram_tensor(f"in_{name}", a.shape, mybir.dt.from_np(a.dtype), kind="ExternalInput").ap()
         for name, a in arrays.items()}
    out = nc.dram_tensor("out_y", (SEQ, D), F32, kind="ExternalOutput").ap()
    program(nc, A, out)
    r = run_bass_kernel_spmd(nc, [{f"in_{name}": a for name, a in arrays.items()}], core_ids=[0])
    return r.results[0]["out_y"].reshape(1, SEQ, D)
```

```python
from contextlib import ExitStack

import numpy as np

import concourse.bass as bass
from concourse import mybir
from concourse.alu_op_type import AluOpType as ALU

ACT = mybir.ActivationFunctionType
F32 = mybir.dt.float32
BF16 = mybir.dt.bfloat16
U32 = mybir.dt.uint32
AX_X = mybir.AxisListType.X

P = 128
SEQ, D = 512, 1024
KC = D // P
NT = SEQ // P
META, PREFIX = 16, 128
NK = META + SEQ
HALF = NK // 2
EPS = 1e-6
NEG = -1e30
RH, RDK, RDV, CHUNK = 4, 64, 128, 64
FH, FDH = 8, 64
F = 2816
NF = F // P
CTX = 256
NKV = SEQ + CTX
AH, NOPE, ROPE, VD = 16, 64, 32, 64
QK = NOPE + ROPE
TAPS = 31
PH, TOPK, NKEY = 8, 16, 128
NEXP = NKEY * NKEY
UNIT = 4096
BANK = 512

COLUMNS = dict(attn_g=KC, ret_g=RH, ffn_g=KC, conv_w=3 * NF, conv_b=NF, norm1_g=KC, q_g=2, kv_g=1,
               dw_w=TAPS * KC, dw_b=KC, ln_g=KC, ln_b=KC, cond=2 * KC, b_mod=6 * KC)


def column_places():
    at, places = 0, {}
    for name, n in COLUMNS.items():
        places[name] = (at, at + n)
        at += n
    return places, at


class Sync:

    def __init__(self, nc, ctx):
        self.nc, self.ctx = nc, ctx
        self.engines = {"pe": nc.tensor, "dve": nc.vector, "act": nc.scalar, "pool": nc.gpsimd, "sp": nc.sync}
        self.sems, self.count, self.last = {}, {}, {}
        self.seen = {e: {} for e in self.engines}

    def mark(self, ins, name, by=1):
        if name not in self.sems:
            self.sems[name] = self.ctx.enter_context(self.nc.semaphore(name))
            self.count[name] = 0
        ins.then_inc(self.sems[name], by)
        self.count[name] += by
        token = (name, self.count[name])
        if by == 1:
            self.last[name.split("_")[0]] = token
        return token

    def need(self, engine, *tokens):
        for t in tokens:
            if t is None:
                continue
            if isinstance(t, list):
                self.need(engine, *t)
                continue
            name, value = t
            if self.seen[engine].get(name, 0) < value:
                self.seen[engine][name] = value
                self.engines[engine].wait_ge(self.sems[name], value)

    def fence(self, engines=("pe", "dve", "act", "pool", "sp")):
        for e in engines:
            self.need(e, *[t for who, t in self.last.items()])


class Ring:

    def __init__(self, buffers):
        self.buffers, self.free, self.at = buffers, [[] for _ in buffers], 0

    def take(self):
        i = self.at % len(self.buffers)
        self.at += 1
        free, self.free[i] = self.free[i], []
        return i, self.buffers[i], free


class Psum:

    def __init__(self, tensor):
        self.tensor, self.free, self.at, self.held = tensor, [[] for _ in range(8)], 0, set()

    def take(self, n=1):
        while self.at % n or any((self.at + k) % 8 in self.held for k in range(n)):
            self.at += 1
        b = self.at % 8
        self.at += n
        free = sum(self.free[b:b + n], [])
        for k in range(b, b + n):
            self.free[k] = []
            self.held.add(k)
        return b, (self.tensor[:, b, :] if n == 1 else self.tensor[:, b:b + 2, :]), free

    def release(self, b, *tokens, n=1):
        for k in range(b, b + n):
            self.free[k] += tokens
            self.held.discard(k)


def program(nc, A, out):
    ctx = ExitStack()
    with ctx:
        S = Sync(nc, ctx)
        mark, need = S.mark, S.need
        pe, dve, act, pool, sp = nc.tensor, nc.vector, nc.scalar, nc.gpsimd, nc.sync

        def sb(stack, name, shape, dt=F32):
            return stack.enter_context(nc.sbuf_tensor(name, shape, dt))

        psum = Psum(ctx.enter_context(nc.psum_tensor("psum", [P, 8, BANK], F32)))

        ident = sb(ctx, "ident", [P, P])
        ident16 = sb(ctx, "ident16", [P, P], BF16)
        ones = sb(ctx, "ones", [P, P])
        eps = sb(ctx, "eps", [P, 1])
        places, n_columns = column_places()
        cols = sb(ctx, "cols", [P, n_columns])
        x = sb(ctx, "x", [P, NT, D])
        spare_row = sb(ctx, "spare_row", [P, D])
        stat = sb(ctx, "stat", [P, 3, 8])

        def col(name, i=0, n=1):
            a = places[name][0] + i
            return cols[:, a:a + n]

        t_x = [mark(sp.dma_start(x[:, i, :], A["x"][i * P:(i + 1) * P, :]), f"ld_x{i}", 16) for i in range(NT)]
        t_const = [mark(act.dma_start(ident[:], A["ident"]), "ld_const", 16),
                   mark(act.dma_start(cols[:], A["cols"]), "ld_const", 16)][-1]
        t_ones = [mark(pool.memset(ones[:], 1.0), "pool_const"), mark(pool.memset(eps[:], EPS), "pool_const")][-1]
        need("dve", t_const)
        t_ident16 = mark(dve.tensor_copy(ident16[:], ident[:]), "dve_const")

        wring = Ring([sb(ctx, f"weights{i}", [P, UNIT]) for i in range(3)])

        def weights(name, unit, k, n):
            i, buffer, free = wring.take()
            need("sp", *free)
            view = buffer[:, 0:k * n]
            arrived = mark(sp.dma_start(view, A[name][unit][:, 0:k * n]), f"ld_weights{i}", 16)
            return view.rearrange("p (k n) -> p k n", k=k), arrived, wring.free[i]

        def chain(out_ap, pairs, name, start=True, stop=True):
            for k, (lhsT, rhs) in enumerate(pairs):
                last = pe.matmul(out_ap, lhsT, rhs, start=start and k == 0, stop=stop and k == len(pairs) - 1)
            return mark(last, name)

        def token_rstd(src, n, j, scratch, arrived, name):
            need("act", arrived, t_const, t_ones)
            t = mark(act.activation(scratch[0:n, :], src, ACT.Square, accum_out=stat[0:n, 0, j:j + 1]), f"act_{name}")
            need("act", t)
            t = mark(act.activation(stat[0:n, 1, j:j + 1], stat[0:n, 0, j:j + 1], ACT.Sqrt, bias=eps[0:n, :],
                                    scale=1.0 / D), f"act_{name}")
            need("dve", t)
            return mark(dve.reciprocal(stat[0:n, 2, j:j + 1], stat[0:n, 1, j:j + 1]), f"dve_{name}")

        def transposed(src, n_tiles, dst, scale, shift, name, ready, at=0):
            done = []
            for c in range(KC):
                b, bank, free = psum.take()
                need("pe", *free, t_const)
                for i in range(n_tiles):
                    need("pe", ready[i])
                    last = pe.transpose(bank[:, i * P:(i + 1) * P], src[:, i, c * P:(c + 1) * P], ident[:])
                t = mark(last, f"pe_{name}")
                o = dst[:, c, at:at + n_tiles * P]
                engine = "act" if c % 2 else "dve"
                need(engine, t)
                if engine == "act":
                    t = mark(act.activation(o, bank[:, 0:n_tiles * P], ACT.Identity, scale=scale[c],
                                            bias=shift[c] if shift else 0.0), f"act_{name}")
                elif shift:
                    t = mark(dve.tensor_scalar(o, bank[:, 0:n_tiles * P], scale[c], shift[c], ALU.mult, ALU.add), f"dve_{name}")
                else:
                    t = mark(dve.tensor_scalar(o, bank[:, 0:n_tiles * P], scale[c], None, ALU.mult), f"dve_{name}")
                psum.release(b, t)
                done.append(t)
            return done

        def meta_transposed(src, dst, gain, name, ready):
            b, bank, free = psum.take()
            need("pe", *free, ready)
            for c in range(KC):
                last = pe.transpose(bank[:, c * META:(c + 1) * META], src[:, c * P:(c + 1) * P], ident[0:META, 0:META])
            t = mark(last, f"pe_{name}")
            need("dve", t)
            t = mark(dve.tensor_tensor(dst[:, :, 0:META], bank[:, 0:KC * META].rearrange("p (c m) -> p c m", c=KC),
                                       gain.unsqueeze(2).to_broadcast([P, KC, META]), ALU.mult), f"dve_{name}")
            psum.release(b, t)
            return t

        def halves(ap):
            return ap.rearrange("p (a n) -> p a n", a=2)

        def project_halves(w, k0, n, src, name, ready, m=P):
            b, pair, free = psum.take(2)
            need("pe", *free, *ready)
            for a in range(2):
                t = chain(pair[0:m, a, 0:HALF], [(w[:, c, k0:k0 + m], src[:, c, a * HALF:(a + 1) * HALF])
                                                 for c in range(KC)], name)
            return b, pair[0:m, :, 0:HALF], t

        mixer = ctx.enter_context(ExitStack())
        xm = spare_row[0:META, :]
        xnT = sb(mixer, "xnT", [P, KC, NK])
        mixedT = sb(mixer, "mixedT", [P, KC, NK])
        rv = sb(mixer, "rv", [P, NT + 1, RH * RDV])
        fv = sb(mixer, "fv", [P, NT + 1, FH * FDH])
        rqk = sb(mixer, "rqk", [P, 4, NK])
        fqk = sb(mixer, "fqk", [P, 8, NK])
        silu_rg = sb(mixer, "silu_rg", [P, RH, NK])
        t_xm = mark(sp.dma_start(xm[:], A["meta"]), "ld_meta", 16)

        first = ctx.enter_context(ExitStack())
        xn = sb(first, "xn", [P, NT, D])
        xnm = sb(first, "xnm", [META, D])
        scratch = sb(first, "scratch", [P, D])

        def normalise(name, t_src, t_src_m, meta=META):
            ready = []
            for i in range(NT):
                t = token_rstd(x[:, i, :], P, i, scratch, t_src[i], name)
                need("dve", t)
                ready.append(mark(dve.tensor_scalar(xn[:, i, :], x[:, i, :], stat[:, 2, i:i + 1], None, ALU.mult), f"dve_{name}"))
            t = token_rstd(xm[:], META, 4, scratch, t_src_m, name)
            need("dve", t)
            ready_m = mark(dve.tensor_scalar(xnm[:], xm[:], stat[0:META, 2, 4:5], None, ALU.mult), f"dve_{name}")
            return ready, ready_m

        ready, ready_m = normalise("norm1", t_x, t_xm)
        t_xnT = [meta_transposed(xnm[:], xnT, col("attn_g", 0, KC), "norm1", ready_m)]
        t_xnT += transposed(xn, NT, xnT, [col("attn_g", c) for c in range(KC)], None, "norm1", ready, META)
        S.fence()
        first.close()

        second = ctx.enter_context(ExitStack())
        raw = Ring([sb(second, f"raw{i}", [P, NK]) for i in range(2)])
        turned = Ring([sb(second, f"turned{i}", [P, NK]) for i in range(2)])
        tables = Ring([sb(second, f"rope{i}", [P, 2, NK]) for i in range(2)])
        swap = sb(second, "swap", [P, P])
        forget = sb(second, "forget", [FH, 4, NK])
        wff = sb(second, "wff", [P, KC, FH])
        fb = sb(second, "fb", [FH, 1])
        sel = sb(second, "sel", [FH, FH, P])
        t_small = [mark(act.dma_start(d, A[n]), "ld_mixer", 16) for d, n in
                   ((swap[:], "swap1"), (wff[:], "w_ff"), (fb[:], "fox_b"), (sel[:], "sel"))][-1]

        t_v = {}
        for unit, (dst, key) in enumerate(((rv, "rv"), (fv, "fv"))):
            w, arrived, free_w = weights("w_in_v", unit, KC, 512)
            need("pe", arrived, *t_xnT)
            for i in range(NT + 1):
                n, at = (P, META + i * P) if i < NT else (META, 0)
                b, bank, free = psum.take()
                need("pe", *free)
                t = chain(bank[0:n, :], [(xnT[:, c, at:at + n], w[:, c, :]) for c in range(KC)], "pe_values")
                need("act", t)
                t_v[key, i] = mark(act.activation(dst[0:n, i, :], bank[0:n, :], ACT.Copy), "act_values")
                psum.release(b, t_v[key, i])
            free_w.append(t)

        need("pe", t_small)
        b, pair, t = project_halves(wff, 0, FH, xnT, "pe_forget", t_xnT, FH)
        need("dve", t, t_small)
        z, e, m0, run = (forget[:, k, :] for k in range(4))
        t = mark(dve.tensor_scalar(halves(z), pair, fb[:, 0:1], None, ALU.add), "dve_forget")
        psum.release(b, t, n=2)
        need("dve", t)
        need("act", t)
        t2 = mark(act.activation(e, z, ACT.Abs), "act_forget")
        need("act", t2)
        t = mark(act.activation(e, e, ACT.Exp, scale=-1.0), "act_forget")
        need("act", t, t_ones)
        t = mark(act.activation(e, e, ACT.Ln, bias=ones[0:FH, 0:1]), "act_forget")
        t2 = mark(dve.tensor_scalar(m0, z, 0.0, None, ALU.min), "dve_forget")
        need("dve", t, t2)
        t = mark(dve.tensor_tensor(z, m0, e, ALU.subtract), "dve_forget")
        need("dve", t)
        t2 = mark(dve.memset(m0, 1.0), "dve_forget")
        need("dve", t, t2)
        t_run = mark(dve.tensor_tensor_scan(run, m0, z, 0.0, ALU.mult, ALU.add), "dve_forget")

        t_rqk = []
        w, arrived, free_w = weights("w_in_t", 0, KC, 512)
        for j in range(4):
            need("pe", arrived)
            b, pair, t = project_halves(w, j * P, P, xnT, "pe_rqk", [])
            r, rbuf, rfree = raw.take()
            need("act", t, *rfree)
            t_raw = mark(act.activation(halves(rbuf[:]), pair, ACT.Copy), "act_rqk")
            psum.release(b, t_raw, n=2)
            ti, table, tfree = tables.take()
            need("sp", *tfree)
            t_table = mark(sp.dma_start(table[:], A["rope1"][j]), f"ld_rope{ti}", 16)
            b, pair, free = psum.take(2)
            need("pe", *free, t_raw, t_small)
            for a in range(2):
                t = chain(pair[:, a, 0:HALF], [(swap[:], rbuf[:, a * HALF:(a + 1) * HALF])], "pe_rqk")
            need("dve", t_raw, t_table)
            u, ubuf, ufree = turned.take()
            need("dve", *ufree)
            t1 = mark(dve.tensor_tensor(rqk[:, j, :], rbuf[:], table[:, 0, :], ALU.mult), "dve_rqk")
            need("dve", t)
            t2 = mark(dve.tensor_tensor(halves(ubuf[:]), pair[:, :, 0:HALF], halves(table[:, 1, :]), ALU.mult), "dve_rqk")
            psum.release(b, t2, n=2)
            tables.free[ti] += [t1, t2]
            raw.free[r] += [t1, t]
            need("dve", t1, t2)
            t3 = mark(dve.tensor_tensor(rqk[:, j, :], rqk[:, j, :], ubuf[:], ALU.add), "dve_rqk")
            turned.free[u].append(t3)
            t_rqk.append(t3)
        free_w.append(t)

        w, arrived, free_w = weights("w_in_t", 1, KC, 512)
        t_rg = []
        for j in range(RH):
            need("pe", arrived)
            b, pair, t = project_halves(w, j * P, P, xnT, "pe_rg", [])
            need("act", t)
            t_rg.append(mark(act.activation(halves(silu_rg[:, j, :]), pair, ACT.Silu), "act_rg"))
            psum.release(b, t_rg[-1], n=2)
        free_w.append(t)

        t_fqk = []
        for unit in range(2):
            w, arrived, free_w = weights("w_in_t", 2 + unit, KC, 512)
            for j in range(4):
                need("pe", arrived)
                b, pair, t = project_halves(w, j * P, P, xnT, "pe_fqk", [])
                need("act", t)
                t_fqk.append(mark(act.activation(halves(fqk[:, 4 * unit + j, :]), pair, ACT.Copy,
                                                 scale=(FDH ** -0.5 if unit == 0 else 1.0)), "act_fqk"))
                psum.release(b, t_fqk[-1], n=2)
            free_w.append(t)

        diag = sb(second, "diag", [P, RH, P])
        causal16 = sb(second, "causal16", [P, P], BF16)
        causal = sb(second, "causal", [P, P])
        t_diag = [mark(act.dma_start(d, A[n]), "ld_diag", 16) for d, n in ((diag[:], "ret_diag"), (causal[:], "causal"))][-1]
        need("dve", t_diag)
        t_causal = mark(dve.tensor_copy(causal16[:], causal[:]), "dve_mask")
        scoresT = Ring([sb(second, "scoresT0", [P, NT + 1, NK]), xnT[:, 0:NT + 1, :]])
        wide = Ring([sb(second, f"wide{i}", [P, NK]) for i in range(2)])

        def tiles():
            return [(NT, META, 0)] + [(j, P, META + j * P) for j in range(NT)]

        t_mixed = [None] * RH

        def retention_scores(h):
            rows = slice((h % 2) * RDK, (h % 2) * RDK + RDK)
            q, k = rqk[rows, h // 2, :], rqk[rows, 2 + h // 2, :]
            si, sT, sfree = scoresT.take()
            done = {}
            for j, n, at in tiles():
                b, pair, free = psum.take(2)
                need("pe", *free, *t_rqk)
                if j == NT:
                    for a in range(2):
                        t = chain(pair[0:n, a, 0:HALF], [(k[:, at:at + n], q[:, a * HALF:(a + 1) * HALF])], "pe_ret")
                    src, dst = pair[0:n, :, 0:HALF], halves(sT[0:n, j, :])
                else:
                    t = chain(pair[:, 0, 0:NK - at], [(k[:, at:at + n], q[:, at:NK])], "pe_ret")
                    src, dst = pair[:, 0, 0:NK - at], sT[:, j, at:NK]
                need("act", t, *sfree)
                t_copy = mark(act.activation(dst, src, ACT.Copy), "act_ret")
                psum.release(b, t_copy, n=2)
                need("dve", t_copy, t_diag)
                done[j] = mark(dve.tensor_tensor(sT[0:n, j, at:at + n], sT[0:n, j, at:at + n], diag[0:n, h, 0:n], ALU.mult), "dve_ret")
            return si, sT, done

        def retention_values(h, si, sT, done):
            b, pair, free = psum.take(2)
            need("pe", *free)
            for j, n, at in tiles()[1:] + tiles()[:1]:
                need("pe", t_v["rv", j], done[j])
                v = rv[0:n, j, h * RDV:(h + 1) * RDV]
                if j == NT:
                    pe.matmul(pair[:, 1, 0:META], v, sT[0:n, j, 0:META], start=True, stop=True)
                    last = pe.matmul(pair[:, 0, 0:SEQ], v, sT[0:n, j, META:NK], start=False, stop=True)
                else:
                    pe.matmul(pair[:, 0, at - META:SEQ], v, sT[:, j, at:NK], start=j == 0, stop=False)
            t_o = mark(last, "pe_ret")
            scoresT.free[si].append(t_o)
            wi, obuf, ofree = wide.take()
            need("act", t_o, *ofree)
            mark(act.activation(obuf[:, META:NK], pair[:, 0, 0:SEQ], ACT.Copy), "act_ret")
            t_oc = mark(act.activation(obuf[:, 0:META], pair[:, 1, 0:META], ACT.Copy), "act_ret")
            psum.release(b, t_oc, n=2)
            r, sq, rfree = raw.take()
            need("act", t_oc, *rfree)
            t_sq = mark(act.activation(sq[:], obuf[:], ACT.Square), "act_ret")
            return wi, obuf, t_oc, r, sq, t_sq

        def retention_norm(h, wi, obuf, t_oc, r, sq, t_sq):
            b, pair, free = psum.take(2)
            need("pe", *free, t_sq, t_ones)
            for a in range(2):
                t = chain(pair[:, a, 0:HALF], [(ones[:], sq[:, a * HALF:(a + 1) * HALF])], "pe_ret")
            raw.free[r].append(t)
            u, root, ufree = turned.take()
            need("act", t, *ufree)
            t_root = mark(act.activation(halves(root[:]), pair[:, :, 0:HALF], ACT.Sqrt, bias=eps[:, :], scale=1.0 / RDV), "act_ret")
            psum.release(b, t_root, n=2)
            need("dve", t_root)
            t = mark(dve.reciprocal(root[:], root[:]), "dve_ret")
            need("dve", t, t_oc)
            t = mark(dve.tensor_tensor(obuf[:], obuf[:], root[:], ALU.mult), "dve_ret")
            turned.free[u].append(t)
            need("dve", t, t_rg[h])
            t = mark(dve.scalar_tensor_tensor(mixedT[:, h, :], obuf[:], col("ret_g", h), silu_rg[:, h, :],
                                              ALU.mult, ALU.mult), "dve_ret")
            wide.free[wi].append(t)
            t_mixed[h] = t

        ahead = retention_scores(0)
        for h in range(RH):
            now, ahead = ahead, retention_scores(h + 1) if h + 1 < RH else None
            sums = retention_values(h, *now)
            if h:
                retention_norm(h - 1, *before)
            before = sums
        retention_norm(RH - 1, *before)

        S.fence(("dve", "act", "pe"))
        third = ctx.enter_context(ExitStack())
        bias = Ring([raw.buffers[0], raw.buffers[1]])
        logits = Ring([wide.buffers[0], wide.buffers[1], turned.buffers[0], turned.buffers[1]])
        negmax = sb(third, "negmax", [P, 4, 4])
        pT = Ring(scoresT.buffers)
        small = Ring([negmax[:, i, :] for i in range(4)])

        def fox_bias(h):
            b, pair, free = psum.take(2)
            need("pe", *free, t_run, t_small)
            for a in range(2):
                t = chain(pair[:, a, 0:HALF], [(sel[:, h, :], run[:, a * HALF:(a + 1) * HALF])], "pe_bias")
            bi, negc, bfree = bias.take()
            need("act", t, *bfree)
            t = mark(act.activation(halves(negc[:]), pair[:, :, 0:HALF], ACT.Copy, scale=-1.0), "act_fox")
            psum.release(b, t, n=2)
            return bi, negc, t

        def fox_scores(h, i, n, at, head):
            bi, negc, t_negc = head["bias"]
            rows = slice((h % 2) * FDH, (h % 2) * FDH + FDH)
            q, k = fqk[rows, h // 2, :], fqk[rows, 4 + h // 2, :]
            b, pair, free = psum.take(2)
            need("pe", *free, *t_fqk, t_causal)
            width = META if i == NT else at + P
            if i == NT:
                pe.matmul(pair[0:n, 0, 0:n], q[:, 0:n], k[:, 0:n], start=True, stop=False)
                last = pe.matmul(pair[0:n, 0, 0:n], ident16[0:n, 0:n], causal16[0:n, 0:n], start=False, stop=True)
                view, shape = pair[0:n, 0, 0:n], (lambda ap: ap)
            elif width <= BANK:
                pe.matmul(pair[:, 0, 0:width], q[:, at:at + n], k[:, 0:width], start=True, stop=True)
                last = pe.matmul(pair[:, 0, at:width], ident16[:], causal16[:], start=False, stop=True, skip_group_check=True)
                view, shape = pair[:, 0, 0:width], (lambda ap: ap)
            else:
                pe.matmul(pair[:, 0, 0:HALF], q[:, at:at + n], k[:, 0:HALF], start=True, stop=True)
                pe.matmul(pair[:, 1, 0:HALF], q[:, at:at + n], k[:, HALF:NK], start=True, stop=True)
                last = pe.matmul(pair[:, 1, at - HALF:HALF], ident16[:], causal16[:], start=False, stop=True, skip_group_check=True)
                view, shape = pair[:, :, 0:HALF], halves
            t = mark(last, "pe_fox")
            li, L, lfree = logits.take()
            ni, nm, nfree = small.take()
            need("dve", t, t_negc, *lfree, *nfree)
            t_max = mark(dve.tensor_tensor_reduce(shape(L[0:n, 0:width]), view, shape(negc[0:n, 0:width]), 1.0, NEG * 1e8,
                                                  ALU.add, ALU.max, nm[0:n, 0:1]), "dve_fox")
            psum.release(b, t_max, n=2)
            if i == NT - 1:
                bias.free[bi].append(t_max)
            need("dve", t_max)
            t = mark(dve.tensor_scalar(nm[0:n, 1:2], nm[0:n, 0:1], -1.0, None, ALU.mult), "dve_fox")
            need("act", t, t_max)
            t = mark(act.activation(L[0:n, 0:width], L[0:n, 0:width], ACT.Exp, bias=nm[0:n, 1:2],
                                    accum_out=nm[0:n, 2:3]), "act_fox")
            return dict(h=h, i=i, n=n, at=at, width=width, li=li, L=L, ni=ni, nm=nm, exp=t, head=head)

        def fox_weights(c):
            n, L, nm, width = c["n"], c["L"], c["nm"], c["width"]
            need("dve", c["exp"])
            t = mark(dve.reciprocal(nm[0:n, 3:4], nm[0:n, 2:3]), "dve_fox")
            need("dve", t)
            c["p"] = mark(dve.tensor_scalar(L[0:n, 0:width], L[0:n, 0:width], nm[0:n, 3:4], None, ALU.mult), "dve_fox")
            small.free[c["ni"]].append(c["p"])

        def fox_transpose(c):
            i, n, at, L, head = c["i"], c["n"], c["at"], c["L"], c["head"]
            if "pt" not in head:
                head["pt"] = pT.take()
            pi, pt, pfree = head["pt"]
            b, pair, free = psum.take(2)
            need("pe", *free, c["p"])
            if i == NT:
                t = mark(pe.transpose(pair[0:n, 0, 0:n], L[0:n, 0:n], ident[0:n, 0:n]), "pe_fox")
                need("act", t, *pfree)
                head["done"].append(mark(act.activation(pt[0:n, NT, 0:n], pair[0:n, 0, 0:n], ACT.Copy), "act_fox"))
                psum.release(b, head["done"][-1], n=2)
            else:
                t_m = mark(pe.transpose(pair[0:META, 1, 0:P], L[:, 0:META], ident[:]), "pe_fox")
                for j in range(i + 1):
                    last = pe.transpose(pair[:, 0, j * P:(j + 1) * P], L[:, META + j * P:META + (j + 1) * P], ident[:])
                t = mark(last, "pe_fox")
                need("dve", t_m, *pfree)
                head["done"].append(mark(dve.tensor_copy(pt[0:META, NT, at:at + P], pair[0:META, 1, 0:P]), "dve_fox"))
                psum.release(b + 1, head["done"][-1])
                need("act", t, *pfree)
                head["done"].append(mark(act.activation(pt[:, 0:i + 1, at:at + P],
                                                        pair[:, 0, 0:(i + 1) * P].rearrange("p (j t) -> p j t", t=P), ACT.Copy), "act_fox"))
                psum.release(b, head["done"][-1])
            logits.free[c["li"]].append(t)

        def fox_values(h, head):
            rows = slice((h % 2) * FDH, (h % 2) * FDH + FDH)
            pi, pt, _ = head["pt"]
            b, pair, free = psum.take(2)
            need("pe", *free, *head["done"])
            for j, n, at in tiles()[1:] + tiles()[:1]:
                need("pe", t_v["fv", j])
                v = fv[0:n, j, h * FDH:(h + 1) * FDH]
                if j == NT:
                    pe.matmul(pair[rows, 1, 0:META], v, pt[0:n, j, 0:META], start=True, stop=True)
                    last = pe.matmul(pair[rows, 0, 0:SEQ], v, pt[0:n, j, META:NK], start=False, stop=True)
                else:
                    pe.matmul(pair[rows, 0, at - META:SEQ], v, pt[:, j, at:NK], start=j == 0, stop=False)
            t = mark(last, "pe_fox")
            pT.free[pi].append(t)
            need("act", t)
            mark(act.activation(mixedT[rows, 4 + h // 2, META:NK], pair[rows, 0, 0:SEQ], ACT.Copy), "act_fox")
            t_mixed.append(mark(act.activation(mixedT[rows, 4 + h // 2, 0:META], pair[rows, 1, 0:META], ACT.Copy), "act_fox"))
            psum.release(b, t_mixed[-1], n=2)

        heads = [dict(done=[]) for _ in range(FH)]
        heads[0]["bias"] = fox_bias(0)
        items, flow = [(h, *tile) for h in range(FH) for tile in tiles()], []
        for c in range(len(items) + 3):
            if c < len(items):
                h, i, n, at = items[c]
                flow.append(fox_scores(h, i, n, at, heads[h]))
                if i == NT - 1 and h + 1 < FH:
                    heads[h + 1]["bias"] = fox_bias(h + 1)
            if 0 <= c - 1 < len(items):
                fox_weights(flow[c - 1])
            if 0 <= c - 2 < len(items):
                fox_transpose(flow[c - 2])
            if c >= 3 and flow[c - 3]["i"] == NT - 1:
                fox_values(flow[c - 3]["h"], flow[c - 3]["head"])

        t_x2 = [None] * (NT + 1)
        for half in range(2):
            w, arrived, free_w = weights("w_out", half, KC, 512)
            need("pe", arrived, *t_mixed)
            for i, n, at in tiles():
                b, bank, free = psum.take()
                need("pe", *free)
                t = chain(bank[0:n, :], [(mixedT[:, c, at:at + n], w[:, c, :]) for c in range(KC)], "pe_out")
                need("dve", t)
                dst = (xm[:, half * 512:(half + 1) * 512] if i == NT else x[:, i, half * 512:(half + 1) * 512])
                t_x2[i] = mark(dve.tensor_tensor(dst, dst, bank[0:n, :], ALU.add), "dve_out")
                psum.release(b, t_x2[i])
            free_w.append(t)
        S.fence()
        third.close()
        second.close()
        mixer.close()

        late = ctx.enter_context(ExitStack())
        modc = sb(late, "modc", [P, 2, 6 * KC])
        gain1 = sb(late, "gain1", [P, 2, KC])
        silu_c = sb(late, "silu_c", [P, KC, 2])
        ffn = ctx.enter_context(ExitStack())
        LEAD = 2
        NA = LEAD + SEQ
        gT = sb(ffn, "gT", [P, NF, SEQ])
        xnT = sb(ffn, "xnT2", [P, KC, NK])
        xn = sb(ffn, "xn2", [P, NT, D])
        xnm = sb(ffn, "xnm2", [META, D])
        scratch = sb(ffn, "scratch2", [P, D])
        branch = Ring([sb(ffn, f"branch{i}", [P, NA]) for i in range(3)])
        acc = Ring([sb(ffn, f"acc{i}", [P, SEQ]) for i in range(3)])
        ready, ready_m = normalise("norm2", t_x2, t_x2[NT])
        t_xnT = [meta_transposed(xnm[:], xnT, col("ffn_g", 0, KC), "norm2", ready_m)]
        t_xnT += transposed(xn, NT, xnT, [col("ffn_g", c) for c in range(KC)], None, "norm2", ready, META)
        NAH = NA // 2
        modacc = Ring([sb(ffn, f"modacc{i}", [P, 512]) for i in range(4)])
        t_silu_c = mark(act.activation(silu_c[:].rearrange("p k t -> p (k t)"), col("cond", 0, 2 * KC), ACT.Silu), "act_mod")

        def mod_sums(m):
            w, arrived, free_w = weights("w_mod", m, KC, 512)
            need("dve", arrived, t_silu_c)
            sums = []
            for r in range(2 if m < 4 else 1):
                ai, a, afree = modacc.take()
                need("dve", *afree)
                t = mark(dve.tensor_scalar(a[:], w[:, 0, :], silu_c[:, 0, r:r + 1], None, ALU.mult), "dve_mod")
                for c in range(1, KC):
                    need("dve", t)
                    t = mark(dve.scalar_tensor_tensor(a[:], w[:, c, :], silu_c[:, c, r:r + 1], a[:], ALU.mult, ALU.add), "dve_mod")
                sums.append((r, ai, a, t))
            free_w.append(t)
            return m, sums

        def mod_finish(m, sums):
            for r, ai, a, t in sums:
                b, bank, free = psum.take()
                need("pe", *free, t, t_ones)
                for j in range(4):
                    last = pe.matmul(bank[:, j:j + 1], a[:, j * P:(j + 1) * P], ones[:, 0:1], start=True, stop=True)
                t = mark(last, "pe_mod")
                need("dve", t)
                t_mod = mark(dve.tensor_tensor(modc[:, r, 4 * m:4 * m + 4], bank[:, 0:4], col("b_mod", 4 * m, 4), ALU.add), "dve_mod")
                psum.release(b, t_mod)
                modacc.free[ai].append(t)
            return t_mod

        mod_ahead = mod_sums(0)
        for u in range(NF // 2):
            w, arrived, free_w = weights("w_up", u, KC, 512)
            need("pe", arrived, *t_xnT)
            for v in range(2):
                f = 2 * u + v
                b, pair, free = psum.take(2)
                need("pe", *free)
                for a in range(2):
                    at = META - LEAD + a * NAH
                    t = chain(pair[:, a, 0:NAH], [(w[:, c, v * P:(v + 1) * P], xnT[:, c, at:at + NAH]) for c in range(KC)], "pe_up")
                bi, abuf, bfree = branch.take()
                need("act", t, *bfree)
                t_a = mark(act.activation(abuf[:].rearrange("p (a n) -> p a n", a=2), pair[:, :, 0:NAH], ACT.Copy), "act_up")
                psum.release(b, t_a, n=2)
                ai, cbuf, afree = acc.take()
                need("dve", t_a, *afree)
                t = mark(dve.tensor_scalar(cbuf[:], abuf[:, 0:SEQ], col("conv_w", f), col("conv_b", f), ALU.mult, ALU.add), "dve_up")
                for j in range(1, 3):
                    need("dve", t)
                    t = mark(dve.scalar_tensor_tensor(cbuf[:], abuf[:, j:j + SEQ], col("conv_w", j * NF + f), cbuf[:],
                                                      ALU.mult, ALU.add), "dve_up")
                branch.free[bi].append(t)
                need("act", t)
                t_s = mark(act.activation(cbuf[:], cbuf[:], ACT.Silu), "act_up")
                b, bank, free = psum.take()
                need("pe", *free)
                t = chain(bank[:, :], [(w[:, c, 256 + v * P:256 + (v + 1) * P], xnT[:, c, META:NK]) for c in range(KC)], "pe_up")
                need("dve", t, t_s)
                t_g = mark(dve.tensor_tensor(gT[:, f, :], bank[:, :], cbuf[:], ALU.mult), "dve_up")
                psum.release(b, t_g)
                acc.free[ai].append(t_g)
            free_w.append(t)
            mod_now, mod_ahead = mod_ahead, mod_sums(u + 1)
            t_mod = mod_finish(*mod_now)
        t_mod = mod_finish(*mod_ahead)
        need("dve", t_mod)
        for r in range(2):
            t_gain = mark(dve.scalar_tensor_tensor(gain1[:, r, :], modc[:, r, KC:2 * KC], 1.0, col("norm1_g", 0, KC),
                                                   ALU.add, ALU.mult), "dve_mod")
        t_x3 = [None] * NT
        splits = [(0, 8), (8, 16), (16, NF)]
        for half in range(2):
            banks = [psum.take() for _ in range(NT)]
            for s, (f0, f1) in enumerate(splits):
                w, arrived, free_w = weights("w_down", half * len(splits) + s, f1 - f0, 512)
                need("pe", arrived, t_g)
                for i in range(NT):
                    need("pe", *banks[i][2])
                    t = chain(banks[i][1][:, :], [(gT[:, f, i * P:(i + 1) * P], w[:, f - f0, :]) for f in range(f0, f1)],
                              "pe_down", start=s == 0, stop=s == len(splits) - 1)
                    if s == len(splits) - 1:
                        need("dve", t)
                        dst = x[:, i, half * 512:(half + 1) * 512]
                        t_x3[i] = mark(dve.tensor_tensor(dst, dst, banks[i][1][:, :], ALU.add), "dve_down")
                        psum.release(banks[i][0], t_x3[i])
                free_w.append(t)
        S.fence()
        ffn.close()

        block2 = ctx.enter_context(ExitStack())
        merged = sb(block2, "merged", [P, KC, SEQ])
        sig_a = sb(block2, "sig_a", [P, KC, SEQ])
        latent = sb(block2, "latent", [P, 2 * SEQ + 2 * NKV])
        cq = latent[:, 0:2 * SEQ].rearrange("p (k n) -> p k n", k=2)
        ckv = latent[:, 2 * SEQ:2 * SEQ + NKV]
        kr = latent[:, 2 * SEQ + NKV:]
        swap2 = spare_row[:, NKV:NKV + P]
        rope2 = sb(block2, "rope2", [P, 2, SEQ])
        t_rope2 = [mark(act.dma_start(d, A[n]), "ld_rope2", 16) for d, n in ((swap2, "swap2"), (rope2[:], "rope2"))][-1]

        pre = ctx.enter_context(ExitStack())
        hT = sb(pre, "hT", [P, KC, SEQ])
        hcT = sb(pre, "hcT", [P, KC, CTX])
        norm = ctx.enter_context(ExitStack())
        xn = sb(norm, "xn3", [P, NT, D])
        ctxn = sb(norm, "ctxn", [P, 2, D])
        scratch = sb(norm, "scratch3", [P, D])
        final1 = sb(norm, "final1", [P, D])
        t_ctx = mark(act.dma_start(ctxn[:], A["ctx"]), "ld_ctx", 16)
        t_final1 = mark(act.dma_start(final1[:], A["final1"]), "ld_final1", 16)

        ready = []
        for i in range(NT):
            t = token_rstd(x[:, i, :], P, i, scratch, t_x3[i], "norm3")
            need("dve", t, t_final1)
            t = mark(dve.scalar_tensor_tensor(x[:, i, :], x[:, i, :], stat[:, 2, i:i + 1], final1[:], ALU.mult, ALU.mult), "dve_norm3")
            t = token_rstd(x[:, i, :], P, i, scratch, t, "norm3")
            need("dve", t)
            ready.append(mark(dve.tensor_scalar(xn[:, i, :], x[:, i, :], stat[:, 2, i:i + 1], None, ALU.mult), "dve_norm3"))
        need("dve", t_ctx)
        ready_c = []
        for i in range(2):
            t = token_rstd(ctxn[:, i, :], P, 5 + i, scratch, t_ctx, "norm3")
            need("dve", t)
            ready_c.append(mark(dve.tensor_scalar(ctxn[:, i, :], ctxn[:, i, :], stat[:, 2, 5 + i:6 + i], None, ALU.mult), "dve_norm3"))
        need("act", t_gain)
        need("dve", t_gain)
        t_hT = transposed(xn, NT, hT, [gain1[:, 0, c:c + 1] for c in range(KC)], [modc[:, 0, c:c + 1] for c in range(KC)], "norm3", ready)
        t_hcT = transposed(ctxn, 2, hcT, [gain1[:, 1, c:c + 1] for c in range(KC)], [modc[:, 1, c:c + 1] for c in range(KC)], "norm3", ready_c)
        S.fence()
        norm.close()

        conv = ctx.enter_context(ExitStack())
        sig_c = sb(conv, "sig_c", [P, KC, SEQ])
        EDGE = TAPS // 2
        padded = sb(conv, "padded", [P, KC, SEQ + 2 * EDGE])
        sg = Ring([sb(conv, f"sg{i}", [P, SEQ]) for i in range(3)])
        mark(pool.memset(padded[:, :, 0:EDGE], 0.0), "pool_pad")
        t_pad = mark(pool.memset(padded[:, :, EDGE + SEQ:], 0.0), "pool_pad")
        need("dve", t_pad)
        t_conv = [None] * KC
        for u in range(4):
            w, arrived, free_w = weights("w_in2", 1 + u, KC, 512)
            need("pe", arrived, *t_hT)
            for v in range(2):
                k = 2 * u + v
                b, bank, free = psum.take()
                need("pe", *free)
                t = chain(bank[:, :], [(w[:, c, 256 + v * P:256 + (v + 1) * P], hT[:, c, :]) for c in range(KC)], "pe_glu")
                gi, gbuf, gfree = sg.take()
                need("act", t, *gfree)
                t_sg = mark(act.activation(gbuf[:], bank[:, :], ACT.Sigmoid), "act_glu")
                psum.release(b, t_sg)
                b, bank, free = psum.take()
                need("pe", *free)
                t = chain(bank[:, :], [(w[:, c, v * P:(v + 1) * P], hT[:, c, :]) for c in range(KC)], "pe_glu")
                need("dve", t, t_sg)
                t_y = mark(dve.tensor_tensor(padded[:, k, EDGE:EDGE + SEQ], bank[:, :], gbuf[:], ALU.mult), "dve_glu")
                psum.release(b, t_y)
                sg.free[gi].append(t_y)
            free_w.append(t)
            need("dve", t_y)
            pair_t = {}
            for j in range(TAPS):
                for k in (2 * u, 2 * u + 1):
                    src = padded[:, k, j:j + SEQ]
                    if j == 0:
                        pair_t[k] = mark(dve.tensor_scalar(merged[:, k, :], src, col("dw_w", k), col("dw_b", k), ALU.mult, ALU.add), "dve_conv")
                    else:
                        need("dve", pair_t[k])
                        pair_t[k] = mark(dve.scalar_tensor_tensor(merged[:, k, :], src, col("dw_w", j * KC + k), merged[:, k, :],
                                                                  ALU.mult, ALU.add), "dve_conv")
                    t_conv[k] = pair_t[k]

        w, arrived, free_w = weights("w_in2", 0, KC, 416)
        need("pe", arrived, *t_hcT)
        lat = {}
        for j in range(3):
            b, bank, free = psum.take()
            need("pe", *free)
            t = chain(bank[:, :], [(w[:, c, j * P:(j + 1) * P], hT[:, c, :]) for c in range(KC)], "pe_ckv")
            dst = cq[:, j, :] if j < 2 else ckv[:, 0:SEQ]
            need("act", t)
            lat[j] = mark(act.activation(dst, bank[:, :], ACT.Copy), "act_ckv")
            psum.release(b, lat[j])
        b, bank, free = psum.take()
        need("pe", *free)
        t = chain(bank[:, 0:CTX], [(w[:, c, 2 * P:3 * P], hcT[:, c, :]) for c in range(KC)], "pe_ckv")
        need("act", t)
        t_ckv = mark(act.activation(ckv[:, SEQ:NKV], bank[:, 0:CTX], ACT.Copy), "act_ckv")
        psum.release(b, t_ckv)
        R = slice(NOPE, QK)
        for src, n, at in ((hT, SEQ, 0), (hcT, CTX, SEQ)):
            b, bank, free = psum.take()
            need("pe", *free)
            t = chain(bank[R, 0:n], [(w[:, c, 3 * P:3 * P + ROPE], src[:, c, :]) for c in range(KC)], "pe_ckv")
            need("act", t)
            t_kr = mark(act.activation(kr[R, at:at + n], bank[R, 0:n], ACT.Copy), "act_ckv")
            psum.release(b, t_kr)
        free_w.append(t)
        b, bank, free = psum.take()
        need("pe", *free, t_kr, t_rope2)
        t = chain(bank[R, :], [(swap2[R, R], kr[R, 0:SEQ])], "pe_ckv")
        gi, gbuf, gfree = sg.take()
        need("dve", t, t_kr, t_rope2, *gfree)
        t1 = mark(dve.tensor_tensor(gbuf[R, :], bank[R, :], rope2[R, 1, :], ALU.mult), "dve_ckv")
        psum.release(b, t1)
        t2 = mark(dve.tensor_tensor(kr[R, 0:SEQ], kr[R, 0:SEQ], rope2[R, 0, :], ALU.mult), "dve_ckv")
        need("dve", t1, t2)
        t_kr = mark(dve.tensor_tensor(kr[R, 0:SEQ], kr[R, 0:SEQ], gbuf[R, :], ALU.add), "dve_ckv")
        sg.free[gi].append(t_kr)

        def feature_norm(views, n, rank, gains, name, ready):
            b, bank, free = psum.take()
            need("pe", *free, t_ones)
            for k, view in enumerate(views):
                gi, sq, gfree = sg.take()
                need("act", *gfree, *ready)
                t = mark(act.activation(sq[:, 0:n], view, ACT.Square), f"act_{name}")
                need("pe", t)
                t = mark(pe.matmul(bank[:, 0:n], ones[:], sq[:, 0:n], start=k == 0, stop=k == len(views) - 1), f"pe_{name}")
                sg.free[gi].append(t)
            gi, root, gfree = sg.take()
            need("act", t, *gfree)
            t = mark(act.activation(root[:, 0:n], bank[:, 0:n], ACT.Sqrt, bias=eps[:, :], scale=1.0 / rank), f"act_{name}")
            psum.release(b, t)
            need("dve", t, *ready)
            t = mark(dve.reciprocal(root[:, 0:n], root[:, 0:n]), f"dve_{name}")
            need("dve", t)
            for view, g in zip(views, gains):
                t = mark(dve.scalar_tensor_tensor(view, view, g, root[:, 0:n], ALU.mult, ALU.mult), f"dve_{name}")
            sg.free[gi].append(t)
            return t

        t_cq = feature_norm([cq[:, 0, :], cq[:, 1, :]], SEQ, 256, [col("q_g", 0), col("q_g", 1)], "cnorm", [lat[0], lat[1]])
        t_ckv1 = feature_norm([ckv[:, 0:SEQ]], SEQ, 128, [col("kv_g")], "cnorm", [lat[2]])
        t_ckv2 = feature_norm([ckv[:, SEQ:NKV]], CTX, 128, [col("kv_g")], "cnorm", [t_ckv])

        t_gate = {}
        for u in range(4):
            w, arrived, free_w = weights("w_in2", 5 + u, KC, 512)
            need("pe", arrived)
            for v in range(4):
                k = 4 * u + v
                b, bank, free = psum.take()
                need("pe", *free)
                t = chain(bank[:, :], [(w[:, c, v * P:(v + 1) * P], hT[:, c, :]) for c in range(KC)], "pe_gate")
                need("act", t)
                dst = sig_a[:, k, :] if k < KC else sig_c[:, k - KC, :]
                t_gate[k] = mark(act.activation(dst, bank[:, :], ACT.Sigmoid), "act_gate")
                psum.release(b, t_gate[k])
            free_w.append(t)

        b, bank, free = psum.take()
        need("pe", *free, *t_conv)
        t = chain(bank[:, :], [(ones[:], merged[:, k, :]) for k in range(KC)], "pe_ln")
        mi, mean, mfree = sg.take()
        need("act", t, *mfree)
        t_mean = mark(act.activation(mean[:], bank[:, :], ACT.Copy, scale=1.0 / D), "act_ln")
        psum.release(b, t_mean)
        b, bank, free = psum.take()
        need("pe", *free)
        t_cent = []
        for k in range(KC):
            need("dve", t_mean, t_conv[k])
            t_cent.append(mark(dve.tensor_tensor(merged[:, k, :], merged[:, k, :], mean[:], ALU.subtract), "dve_ln"))
        sg.free[mi].append(t_cent[-1])
        for k in range(KC):
            gi, sq, gfree = sg.take()
            need("act", *gfree, t_cent[k])
            t = mark(act.activation(sq[:], merged[:, k, :], ACT.Square), "act_ln")
            need("pe", t)
            t = mark(pe.matmul(bank[:, :], ones[:], sq[:], start=k == 0, stop=k == KC - 1), "pe_ln")
            sg.free[gi].append(t)
        gi, root, gfree = sg.take()
        need("act", t, *gfree)
        t = mark(act.activation(root[:], bank[:, :], ACT.Sqrt, bias=eps[:, :], scale=1.0 / D), "act_ln")
        psum.release(b, t)
        need("dve", t)
        t = mark(dve.reciprocal(root[:], root[:]), "dve_ln")
        need("dve", t)
        t_sw = []
        for k in range(KC):
            t = mark(dve.tensor_tensor(padded[:, k, 0:SEQ], merged[:, k, :], root[:], ALU.mult), "dve_ln")
            need("act", t)
            t_sw.append(mark(act.activation(padded[:, k, 0:SEQ], padded[:, k, 0:SEQ], ACT.Silu, scale=col("ln_g", k),
                                            bias=col("ln_b", k)), "act_ln"))
        for u in range(2):
            w, arrived, free_w = weights("w_pw", u, KC, 512)
            need("pe", arrived, *t_sw)
            for v in range(4):
                k = 4 * u + v
                b, bank, free = psum.take()
                need("pe", *free)
                t = chain(bank[:, :], [(w[:, c, v * P:(v + 1) * P], padded[:, c, 0:SEQ]) for c in range(KC)], "pe_pw")
                need("dve", t, t_gate[KC + k])
                t_m = mark(dve.tensor_tensor(merged[:, k, :], bank[:, :], sig_c[:, k, :], ALU.mult), "dve_pw")
                psum.release(b, t_m)
            free_w.append(t)
        S.fence()
        conv.close()
        pre.close()

        attn = ctx.enter_context(ExitStack())
        values = sb(attn, "values", [P, NKV // P, AH * VD])
        headsT = sb(attn, "headsT", [P, KC, SEQ])
        Qs = Ring([sb(attn, f"Qs{i}", [P, 4, SEQ]) for i in range(2)])
        Ks = Ring([sb(attn, f"Ks{i}", [P, 2, NKV]) for i in range(2)])
        probs = Ring([sb(attn, f"probs{i}", [P, NKV]) for i in range(2)] + [spare_row[:, 0:NKV]])
        turn = Ring([sb(attn, f"turn{i}", [P, SEQ]) for i in range(2)])
        mstat = sb(attn, "mstat", [P, 4, 4])
        ms = Ring([mstat[:, i, :] for i in range(4)])
        wq, t_wq, free_wq = weights("w_uq", 0, 2, 1536)
        wkv, t_wkv, free_wkv = weights("w_ukv", 0, 1, 2048)
        lent, lent_buffer, lent_free = wring.take()
        probsT = Ring([sb(attn, "probsT0", [P, NKV // P, SEQ]),
                       lent_buffer[:, 0:NKV // P * SEQ].rearrange("p (j t) -> p j t", t=SEQ)])
        probsT.free[1] += lent_free
        t_under = []
        for buffer in Ks.buffers:
            for s in range(2):
                t_under.append(mark(pool.tensor_copy(buffer[R, s, :], kr[R, :]), "pool_kr"))
        need("pe", t_wkv, t_ckv1, t_ckv2)
        t_values = []
        for j in range(NKV // P):
            for half in range(2):
                b, bank, free = psum.take()
                need("pe", *free)
                t = chain(bank[:, :], [(ckv[:, j * P:(j + 1) * P], wkv[:, 0, 1024 + half * 512:1024 + (half + 1) * 512])], "pe_values2")
                need("act", t)
                t_values.append(mark(act.activation(values[:, j, half * 512:(half + 1) * 512], bank[:, :], ACT.Copy), "act_values2"))
                psum.release(b, t_values[-1])
        t_heads = []
        KH = NKV // 2

        def queries(g):
            qi, Q, qfree = Qs.take()
            need("pe", t_wq, t_cq)
            done = []
            for v in range(2):
                b, bank, free = psum.take()
                need("pe", *free)
                t = chain(bank[:, :], [(wq[:, c, (2 * g + v) * P:(2 * g + v + 1) * P], cq[:, c, :]) for c in range(2)], "pe_q")
                need("act", t, *qfree)
                mark(act.activation(Q[0:NOPE, 2 * v, :], bank[0:NOPE, :], ACT.Copy), "act_q")
                t = mark(act.activation(Q[0:NOPE, 2 * v + 1, :], bank[NOPE:P, :], ACT.Copy), "act_q")
                psum.release(b, t)
                done.append(t)
            b, bank, free = psum.take()
            need("pe", *free)
            t = chain(bank[:, :], [(wq[:, c, AH * NOPE + g * P:AH * NOPE + (g + 1) * P], cq[:, c, :]) for c in range(2)], "pe_q")
            ti, plain, tfree = turn.take()
            need("act", t, *tfree)
            t_plain = mark(act.activation(plain[:], bank[:, :], ACT.Copy), "act_q")
            psum.release(b, t_plain)
            b, bank, free = psum.take()
            need("pe", *free, t_plain)
            t = chain(bank[:, :], [(swap2, plain[:])], "pe_q")
            ui, cross, ufree = turn.take()
            need("dve", t, *ufree)
            t1 = mark(dve.tensor_tensor(cross[:], bank[:, :], rope2[:, 1, :], ALU.mult), "dve_q")
            psum.release(b, t1)
            t2 = mark(dve.tensor_tensor(plain[:], plain[:], rope2[:, 0, :], ALU.mult), "dve_q")
            need("dve", t1, t2, *qfree)
            for j in range(4):
                t = mark(dve.tensor_tensor(Q[R, j, :], plain[j * ROPE:(j + 1) * ROPE, :], cross[j * ROPE:(j + 1) * ROPE, :], ALU.add), "dve_q")
            done.append(t)
            turn.free[ti].append(t)
            turn.free[ui].append(t)
            return qi, Q, done

        def keys(p):
            ki, K, kfree = Ks.take()
            b, pair, free = psum.take(2)
            need("pe", *free)
            for a in range(2):
                t = chain(pair[:, a, 0:KH], [(wkv[:, 0, p * P:(p + 1) * P], ckv[:, a * KH:(a + 1) * KH])], "pe_k")
            need("act", t, *kfree)
            mark(act.activation(K[0:NOPE, 0, :].rearrange("p (a n) -> p a n", a=2), pair[0:NOPE, :, 0:KH], ACT.Copy), "act_k")
            t = mark(act.activation(K[0:NOPE, 1, :].rearrange("p (a n) -> p a n", a=2), pair[NOPE:P, :, 0:KH], ACT.Copy), "act_k")
            psum.release(b, t, n=2)
            return ki, K, t

        scale2 = QK ** -0.5

        def scores2(h, i, head):
            b, pair, free = psum.take(2)
            need("pe", *free, *head["Q"][2], head["K"][2], *t_under)
            for a in range(2):
                last = pe.matmul(pair[:, a, 0:KH], head["Q"][1][0:QK, h % 4, i * P:(i + 1) * P],
                                 head["K"][1][0:QK, h % 2, a * KH:(a + 1) * KH], start=True, stop=True)
            t_s = mark(last, "pe_scores2")
            if i == NT - 1:
                if h % 4 == 3:
                    Qs.free[head["Q"][0]].append(t_s)
                if h % 2 == 1:
                    Ks.free[head["K"][0]].append(t_s)
            mi, st, mfree = ms.take()
            need("dve", t_s, *mfree)
            t = mark(dve.tensor_reduce(st[:, 0:1], pair[:, :, 0:KH], mybir.AxisListType.XY, ALU.max), "dve_attn2")
            need("dve", t)
            t = mark(dve.tensor_scalar(st[:, 1:2], st[:, 0:1], -scale2, None, ALU.mult), "dve_attn2")
            li, L, lfree = probs.take()
            need("act", t, t_s, *lfree)
            t = mark(act.activation(L[:].rearrange("p (a n) -> p a n", a=2), pair[:, :, 0:KH], ACT.Exp, bias=st[:, 1:2],
                                    scale=scale2, accum_out=st[:, 2:3]), "act_attn2")
            psum.release(b, t, n=2)
            return dict(h=h, i=i, mi=mi, st=st, li=li, L=L, exp=t, head=head)

        def weights2(c):
            st, L = c["st"], c["L"]
            need("dve", c["exp"])
            t = mark(dve.reciprocal(st[:, 3:4], st[:, 2:3]), "dve_attn2")
            need("dve", t)
            c["p"] = mark(dve.tensor_scalar(L[:], L[:], st[:, 3:4], None, ALU.mult), "dve_attn2")
            ms.free[c["mi"]].append(c["p"])

        def transpose2(c):
            i, L, head = c["i"], c["L"], c["head"]
            if "pt" not in head:
                head["pt"] = probsT.take()
            pi, pt, pfree = head["pt"]
            b, pair, free = psum.take(2)
            need("pe", *free, c["p"])
            for j in range(NKV // P):
                last = pe.transpose(pair[:, j // 3, (j % 3) * P:(j % 3 + 1) * P], L[:, j * P:(j + 1) * P], ident[:])
            t = mark(last, "pe_attn2")
            probs.free[c["li"]].append(t)
            need("act", t, *pfree)
            t = mark(act.activation(pt[:, :, i * P:(i + 1) * P].rearrange("p (a j) t -> p a j t", a=2),
                                    pair[:, :, 0:KH].rearrange("p a (j t) -> p a j t", t=P), ACT.Copy), "act_attn2")
            psum.release(b, t, n=2)
            head["done"].append(t)

        def values2(h, head):
            rows = slice((h % 2) * VD, (h % 2) * VD + VD)
            pi, pt, _ = head["pt"]
            b, bank, free = psum.take()
            need("pe", *free, *head["done"], *t_values)
            t = chain(bank[rows, :], [(values[:, j, h * VD:(h + 1) * VD], pt[:, j, :]) for j in range(NKV // P)], "pe_attn2")
            probsT.free[pi].append(t)
            need("dve", t)
            t_heads.append(mark(dve.tensor_copy(headsT[rows, h // 2, :], bank[rows, :]), "dve_heads"))
            psum.release(b, t_heads[-1])
            return t

        heads = [dict(done=[]) for _ in range(AH)]
        Q_now, K_now = queries(0), keys(0)
        items, flow = [(h, i) for h in range(AH) for i in range(NT)], []
        for c in range(len(items) + 3):
            if c < len(items):
                h, i = items[c]
                if i == 0:
                    if h and h % 4 == 0:
                        Q_now = Q_next
                    if h and h % 2 == 0:
                        K_now = K_next
                    heads[h].update(Q=Q_now, K=K_now)
                flow.append(scores2(h, i, heads[h]))
                if i == 1 and h % 4 == 3 and h + 1 < AH:
                    Q_next = queries(h // 4 + 1)
                if i == 1 and h % 2 == 1 and h + 1 < AH:
                    K_next = keys(h // 2 + 1)
            if 0 <= c - 1 < len(items):
                weights2(flow[c - 1])
            if 0 <= c - 2 < len(items):
                transpose2(flow[c - 2])
            if c >= 3 and flow[c - 3]["i"] == NT - 1:
                t = values2(flow[c - 3]["h"], flow[c - 3]["head"])
        free_wq.append(t)
        free_wkv.append(t)
        wring.free[lent].append(t)

        for u in range(2):
            w, arrived, free_w = weights("w_o_mla", u, KC, 512)
            need("pe", arrived, *t_heads)
            for v in range(4):
                k = 4 * u + v
                b, bank, free = psum.take()
                need("pe", *free)
                t = chain(bank[:, :], [(w[:, c, v * P:(v + 1) * P], headsT[:, c, :]) for c in range(KC)], "pe_o")
                need("dve", t, t_gate[k])
                t1 = mark(dve.tensor_tensor(sig_a[:, k, :], bank[:, :], sig_a[:, k, :], ALU.mult), "dve_o")
                psum.release(b, t1)
                need("dve", t1, t_m)
                t_merged = mark(dve.tensor_tensor(merged[:, k, :], merged[:, k, :], sig_a[:, k, :], ALU.add), "dve_o")
            free_w.append(t)
        S.fence()
        attn.close()

        rest = ctx.enter_context(ExitStack())
        h2 = sb(rest, "h2", [P, NT, D])
        final2 = sb(rest, "final2", [P, D])
        qT = sb(rest, "qT", [P, 2 * PH, SEQ])
        subkeys = sb(rest, "subkeys", [P, 2 * PH, NKEY])
        peer = ctx.enter_context(ExitStack())
        mod_rows = sb(rest, "mod_rows", [P, 4, D])
        spread = sb(rest, "spread", [P, D])
        rows_ = {name: mod_rows[:, k, :] for k, name in enumerate(("g1", "sh2", "sc2", "g2"))}

        def modulation_row(k, after):
            need("dve", after)
            t = mark(dve.tensor_tensor(spread[:].rearrange("p (c n) -> p c n", c=KC), ident[:].unsqueeze(1).to_broadcast([P, KC, P]),
                                       modc[:, 0, (2 + k) * KC:(3 + k) * KC].unsqueeze(2).to_broadcast([P, KC, P]), ALU.mult), "dve_row")
            b, pair, free = psum.take(2)
            need("pe", *free, t)
            for a in range(2):
                t = chain(pair[:, a, :], [(ones[:], spread[:, a * 512:(a + 1) * 512])], "pe_row")
            need("act", t)
            t_row = mark(act.activation(mod_rows[:, k, :].rearrange("p (a n) -> p a n", a=2), pair, ACT.Copy), "act_row")
            psum.release(b, t_row, n=2)
            return t, t_row

        t_norm2 = mark(act.dma_start(final2[:], A["norm2_g"]), "ld_norm2", 16)
        t_sub = mark(act.dma_start(subkeys[:], A["sub_keys"]), "ld_sub", 16)
        t_x4 = [[] for _ in range(NT)]
        spread_read, t_rows = None, []
        for half in range(2):
            cut = slice(half * 512, (half + 1) * 512)
            w, arrived, free_w = weights("w_out2", half, KC, 512)
            need("pe", arrived, t_merged)
            for i in range(NT):
                b, bank, free = psum.take()
                need("pe", *free)
                t = chain(bank[:, :], [(merged[:, c, i * P:(i + 1) * P], w[:, c, :]) for c in range(KC)], "pe_out2")
                if half == 0:
                    spread_read, t_row = modulation_row(i, spread_read)
                    t_rows.append(t_row)
                need("dve", t, t_rows[0])
                t1 = mark(dve.tensor_tensor(h2[:, i, cut], bank[:, :], rows_["g1"][:, cut], ALU.mult), "dve_out2")
                psum.release(b, t1)
                need("dve", t1)
                t_x4[i].append(mark(dve.tensor_tensor(x[:, i, cut], x[:, i, cut], h2[:, i, cut], ALU.add), "dve_out2"))
            free_w.append(t)
        need("dve", t_norm2, *t_rows)
        t_gain2 = mark(dve.scalar_tensor_tensor(rows_["sc2"], rows_["sc2"], 1.0, final2[:], ALU.add, ALU.mult), "dve_mod2")
        need("act", t_gain2)
        t_final2 = mark(act.dma_start(final2[:], A["final_g"]), "ld_final2", 16)
        need("act", t_merged)
        scratch, h2T = sig_a[:, 0:2, :].rearrange("p a n -> p (a n)"), merged
        ready = []
        for i in range(NT):
            t = token_rstd(x[:, i, :], P, i, scratch, t_x4[i], "norm4")
            t_sq4 = [t]
            need("dve", t, t_gain2)
            t = mark(dve.scalar_tensor_tensor(h2[:, i, :], x[:, i, :], stat[:, 2, i:i + 1], rows_["sc2"], ALU.mult, ALU.mult), "dve_norm4")
            need("dve", t)
            ready.append(mark(dve.tensor_tensor(h2[:, i, :], h2[:, i, :], rows_["sh2"], ALU.add), "dve_norm4"))
        t_h2T = transposed(h2, NT, h2T, [ones[:, 0:1]] * KC, None, "norm4", ready)

        GROUP = 4
        BH = PH // 2
        PICKS = BH * TOPK
        scores = mod_rows[:, 0, :].rearrange("p (r k) -> p r k", k=NKEY)
        left = mod_rows[:, 1, :].rearrange("p (r k) -> p r k", k=NKEY)
        cand_rows = latent[:, 0:BH * TOPK * TOPK].rearrange("p (h n) -> p h n", h=BH)
        cand = cand_rows.rearrange("p h (a b) -> p h a b", a=TOPK)
        rest2 = latent[:, D:D + BH * TOPK * TOPK].rearrange("p (h n) -> p h n", h=BH)
        top = sb(peer, "top", [P, 2 * BH, TOPK])
        topi = sb(peer, "topi", [P, 2 * BH, TOPK], U32)
        topf = sb(peer, "topf", [P, 2 * BH, TOPK])
        best = sb(peer, "best", [P, BH, TOPK])
        besti = sb(peer, "besti", [P, BH, TOPK], U32)
        part = sb(peer, "part", [P, 2, BH, TOPK], U32)
        partf = sb(peer, "partf", [P, 2, BH, TOPK])
        picked = sb(peer, "picked", [P, 2, BH, TOPK])
        gsum = sb(peer, "gsum", [P, 2, BH])
        count = sb(peer, "count", [P, TOPK])
        t_count = mark(act.dma_start(count[:], A["count16"]), "ld_count", 16)
        batches = Ring([dict(expert=sb(peer, f"expert{i}", [P, PICKS], U32), gate=sb(peer, f"gate{i}", [P, BH, TOPK]),
                             hidden=sb(peer, f"hidden{i}", [P, PICKS]), coef=sb(peer, f"coef{i}", [P, PICKS])) for i in range(2)])
        diags = Ring([spread[:, a:a + P] for a in range(0, D, P)])
        need("dve", *ready)
        need("act", *ready)
        LOW = -3.0e38

        def top16(n, row, spare, values_, index, ready):
            need("dve", *ready)
            def each(step):
                return [mark(step(r), "dve_top") for r in range(n)]
            a = each(lambda r: dve.max(values_[:, r, 0:8], row(r)))
            yield
            need("dve", *a)
            each(lambda r: dve.max_index(index[:, r, 0:8], values_[:, r, 0:8], row(r)))
            yield
            b_ = each(lambda r: dve.match_replace(spare(r), values_[:, r, 0:8], row(r), LOW))
            yield
            need("dve", *b_)
            c_ = each(lambda r: dve.max(values_[:, r, 8:16], spare(r)))
            yield
            need("dve", *c_)
            yield each(lambda r: dve.max_index(index[:, r, 8:16], values_[:, r, 8:16], spare(r)))

        t_qT = []
        scores_read = []
        flat = lambda ap: ap.rearrange("p h k -> p (h k)")

        def route(i, q, batch):
            bi, bufs, bfree = batches.take()
            batch.update(index=bi, **bufs)
            t_sc = []
            for u in range(2):
                b, bank, free = psum.take()
                need("pe", *free, t_sub, *t_qT[0:8 * (q + 1)])
                for v in range(4):
                    r = 4 * u + v
                    last = pe.matmul(bank[:, v * P:(v + 1) * P], qT[:, 8 * q + r, i * P:(i + 1) * P], subkeys[:, 8 * q + r, :],
                                     start=True, stop=True)
                t = mark(last, "pe_route")
                need("act", t, *scores_read)
                t_sc.append(mark(act.activation(scores[:, 4 * u:4 * u + 4, :].rearrange("p r k -> p (r k)"), bank[:, :], ACT.Copy), "act_route"))
                psum.release(b, t_sc[-1])
            yield
            for t in top16(2 * BH, lambda r: scores[:, r, :], lambda r: left[:, r, :], top, topi, t_sc):
                yield
            need("dve", *t)
            by_head = top[:].rearrange("p (h a) k -> p h a k", a=2)
            t = mark(dve.tensor_tensor(cand, by_head[:, :, 0, :].unsqueeze(3).to_broadcast([P, BH, TOPK, TOPK]),
                                       by_head[:, :, 1, :].unsqueeze(2).to_broadcast([P, BH, TOPK, TOPK]), ALU.add), "dve_route")
            yield
            for t in top16(BH, lambda r: cand_rows[:, r, :], lambda r: rest2[:, r, :], best, besti, [t]):
                yield
            need("dve", *t, *bfree)
            g, e = batch["gate"], batch["expert"]
            t = mark(dve.tensor_tensor(g[:], best[:], best[:, :, 0:1].to_broadcast([P, BH, TOPK]), ALU.subtract), "dve_route")
            need("act", t)
            t_exp = mark(act.activation(flat(g[:]), flat(g[:]), ACT.Exp), "act_route")
            t1 = mark(dve.tensor_scalar(flat(part[:, 0]), flat(besti[:]), 4, None, ALU.logical_shift_right), "dve_route")
            t2 = mark(dve.tensor_scalar(flat(part[:, 1]), flat(besti[:]), 15, None, ALU.bitwise_and), "dve_route")
            need("dve", t1, t2)
            t1 = mark(dve.tensor_copy(partf[:].rearrange("p a h k -> p (a h k)"), part[:].rearrange("p a h k -> p (a h k)")), "dve_route")
            t2 = mark(dve.tensor_copy(flat(topf[:]), flat(topi[:])), "dve_route")
            need("dve", t1, t2, t_count)
            yield
            topf_h = topf[:].rearrange("p (h a) k -> p h a k", a=2)
            for a, hot in enumerate((cand, rest2.rearrange("p h (a b) -> p h a b", a=TOPK))):
                t = mark(dve.tensor_tensor(hot, partf[:, a].unsqueeze(3).to_broadcast([P, BH, TOPK, TOPK]),
                                           count[:].unsqueeze(1).unsqueeze(1).to_broadcast([P, BH, TOPK, TOPK]), ALU.is_equal), "dve_route")
                need("dve", t)
                t = mark(dve.tensor_tensor(hot, hot, topf_h[:, :, a, :].unsqueeze(2).to_broadcast([P, BH, TOPK, TOPK]), ALU.mult), "dve_route")
                yield
                need("dve", t)
                t = mark(dve.tensor_reduce(picked[:, a], hot, AX_X, ALU.add), "dve_route")
                need("dve", t)
                yield
            batch["t_expert"] = mark(dve.scalar_tensor_tensor(e[:], flat(picked[:, 0]), float(NKEY), flat(picked[:, 1]),
                                                              ALU.mult, ALU.add), "dve_route")
            need("dve", t_exp)
            t = mark(dve.tensor_reduce(gsum[:, 0, :], g[:], AX_X, ALU.add), "dve_route")
            need("dve", t)
            t = mark(dve.reciprocal(gsum[:, 1, :], gsum[:, 0, :]), "dve_route")
            need("dve", t)
            t = mark(dve.tensor_tensor(g[:], g[:], gsum[:, 1, :].unsqueeze(2).to_broadcast([P, BH, TOPK]), ALU.mult), "dve_route")
            batch["t_gate"] = t
            scores_read[:] = [t]
            need("dve", t, batch["t_expert"])

        order = [(i, q) for i in range(NT) for q in range(2)]
        batch = {}
        routing = route(*order[0], batch)
        for u in range(4):
            w, arrived, free_w = weights("w_pq", u, KC, 512)
            need("pe", arrived, *t_h2T)
            for v in range(4):
                b, bank, free = psum.take()
                need("pe", *free)
                t = chain(bank[:, :], [(w[:, c, v * P:(v + 1) * P], h2T[:, c, :]) for c in range(KC)], "pe_pq")
                need("act", t)
                t_qT.append(mark(act.activation(qT[:, 4 * u + v, :], bank[:, :], ACT.Copy), "act_pq"))
                psum.release(b, t_qT[-1])
            free_w.append(t)
            if u == 1:
                for _ in routing:
                    pass
        t_pq = t
        slots = Ring([sig_a[:, a:a + 4, :].rearrange("p a n -> p (a n)") for a in (0, 4)]
                     + [wring.buffers[(wring.at + k) % 3][:, a:a + 2 * D] for k in range(3) for a in (0, 2 * D)]
                     + [merged[:, a:a + 4, :].rearrange("p a n -> p (a n)") for a in (0, 4)])
        for k in range(2):
            slots.free[k] += t_sq4
        for k in range(6):
            slots.free[2 + k] += wring.free[(wring.at + k // 2) % 3]
        for k in range(2):
            slots.free[8 + k] += [t_pq]

        def gather(batch, j):
            s, slot, free = slots.take()
            need("pool", batch["t_expert"], *free)
            t = mark(pool.indirect_dma_start(slot, None, A["experts"],
                                             bass.IndirectOffsetOnAxis(ap=batch["expert"][:, j:j + 1], axis=0)), f"ld_slot{s}", 16)
            return s, slot, t

        for n, (i, q) in enumerate(order):
            now, batch = batch, {}
            routing = route(*order[n + 1], batch) if n + 1 < len(order) else iter(())
            g, hid, cf = now["gate"], now["hidden"], now["coef"]
            if q == 0:
                ob, opair, ofree = psum.take(2)
                need("pe", *ofree)
            for j0 in range(0, PICKS, GROUP):
                group = range(j0, j0 + GROUP)
                gathered = {j: gather(now, j) for j in group}
                for j in group:
                    s, slot, t = gathered[j]
                    need("dve", t)
                    t = mark(dve.tensor_tensor_reduce(slot[:, 0:D], slot[:, 0:D], h2[:, i, :], 1.0, 0.0, ALU.mult, ALU.add,
                                                      hid[:, j:j + 1]), "dve_hidden")
                need("act", t)
                t = mark(act.activation(cf[:, j0:j0 + GROUP], hid[:, j0:j0 + GROUP], ACT.Gelu), "act_gelu")
                need("dve", t, now["t_gate"])
                t = mark(dve.tensor_tensor(cf[:, j0:j0 + GROUP], cf[:, j0:j0 + GROUP], flat(g[:])[:, j0:j0 + GROUP], ALU.mult), "dve_coef")
                need("act", t)
                for j in group:
                    s, slot, arrived = gathered[j]
                    di, dg, dfree = diags.take()
                    need("act", *dfree)
                    t = mark(act.activation(dg, ident[:], ACT.Copy, scale=cf[:, j:j + 1]), "act_diag")
                    need("pe", t, arrived)
                    for half in range(2):
                        last = pe.matmul(opair[:, half, :], dg, slot[:, D + half * 512:D + (half + 1) * 512],
                                         start=q == 0 and j == 0, stop=q == 1 and j == PICKS - 1)
                    t_acc = mark(last, "pe_peer")
                    slots.free[s].append(t_acc)
                    diags.free[di].append(t_acc)
                if j0:
                    for _ in range(2):
                        next(routing, None)
            for _ in routing:
                pass
            batches.free[now["index"]].append(t_acc)
            if q == 0:
                continue
            y = h2[:, i, :]
            need("dve", t_acc)
            t = mark(dve.tensor_tensor(y.rearrange("p (a n) -> p a n", a=2), opair, rows_["g2"].rearrange("p (a n) -> p a n", a=2), ALU.mult), "dve_last")
            psum.release(ob, t, n=2)
            need("dve", t)
            t = mark(dve.tensor_tensor(x[:, i, :], x[:, i, :], y, ALU.add), "dve_last")
            need("dve", t)
            t = token_rstd(x[:, i, :], P, i, y, t, "last")
            need("dve", t, t_final2)
            t = mark(dve.scalar_tensor_tensor(y, x[:, i, :], stat[:, 2, i:i + 1], final2[:], ALU.mult, ALU.mult), "dve_last")
            need("sp", t)
            t_store = mark(sp.dma_start(out[i * P:(i + 1) * P, :], y), "st_out", 16)
        need("sp", t_store)
        peer.close()
        rest.close()
        block2.close()
        late.close()


def constants():
    c = {"ident": np.eye(P, dtype=np.float32)}
    n = np.arange(P)
    pos = (np.arange(NK) + PREFIX - META).astype(np.float64)
    half = RDK // 2
    inv = (1.0 / (np.float32(10000.0) ** (np.arange(half, dtype=np.float32) / np.float32(half)))).astype(np.float32)
    ang = (pos.astype(np.float32)[None, :] * inv[:, None]).astype(np.float32).astype(np.float64)
    cos, sin = np.cos(ang), np.sin(ang)
    log_g = np.log1p(-np.exp2(-5.0 - np.arange(RH)))
    rope1 = np.zeros((4, P, 2, NK))
    mid = pos.mean()
    for j in range(4):
        for s in range(2):
            h = 2 * (j % 2) + s
            decay = np.exp((pos - mid) * log_g[h]) if j < 2 else RDK ** -0.5 * np.exp((mid - pos) * log_g[h])
            for k in range(RDK):
                r = s * RDK + k
                rope1[j, r, 0] = cos[k % half] * decay
                rope1[j, r, 1] = (-sin[k] if k < half else sin[k - half]) * decay
    c["rope1"] = rope1.astype(np.float32)
    swap = np.zeros((P, P), np.float32)
    for b in range(P):
        swap[b + half if b % RDK < half else b - half, b] = 1
    c["swap1"] = swap
    d = n[:, None] - n[None, :]
    same = (n[:, None] // CHUNK) == (n[None, :] // CHUNK)
    c["ret_diag"] = np.stack([np.where(d <= 0, 1.0, np.where(same, np.exp(2.0 * d * log_g[h]), 0.0)) for h in range(RH)],
                             axis=1).astype(np.float32)
    c["causal"] = np.where(d >= 0, 0.0, NEG).astype(np.float32)
    c["sel"] = np.repeat(np.eye(FH, dtype=np.float32)[:, :, None], P, axis=2)
    nf = ROPE // 4
    freq = (np.float32(10000.0) ** (-np.arange(nf, dtype=np.float32) / np.float32(nf))).astype(np.float32)
    t = np.arange(SEQ)
    angle = np.stack([(t // 64)[:, None].astype(np.float32) * freq, (t % 64)[:, None].astype(np.float32) * freq], axis=1)
    angle = angle.astype(np.float32).astype(np.float64)
    rope2 = np.zeros((P, 2, SEQ))
    swap2 = np.zeros((P, P), np.float32)
    for r in range(P):
        a, b, f = (r % ROPE) // 16, (r % 16) // nf, r % nf
        rope2[r, 0] = np.cos(angle[:, a, f])
        rope2[r, 1] = np.sin(angle[:, a, f]) * (-1 if b == 0 else 1)
        swap2[r + nf if b == 0 else r - nf, r] = 1
    c["rope2"] = rope2.astype(np.float32)
    c["swap2"] = swap2
    c["count16"] = np.repeat(np.arange(TOPK, dtype=np.float32)[None], P, axis=0)
    return c


def units(w, pieces, k=KC):
    w3 = w.reshape(k, P, -1).transpose(1, 0, 2)
    out = np.zeros((len(pieces), P, UNIT), w.dtype)
    for u, ranges in enumerate(pieces):
        block = np.concatenate([w3[:, :, a:b] for a, b in ranges], axis=2)
        out[u, :, 0:block.shape[1] * block.shape[2]] = block.reshape(P, -1)
    return out


def plain(n):
    return [[(a, a + 512)] for a in range(0, n, 512)]


def arrange(i):
    f = {k: np.ascontiguousarray(v) for k, v in i.items()}
    a = dict(constants())
    a["x"] = f["x"][0]
    a["meta"] = f["meta_tokens"]
    w = f["w_in"][0]
    a["w_in_v"] = units(w, [[(512, 1024)], [(2560, 3072)]])
    a["w_in_t"] = units(w, [[(0, 512)], [(1024, 1536)], [(1536, 2048)], [(2048, 2560)]])
    a["w_ff"] = w[:, 3072:3080].reshape(KC, P, FH).transpose(1, 0, 2)
    a["fox_b"] = f["fox_forget_b"].reshape(FH, 1)
    a["w_out"] = units(f["w_out"][0], plain(D))
    a["w_up"] = units(f["w_up"][0], [[(256 * u, 256 * u + 256), (F + 256 * u, F + 256 * u + 256)] for u in range(NF // 2)])
    wd = f["w_down"][0]
    down = []
    for half in range(2):
        for f0, f1 in ((0, 8), (8, 16), (16, NF)):
            down.append(units(wd[f0 * P:f1 * P], [[(half * 512, half * 512 + 512)]], f1 - f0))
    a["w_down"] = np.concatenate(down)
    col = lambda v: v.reshape(-1, P).T
    cols = dict(attn_g=col(f["attn_norm_g"][0]), ret_g=col(f["ret_norm_g"][0]), ffn_g=col(f["ffn_norm_g"][0]),
                conv_w=col(f["conv_w"][0].reshape(-1)), conv_b=col(f["conv_b"][0]), norm1_g=col(f["norm1_g_2"][0]),
                q_g=col(f["q_norm_g_2"][0]), kv_g=col(f["kv_norm_g_2"][0]), dw_w=col(f["conv_w_2"][0].reshape(-1)),
                dw_b=col(f["conv_b_2"][0]), ln_g=col(f["conv_ln_g_2"][0]), ln_b=col(f["conv_ln_b_2"][0]),
                cond=np.stack([col(f["c_2"][0]), col(f["c_ctx_2"])], axis=2).reshape(P, -1),
                b_mod=col(f["b_mod_2"][0]))
    a["cols"] = np.concatenate([cols[k] for k in COLUMNS], axis=1)
    a["ctx"] = f["ctx_2"][0].reshape(2, P, D).transpose(1, 0, 2)
    rows = lambda v: np.repeat(v.reshape(1, D), P, axis=0)
    a["final1"], a["norm2_g"], a["final_g"] = rows(f["final_norm_g"]), rows(f["norm2_g_2"]), rows(f["final_g_2"])
    a["w_mod"] = units(f["w_mod_2"][0], plain(6 * D))
    w = f["w_in_2"][0]
    conv0, gate0 = 416, 416 + 2 * D
    a["w_in2"] = units(w, [[(0, 416)]] + [[(conv0 + 256 * u, conv0 + 256 * u + 256),
                                          (conv0 + D + 256 * u, conv0 + D + 256 * u + 256)] for u in range(4)]
                       + [[(gate0 + 512 * u, gate0 + 512 * u + 512)] for u in range(4)])
    uq = f["w_uq_2"][0].reshape(256, AH, QK)
    uq = np.concatenate([uq[:, :, 0:NOPE].reshape(256, -1), uq[:, :, NOPE:].reshape(256, -1)], axis=1)
    a["w_uq"] = units(uq, [[(0, 1536)]], 2)
    ukv = f["w_ukv_2"][0].reshape(P, AH, NOPE + VD)
    ukv = np.concatenate([ukv[:, :, 0:NOPE].reshape(P, -1), ukv[:, :, NOPE:].reshape(P, -1)], axis=1)
    a["w_ukv"] = units(ukv, [[(0, 2048)]], 1)
    a["w_o_mla"] = units(f["w_o_mla_2"][0], plain(D))
    a["w_pw"] = units(f["w_pw_2"][0], plain(D))
    a["w_out2"] = units(f["w_out_2"][0], plain(D))
    a["w_pq"] = units(f["w_pq_2"][0], plain(2048))
    a["sub_keys"] = f["sub_keys_2"][0].reshape(2 * PH, NKEY, P).transpose(2, 0, 1)
    a["experts"] = np.concatenate([f["u_experts_2"][0], f["v_experts_2"][0]], axis=1)
    return {k: np.ascontiguousarray(v) for k, v in a.items()}


def kernel(**inputs):
    import concourse.bacc as bacc
    from concourse.bass_utils import run_bass_kernel_spmd

    nc = bacc.Bacc("TRN2", target_bir_lowering=False, num_devices=1)
    arrays = arrange(inputs)
    A = {name: nc.dram_tensor(f"in_{name}", a.shape, mybir.dt.from_np(a.dtype), kind="ExternalInput").ap()
         for name, a in arrays.items()}
    out = nc.dram_tensor("out_y", (SEQ, D), F32, kind="ExternalOutput").ap()
    program(nc, A, out)
    r = run_bass_kernel_spmd(nc, [{f"in_{name}": a for name, a in arrays.items()}], core_ids=[0])
    return r.results[0]["out_y"].reshape(1, SEQ, D)
```

```python
from contextlib import ExitStack
from itertools import chain as chained

import numpy as np

import concourse.bass as bass
from concourse import mybir
from concourse.alu_op_type import AluOpType as ALU

ACT = mybir.ActivationFunctionType
F32 = mybir.dt.float32
BF16 = mybir.dt.bfloat16
U32 = mybir.dt.uint32
AX_X = mybir.AxisListType.X

P = 128
SEQ, D = 512, 1024
KC = D // P
NT = SEQ // P
META, PREFIX = 16, 128
NK = META + SEQ
HALF = NK // 2
EPS = 1e-6
NEG = -1e30
RH, RDK, RDV, CHUNK = 4, 64, 128, 64
FH, FDH = 8, 64
F = 2816
NF = F // P
CTX = 256
NKV = SEQ + CTX
AH, NOPE, ROPE, VD = 16, 64, 32, 64
QK = NOPE + ROPE
TAPS = 31
PH, TOPK, NKEY = 8, 16, 128
NEXP = NKEY * NKEY
UNIT = 4096
BANK = 512

COLUMNS = dict(attn_g=KC, ret_g=RH, ffn_g=KC, conv_w=3 * NF, conv_b=NF, norm1_g=KC, q_g=2, kv_g=1,
               dw_w=TAPS * KC, dw_b=KC, ln_g=KC, ln_b=KC, cond=2 * KC, b_mod=6 * KC)


def column_places():
    at, places = 0, {}
    for name, n in COLUMNS.items():
        places[name] = (at, at + n)
        at += n
    return places, at


class Sync:

    def __init__(self, nc, ctx):
        self.nc, self.ctx = nc, ctx
        self.engines = {"pe": nc.tensor, "dve": nc.vector, "act": nc.scalar, "pool": nc.gpsimd, "sp": nc.sync}
        self.sems, self.count, self.last = {}, {}, {}
        self.seen = {e: {} for e in self.engines}

    def mark(self, ins, name, by=1):
        if name not in self.sems:
            self.sems[name] = self.ctx.enter_context(self.nc.semaphore(name))
            self.count[name] = 0
        ins.then_inc(self.sems[name], by)
        self.count[name] += by
        token = (name, self.count[name])
        if by == 1:
            self.last[name.split("_")[0]] = token
        return token

    def need(self, engine, *tokens):
        for t in tokens:
            if t is None:
                continue
            if isinstance(t, list):
                self.need(engine, *t)
                continue
            name, value = t
            if self.seen[engine].get(name, 0) < value:
                self.seen[engine][name] = value
                self.engines[engine].wait_ge(self.sems[name], value)

    def fence(self, engines=("dve", "act", "pool")):
        for e in engines:
            self.need(e, *[t for who, t in self.last.items()])


class Ring:

    def __init__(self, buffers):
        self.buffers, self.free, self.at = buffers, [[] for _ in buffers], 0

    def take(self):
        i = self.at % len(self.buffers)
        self.at += 1
        free, self.free[i] = self.free[i], []
        return i, self.buffers[i], free


class Psum:

    def __init__(self, tensor):
        self.tensor, self.free, self.at, self.held = tensor, [[] for _ in range(8)], 0, set()

    def take(self, n=1):
        while self.at % n or any((self.at + k) % 8 in self.held for k in range(n)):
            self.at += 1
        b = self.at % 8
        self.at += n
        free = sum(self.free[b:b + n], [])
        for k in range(b, b + n):
            self.free[k] = []
            self.held.add(k)
        return b, (self.tensor[:, b, :] if n == 1 else self.tensor[:, b:b + 2, :]), free

    def release(self, b, *tokens, n=1):
        for k in range(b, b + n):
            self.free[k] += tokens
            self.held.discard(k)


def program(nc, A, out):
    ctx = ExitStack()
    with ctx:
        S = Sync(nc, ctx)
        mark, need = S.mark, S.need
        pe, dve, act, pool, sp = nc.tensor, nc.vector, nc.scalar, nc.gpsimd, nc.sync

        def sb(stack, name, shape, dt=F32):
            return stack.enter_context(nc.sbuf_tensor(name, shape, dt))

        psum = Psum(ctx.enter_context(nc.psum_tensor("psum", [P, 8, BANK], F32)))

        ident = sb(ctx, "ident", [P, P])
        ident16 = sb(ctx, "ident16", [P, P], BF16)
        ones = sb(ctx, "ones", [P, P])
        eps = sb(ctx, "eps", [P, 1])
        places, n_columns = column_places()
        cols = sb(ctx, "cols", [P, n_columns])
        x = sb(ctx, "x", [P, NT, D])
        spare_row = sb(ctx, "spare_row", [P, D])
        stat = sb(ctx, "stat", [P, 3, 8])

        def col(name, i=0, n=1):
            a = places[name][0] + i
            return cols[:, a:a + n]

        t_x = [mark(sp.dma_start(x[:, i, :], A["x"][i * P:(i + 1) * P, :]), f"ld_x{i}", 16) for i in range(NT)]
        t_const = [mark(act.dma_start(ident[:], A["ident"]), "ld_const", 16),
                   mark(act.dma_start(cols[:], A["cols"]), "ld_const", 16)][-1]
        t_ones = [mark(pool.memset(ones[:], 1.0), "pool_const"), mark(pool.memset(eps[:], EPS), "pool_const")][-1]
        need("dve", t_const)
        t_ident16 = mark(dve.tensor_copy(ident16[:], ident[:]), "dve_const")

        wring = Ring([sb(ctx, f"weights{i}", [P, UNIT]) for i in range(3)])

        def weights(name, unit, k, n):
            i, buffer, free = wring.take()
            need("sp", *free)
            view = buffer[:, 0:k * n]
            arrived = mark(sp.dma_start(view, A[name][unit][:, 0:k * n]), f"ld_weights{i}", 16)
            return view.rearrange("p (k n) -> p k n", k=k), arrived, wring.free[i]

        def chain(out_ap, pairs, name, start=True, stop=True):
            for k, (lhsT, rhs) in enumerate(pairs):
                last = pe.matmul(out_ap, lhsT, rhs, start=start and k == 0, stop=stop and k == len(pairs) - 1)
            return mark(last, name)

        def token_rstd(src, n, j, scratch, arrived, name):
            need("act", arrived, t_const, t_ones)
            t = mark(act.activation(scratch[0:n, :], src, ACT.Square, accum_out=stat[0:n, 0, j:j + 1]), f"act_{name}")
            need("act", t)
            t = mark(act.activation(stat[0:n, 1, j:j + 1], stat[0:n, 0, j:j + 1], ACT.Sqrt, bias=eps[0:n, :],
                                    scale=1.0 / D), f"act_{name}")
            need("dve", t)
            return mark(dve.reciprocal(stat[0:n, 2, j:j + 1], stat[0:n, 1, j:j + 1]), f"dve_{name}")

        def transposed(src, tiles_, dst, scale, shift, name, ready, at=0):
            done = []
            for i in tiles_:
                b, pair, free = psum.take(2)
                need("pe", *free, t_const, ready[i])
                for c in range(KC):
                    last = pe.transpose(pair[:, c // 4, (c % 4) * P:(c % 4 + 1) * P], src[:, i, c * P:(c + 1) * P], ident[:])
                    if c % 4 == 3:
                        t = mark(last, f"pe_{name}")
                        for k in range(c - 3, c + 1):
                            o, part = dst[:, k, at + i * P:at + (i + 1) * P], pair[:, c // 4, (k % 4) * P:(k % 4 + 1) * P]
                            engine = "act" if c > 3 else "dve"
                            need(engine, t)
                            if engine == "act":
                                ins = act.activation(o, part, ACT.Identity, scale=scale[k], bias=shift[k] if shift else 0.0)
                            elif shift:
                                ins = dve.tensor_scalar(o, part, scale[k], shift[k], ALU.mult, ALU.add)
                            else:
                                ins = dve.tensor_scalar(o, part, scale[k], None, ALU.mult)
                            t_k = mark(ins, f"{engine}_{name}")
                        psum.release(b + c // 4, t_k)
                        done.append(t_k)
            return [done[2 * i:2 * i + 2] for i in range(len(done) // 2)]

        def meta_transposed(src, dst, gain, name, ready):
            b, bank, free = psum.take()
            need("pe", *free, ready)
            for c in range(KC):
                last = pe.transpose(bank[:, c * META:(c + 1) * META], src[:, c * P:(c + 1) * P], ident[0:META, 0:META])
            t = mark(last, f"pe_{name}")
            need("dve", t)
            t = mark(dve.tensor_tensor(dst[:, :, 0:META], bank[:, 0:KC * META].rearrange("p (c m) -> p c m", c=KC),
                                       gain.unsqueeze(2).to_broadcast([P, KC, META]), ALU.mult), f"dve_{name}")
            psum.release(b, t)
            return t

        def halves(ap):
            return ap.rearrange("p (a n) -> p a n", a=2)

        def project_halves(w, k0, n, src, name, ready, m=P):
            b, pair, free = psum.take(2)
            need("pe", *free, *ready)
            for a in range(2):
                t = chain(pair[0:m, a, 0:HALF], [(w[:, c, k0:k0 + m], src[:, c, a * HALF:(a + 1) * HALF])
                                                 for c in range(KC)], name)
            return b, pair[0:m, :, 0:HALF], t

        mixer = ctx.enter_context(ExitStack())
        xm = spare_row[0:META, :]
        xnT = sb(mixer, "xnT", [P, KC, NK])
        mixedT = sb(mixer, "mixedT", [P, KC, NK])
        rv = sb(mixer, "rv", [P, NT + 1, RH * RDV])
        fv = sb(mixer, "fv", [P, NT + 1, FH * FDH])
        rqk = sb(mixer, "rqk", [P, 4, NK])
        fqk = sb(mixer, "fqk", [P, 8, NK])
        silu_rg = sb(mixer, "silu_rg", [P, RH, NK])
        t_xm = mark(sp.dma_start(xm[:], A["meta"]), "ld_meta", 16)

        first = ctx.enter_context(ExitStack())
        xn = sb(first, "xn", [P, NT, D])
        xnm = sb(first, "xnm", [META, D])[:]
        scratch = sb(first, "scratch", [P, D])

        def normalise(name, t_src, t_src_m, meta=META):
            ready = []
            for i in range(NT):
                t = token_rstd(x[:, i, :], P, i, scratch, t_src[i], name)
                need("dve", t)
                ready.append(mark(dve.tensor_scalar(xn[:, i, :], x[:, i, :], stat[:, 2, i:i + 1], None, ALU.mult), f"dve_{name}"))
            t = token_rstd(xm[:], META, 4, scratch, t_src_m, name)
            need("dve", t)
            ready_m = mark(dve.tensor_scalar(xnm, xm[:], stat[0:META, 2, 4:5], None, ALU.mult), f"dve_{name}")
            return ready, ready_m

        ready, ready_m = normalise("norm1", t_x, t_xm)
        t_xnT = transposed(xn, range(NT), xnT, [col("attn_g", c) for c in range(KC)], None, "norm1", ready, META)
        t_xnT.append(meta_transposed(xnm, xnT, col("attn_g", 0, KC), "norm1", ready_m))
        S.fence()
        t_first = list(S.last.values())
        first.close()

        second = ctx.enter_context(ExitStack())
        raw = Ring([sb(second, f"raw{i}", [P, NK]) for i in range(2)])
        turned = Ring([sb(second, f"turned{i}", [P, NK]) for i in range(2)])
        tables = Ring([sb(second, f"rope{i}", [P, 2, NK]) for i in range(2)])
        swap = sb(second, "swap", [P, P])
        forget = sb(second, "forget", [FH, 4, NK])
        wff = sb(second, "wff", [P, KC, FH])
        fb = sb(second, "fb", [FH, 1])
        sel = sb(second, "sel", [FH, FH, P])
        t_small = [mark(act.dma_start(d, A[n]), "ld_mixer", 16) for d, n in
                   ((swap[:], "swap1"), (wff[:], "w_ff"), (fb[:], "fox_b"), (sel[:], "sel"))][-1]

        t_v = {}
        for unit, (dst, key) in enumerate(((rv, "rv"), (fv, "fv"))):
            w, arrived, free_w = weights("w_in_v", unit, KC, 512)
            need("pe", arrived)
            for i in range(NT + 1):
                n, at = (P, META + i * P) if i < NT else (META, 0)
                b, bank, free = psum.take()
                need("pe", *free, t_xnT[i])
                t = chain(bank[0:n, :], [(xnT[:, c, at:at + n], w[:, c, :]) for c in range(KC)], "pe_values")
                need("act", t)
                t_v[key, i] = mark(act.activation(dst[0:n, i, :], bank[0:n, :], ACT.Copy), "act_values")
                psum.release(b, t_v[key, i])
            free_w.append(t)

        need("pe", t_small)
        b, pair, t = project_halves(wff, 0, FH, xnT, "pe_forget", t_xnT, FH)
        need("dve", t, t_small)
        z, e, m0, run = (forget[:, k, :] for k in range(4))
        t = mark(dve.tensor_scalar(halves(z), pair, fb[:, 0:1], None, ALU.add), "dve_forget")
        psum.release(b, t, n=2)
        need("dve", t)
        need("act", t)
        t2 = mark(act.activation(e, z, ACT.Abs), "act_forget")
        need("act", t2)
        t = mark(act.activation(e, e, ACT.Exp, scale=-1.0), "act_forget")
        need("act", t, t_ones)
        t = mark(act.activation(e, e, ACT.Ln, bias=ones[0:FH, 0:1]), "act_forget")
        t2 = mark(dve.tensor_scalar(m0, z, 0.0, None, ALU.min), "dve_forget")
        need("dve", t, t2)
        t = mark(dve.tensor_tensor(z, m0, e, ALU.subtract), "dve_forget")
        need("dve", t)
        t2 = mark(dve.memset(m0, 1.0), "dve_forget")
        need("dve", t, t2)
        t_run = mark(dve.tensor_tensor_scan(run, m0, z, 0.0, ALU.mult, ALU.add), "dve_forget")

        t_rqk = []
        w, arrived, free_w = weights("w_in_t", 0, KC, 512)
        for j in range(4):
            need("pe", arrived)
            b, pair, t = project_halves(w, j * P, P, xnT, "pe_rqk", [])
            r, rbuf, rfree = raw.take()
            need("act", t, *rfree)
            t_raw = mark(act.activation(halves(rbuf[:]), pair, ACT.Copy), "act_rqk")
            psum.release(b, t_raw, n=2)
            ti, table, tfree = tables.take()
            need("sp", *tfree, *t_first)
            t_table = mark(sp.dma_start(table[:], A["rope1"][j]), f"ld_rope{ti}", 16)
            b, pair, free = psum.take(2)
            need("pe", *free, t_raw, t_small)
            for a in range(2):
                t = chain(pair[:, a, 0:HALF], [(swap[:], rbuf[:, a * HALF:(a + 1) * HALF])], "pe_rqk")
            need("dve", t_raw, t_table)
            u, ubuf, ufree = turned.take()
            need("dve", *ufree)
            t1 = mark(dve.tensor_tensor(rqk[:, j, :], rbuf[:], table[:, 0, :], ALU.mult), "dve_rqk")
            need("dve", t)
            t2 = mark(dve.tensor_tensor(halves(ubuf[:]), pair[:, :, 0:HALF], halves(table[:, 1, :]), ALU.mult), "dve_rqk")
            psum.release(b, t2, n=2)
            tables.free[ti] += [t1, t2]
            raw.free[r] += [t1, t]
            need("dve", t1, t2)
            t3 = mark(dve.tensor_tensor(rqk[:, j, :], rqk[:, j, :], ubuf[:], ALU.add), "dve_rqk")
            turned.free[u].append(t3)
            t_rqk.append(t3)
        free_w.append(t)

        w, arrived, free_w = weights("w_in_t", 1, KC, 512)
        t_rg = []
        for j in range(RH):
            need("pe", arrived)
            b, pair, t = project_halves(w, j * P, P, xnT, "pe_rg", [])
            need("act", t)
            t_rg.append(mark(act.activation(halves(silu_rg[:, j, :]), pair, ACT.Silu), "act_rg"))
            psum.release(b, t_rg[-1], n=2)
        free_w.append(t)

        t_fqk = []
        for unit in range(2):
            w, arrived, free_w = weights("w_in_t", 2 + unit, KC, 512)
            for j in range(4):
                need("pe", arrived)
                b, pair, t = project_halves(w, j * P, P, xnT, "pe_fqk", [])
                need("act", t)
                t_fqk.append(mark(act.activation(halves(fqk[:, 4 * unit + j, :]), pair, ACT.Copy,
                                                 scale=(FDH ** -0.5 if unit == 0 else 1.0)), "act_fqk"))
                psum.release(b, t_fqk[-1], n=2)
            free_w.append(t)

        diag = sb(second, "diag", [P, RH, P])
        causal16 = sb(second, "causal16", [P, P], BF16)
        causal = sb(second, "causal", [P, P])
        t_diag = [mark(act.dma_start(d, A[n]), "ld_diag", 16) for d, n in ((diag[:], "ret_diag"), (causal[:], "causal"))][-1]
        need("dve", t_diag)
        t_causal = mark(dve.tensor_copy(causal16[:], causal[:]), "dve_mask")
        scoresT = Ring([sb(second, "scoresT0", [P, NT + 1, NK]), xnT[:, 0:NT + 1, :]])
        wide = Ring([sb(second, f"wide{i}", [P, NK]) for i in range(2)])

        def tiles():
            return [(NT, META, 0)] + [(j, P, META + j * P) for j in range(NT)]

        t_mixed = [None] * RH

        def retention_scores(h):
            rows = slice((h % 2) * RDK, (h % 2) * RDK + RDK)
            q, k = rqk[rows, h // 2, :], rqk[rows, 2 + h // 2, :]
            si, sT, sfree = scoresT.take()
            done = {}
            for j, n, at in tiles():
                b, pair, free = psum.take(2)
                need("pe", *free, *t_rqk)
                if j == NT:
                    for a in range(2):
                        t = chain(pair[0:n, a, 0:HALF], [(k[:, at:at + n], q[:, a * HALF:(a + 1) * HALF])], "pe_ret")
                    src, dst = pair[0:n, :, 0:HALF], halves(sT[0:n, j, :])
                else:
                    t = chain(pair[:, 0, 0:NK - at], [(k[:, at:at + n], q[:, at:NK])], "pe_ret")
                    src, dst = pair[:, 0, 0:NK - at], sT[:, j, at:NK]
                need("act", t, *sfree)
                t_copy = mark(act.activation(dst, src, ACT.Copy), "act_ret")
                psum.release(b, t_copy, n=2)
                need("dve", t_copy, t_diag)
                done[j] = mark(dve.tensor_tensor(sT[0:n, j, at:at + n], sT[0:n, j, at:at + n], diag[0:n, h, 0:n], ALU.mult), "dve_ret")
            return si, sT, done

        def retention_values(h, si, sT, done):
            b, pair, free = psum.take(2)
            need("pe", *free)
            for j, n, at in tiles()[1:] + tiles()[:1]:
                need("pe", t_v["rv", j], done[j])
                v = rv[0:n, j, h * RDV:(h + 1) * RDV]
                if j == NT:
                    pe.matmul(pair[:, 1, 0:META], v, sT[0:n, j, 0:META], start=True, stop=True)
                    last = pe.matmul(pair[:, 0, 0:SEQ], v, sT[0:n, j, META:NK], start=False, stop=True)
                else:
                    pe.matmul(pair[:, 0, at - META:SEQ], v, sT[:, j, at:NK], start=j == 0, stop=False)
            t_o = mark(last, "pe_ret")
            scoresT.free[si].append(t_o)
            wi, obuf, ofree = wide.take()
            need("act", t_o, *ofree)
            mark(act.activation(obuf[:, META:NK], pair[:, 0, 0:SEQ], ACT.Copy), "act_ret")
            t_oc = mark(act.activation(obuf[:, 0:META], pair[:, 1, 0:META], ACT.Copy), "act_ret")
            psum.release(b, t_oc, n=2)
            r, sq, rfree = raw.take()
            need("act", t_oc, *rfree)
            t_sq = mark(act.activation(sq[:], obuf[:], ACT.Square), "act_ret")
            return wi, obuf, t_oc, r, sq, t_sq

        def retention_norm(h, wi, obuf, t_oc, r, sq, t_sq):
            b, pair, free = psum.take(2)
            need("pe", *free, t_sq, t_ones)
            for a in range(2):
                t = chain(pair[:, a, 0:HALF], [(ones[:], sq[:, a * HALF:(a + 1) * HALF])], "pe_ret")
            raw.free[r].append(t)
            u, root, ufree = turned.take()
            need("act", t, *ufree)
            t_root = mark(act.activation(halves(root[:]), pair[:, :, 0:HALF], ACT.Sqrt, bias=eps[:, :], scale=1.0 / RDV), "act_ret")
            psum.release(b, t_root, n=2)
            need("dve", t_root)
            t = mark(dve.reciprocal(root[:], root[:]), "dve_ret")
            need("dve", t, t_oc)
            t = mark(dve.tensor_tensor(obuf[:], obuf[:], root[:], ALU.mult), "dve_ret")
            turned.free[u].append(t)
            need("dve", t, t_rg[h])
            t = mark(dve.scalar_tensor_tensor(mixedT[:, h, :], obuf[:], col("ret_g", h), silu_rg[:, h, :],
                                              ALU.mult, ALU.mult), "dve_ret")
            wide.free[wi].append(t)
            t_mixed[h] = t

        ahead = retention_scores(0)
        for h in range(RH):
            now, ahead = ahead, retention_scores(h + 1) if h + 1 < RH else None
            sums = retention_values(h, *now)
            if h:
                retention_norm(h - 1, *before)
            before = sums
        retention_norm(RH - 1, *before)

        S.fence(("dve", "act"))
        third = ctx.enter_context(ExitStack())
        bias = Ring([raw.buffers[0], raw.buffers[1]])
        logits = Ring([wide.buffers[0], wide.buffers[1], turned.buffers[0], turned.buffers[1]])
        negmax = sb(third, "negmax", [P, 4, 4])
        pT = Ring(scoresT.buffers)
        small = Ring([negmax[:, i, :] for i in range(4)])

        def fox_bias(h):
            b, pair, free = psum.take(2)
            need("pe", *free, t_run, t_small)
            for a in range(2):
                t = chain(pair[:, a, 0:HALF], [(sel[:, h, :], run[:, a * HALF:(a + 1) * HALF])], "pe_bias")
            bi, negc, bfree = bias.take()
            need("act", t, *bfree)
            t = mark(act.activation(halves(negc[:]), pair[:, :, 0:HALF], ACT.Copy, scale=-1.0), "act_fox")
            psum.release(b, t, n=2)
            return bi, negc, t

        def fox_scores(h, i, n, at, head):
            bi, negc, t_negc = head["bias"]
            rows = slice((h % 2) * FDH, (h % 2) * FDH + FDH)
            q, k = fqk[rows, h // 2, :], fqk[rows, 4 + h // 2, :]
            b, pair, free = psum.take(2)
            need("pe", *free, *t_fqk, t_causal)
            width = META if i == NT else at + P
            if i == NT:
                pe.matmul(pair[0:n, 0, 0:n], q[:, 0:n], k[:, 0:n], start=True, stop=False)
                last = pe.matmul(pair[0:n, 0, 0:n], ident16[0:n, 0:n], causal16[0:n, 0:n], start=False, stop=True)
                view, shape = pair[0:n, 0, 0:n], (lambda ap: ap)
            elif width <= BANK:
                pe.matmul(pair[:, 0, 0:width], q[:, at:at + n], k[:, 0:width], start=True, stop=True)
                last = pe.matmul(pair[:, 0, at:width], ident16[:], causal16[:], start=False, stop=True, skip_group_check=True)
                view, shape = pair[:, 0, 0:width], (lambda ap: ap)
            else:
                pe.matmul(pair[:, 0, 0:HALF], q[:, at:at + n], k[:, 0:HALF], start=True, stop=True)
                pe.matmul(pair[:, 1, 0:HALF], q[:, at:at + n], k[:, HALF:NK], start=True, stop=True)
                last = pe.matmul(pair[:, 1, at - HALF:HALF], ident16[:], causal16[:], start=False, stop=True, skip_group_check=True)
                view, shape = pair[:, :, 0:HALF], halves
            t = mark(last, "pe_fox")
            li, L, lfree = logits.take()
            ni, nm, nfree = small.take()
            need("dve", t, t_negc, *lfree, *nfree)
            t_max = mark(dve.tensor_tensor_reduce(shape(L[0:n, 0:width]), view, shape(negc[0:n, 0:width]), 1.0, NEG * 1e8,
                                                  ALU.add, ALU.max, nm[0:n, 0:1]), "dve_fox")
            psum.release(b, t_max, n=2)
            if i == NT - 1:
                bias.free[bi].append(t_max)
            need("dve", t_max)
            t = mark(dve.tensor_scalar(nm[0:n, 1:2], nm[0:n, 0:1], -1.0, None, ALU.mult), "dve_fox")
            need("act", t, t_max)
            t = mark(act.activation(L[0:n, 0:width], L[0:n, 0:width], ACT.Exp, bias=nm[0:n, 1:2],
                                    accum_out=nm[0:n, 2:3]), "act_fox")
            return dict(h=h, i=i, n=n, at=at, width=width, li=li, L=L, ni=ni, nm=nm, exp=t, head=head)

        def fox_weights(c):
            n, L, nm, width = c["n"], c["L"], c["nm"], c["width"]
            need("dve", c["exp"])
            t = mark(dve.reciprocal(nm[0:n, 3:4], nm[0:n, 2:3]), "dve_fox")
            need("dve", t)
            c["p"] = mark(dve.tensor_scalar(L[0:n, 0:width], L[0:n, 0:width], nm[0:n, 3:4], None, ALU.mult), "dve_fox")
            small.free[c["ni"]].append(c["p"])

        def fox_transpose(c):
            i, n, at, L, head = c["i"], c["n"], c["at"], c["L"], c["head"]
            if "pt" not in head:
                head["pt"] = pT.take()
            pi, pt, pfree = head["pt"]
            b, pair, free = psum.take(2)
            need("pe", *free, c["p"])
            if i == NT:
                t = mark(pe.transpose(pair[0:n, 0, 0:n], L[0:n, 0:n], ident[0:n, 0:n]), "pe_fox")
                need("act", t, *pfree)
                head["done"].append(mark(act.activation(pt[0:n, NT, 0:n], pair[0:n, 0, 0:n], ACT.Copy), "act_fox"))
                psum.release(b, head["done"][-1], n=2)
            else:
                t_m = mark(pe.transpose(pair[0:META, 1, 0:P], L[:, 0:META], ident[:]), "pe_fox")
                for j in range(i + 1):
                    last = pe.transpose(pair[:, 0, j * P:(j + 1) * P], L[:, META + j * P:META + (j + 1) * P], ident[:])
                t = mark(last, "pe_fox")
                need("dve", t_m, *pfree)
                head["done"].append(mark(dve.tensor_copy(pt[0:META, NT, at:at + P], pair[0:META, 1, 0:P]), "dve_fox"))
                psum.release(b + 1, head["done"][-1])
                need("act", t, *pfree)
                head["done"].append(mark(act.activation(pt[:, 0:i + 1, at:at + P],
                                                        pair[:, 0, 0:(i + 1) * P].rearrange("p (j t) -> p j t", t=P), ACT.Copy), "act_fox"))
                psum.release(b, head["done"][-1])
            logits.free[c["li"]].append(t)

        def fox_values(h, head):
            rows = slice((h % 2) * FDH, (h % 2) * FDH + FDH)
            pi, pt, _ = head["pt"]
            b, pair, free = psum.take(2)
            need("pe", *free, *head["done"])
            for j, n, at in tiles()[1:] + tiles()[:1]:
                need("pe", t_v["fv", j])
                v = fv[0:n, j, h * FDH:(h + 1) * FDH]
                if j == NT:
                    pe.matmul(pair[rows, 1, 0:META], v, pt[0:n, j, 0:META], start=True, stop=True)
                    last = pe.matmul(pair[rows, 0, 0:SEQ], v, pt[0:n, j, META:NK], start=False, stop=True)
                else:
                    pe.matmul(pair[rows, 0, at - META:SEQ], v, pt[:, j, at:NK], start=j == 0, stop=False)
            t = mark(last, "pe_fox")
            pT.free[pi].append(t)
            need("act", t)
            mark(act.activation(mixedT[rows, 4 + h // 2, META:NK], pair[rows, 0, 0:SEQ], ACT.Copy), "act_fox")
            t_mixed.append(mark(act.activation(mixedT[rows, 4 + h // 2, 0:META], pair[rows, 1, 0:META], ACT.Copy), "act_fox"))
            psum.release(b, t_mixed[-1], n=2)

        heads = [dict(done=[]) for _ in range(FH)]
        heads[0]["bias"] = fox_bias(0)
        items, flow = [(h, *tile) for h in range(FH) for tile in tiles()], []
        for c in range(len(items) + 3):
            if c < len(items):
                h, i, n, at = items[c]
                flow.append(fox_scores(h, i, n, at, heads[h]))
                if i == NT - 1 and h + 1 < FH:
                    heads[h + 1]["bias"] = fox_bias(h + 1)
            if 0 <= c - 1 < len(items):
                fox_weights(flow[c - 1])
            if 0 <= c - 2 < len(items):
                fox_transpose(flow[c - 2])
            if c >= 3 and flow[c - 3]["i"] == NT - 1:
                fox_values(flow[c - 3]["h"], flow[c - 3]["head"])

        t_x2 = [None] * (NT + 1)
        for half in range(2):
            w, arrived, free_w = weights("w_out", half, KC, 512)
            need("pe", arrived, *t_mixed)
            for i, n, at in tiles():
                b, bank, free = psum.take()
                need("pe", *free)
                t = chain(bank[0:n, :], [(mixedT[:, c, at:at + n], w[:, c, :]) for c in range(KC)], "pe_out")
                need("dve", t)
                dst = (xm[:, half * 512:(half + 1) * 512] if i == NT else x[:, i, half * 512:(half + 1) * 512])
                t_x2[i] = mark(dve.tensor_tensor(dst, dst, bank[0:n, :], ALU.add), "dve_out")
                psum.release(b, t_x2[i])
            free_w.append(t)
        S.fence()
        third.close()
        second.close()
        mixer.close()

        late = ctx.enter_context(ExitStack())
        modc = sb(late, "modc", [P, 2, 6 * KC])
        gain1 = sb(late, "gain1", [P, 2, KC])
        silu_c = sb(late, "silu_c", [P, KC, 2])
        xn = sb(late, "xn2", [P, NT, D])
        scratch = sb(late, "scratch2", [P, D])
        ctxn = sb(late, "ctxn", [P, 2, D])
        final1 = sb(late, "final1", [P, D])
        hT = sb(late, "hT", [P, KC, SEQ])
        hcT = sb(late, "hcT", [P, KC, CTX])
        t_ctx = mark(act.dma_start(ctxn[:], A["ctx"]), "ld_ctx", 16)
        t_final1 = mark(act.dma_start(final1[:], A["final1"]), "ld_final1", 16)
        ffn = ctx.enter_context(ExitStack())
        LEAD = 2
        NA = LEAD + SEQ
        gT = sb(ffn, "gT", [P, NF, SEQ])
        xnT = sb(ffn, "xnT2", [P, KC, NK])
        xnm = hcT[0:META, 0:4, :].rearrange("p c n -> p (c n)")
        branch = Ring([sb(ffn, f"branch{i}", [P, NA]) for i in range(3)])
        acc = Ring([sb(ffn, f"acc{i}", [P, SEQ]) for i in range(3)])
        ready, ready_m = normalise("norm2", t_x2, t_x2[NT])
        t_xnT = transposed(xn, range(NT), xnT, [col("ffn_g", c) for c in range(KC)], None, "norm2", ready, META)
        t_xnT.append(meta_transposed(xnm, xnT, col("ffn_g", 0, KC), "norm2", ready_m))
        NAH = NA // 2
        modacc = Ring([sb(ffn, f"modacc{i}", [P, 512]) for i in range(2)] + [spare_row[:, a:a + 512] for a in (0, 512)])
        for k in (2, 3):
            modacc.free[k].append(ready_m)
        t_silu_c = mark(act.activation(silu_c[:].rearrange("p k t -> p (k t)"), col("cond", 0, 2 * KC), ACT.Silu), "act_mod")

        def mod_sums(m):
            w, arrived, free_w = weights("w_mod", m, KC, 512)
            need("dve", arrived, t_silu_c)
            sums = []
            for r in range(2 if m < 4 else 1):
                ai, a, afree = modacc.take()
                need("dve", *afree)
                t = mark(dve.tensor_scalar(a[:], w[:, 0, :], silu_c[:, 0, r:r + 1], None, ALU.mult), "dve_mod")
                for c in range(1, KC):
                    need("dve", t)
                    t = mark(dve.scalar_tensor_tensor(a[:], w[:, c, :], silu_c[:, c, r:r + 1], a[:], ALU.mult, ALU.add), "dve_mod")
                sums.append((r, ai, a, t))
            free_w.append(t)
            return m, sums

        def mod_finish(m, sums):
            for r, ai, a, t in sums:
                b, bank, free = psum.take()
                need("pe", *free, t, t_ones)
                for j in range(4):
                    last = pe.matmul(bank[:, j:j + 1], a[:, j * P:(j + 1) * P], ones[:, 0:1], start=True, stop=True)
                t = mark(last, "pe_mod")
                need("dve", t)
                t_mod = mark(dve.tensor_tensor(modc[:, r, 4 * m:4 * m + 4], bank[:, 0:4], col("b_mod", 4 * m, 4), ALU.add), "dve_mod")
                psum.release(b, t_mod)
                modacc.free[ai].append(t)
            return t_mod

        mod_ahead = mod_sums(0)
        t_g = [None] * NF
        for u in range(NF // 2):
            w, arrived, free_w = weights("w_up", u, KC, 512)
            need("pe", arrived, *t_xnT)
            for v in range(2):
                f = 2 * u + v
                b, pair, free = psum.take(2)
                need("pe", *free)
                for a in range(2):
                    at = META - LEAD + a * NAH
                    t = chain(pair[:, a, 0:NAH], [(w[:, c, v * P:(v + 1) * P], xnT[:, c, at:at + NAH]) for c in range(KC)], "pe_up")
                bi, abuf, bfree = branch.take()
                need("act", t, *bfree)
                t_a = mark(act.activation(abuf[:].rearrange("p (a n) -> p a n", a=2), pair[:, :, 0:NAH], ACT.Copy), "act_up")
                psum.release(b, t_a, n=2)
                ai, cbuf, afree = acc.take()
                need("dve", t_a, *afree)
                t = mark(dve.tensor_scalar(cbuf[:], abuf[:, 0:SEQ], col("conv_w", f), col("conv_b", f), ALU.mult, ALU.add), "dve_up")
                for j in range(1, 3):
                    need("dve", t)
                    t = mark(dve.scalar_tensor_tensor(cbuf[:], abuf[:, j:j + SEQ], col("conv_w", j * NF + f), cbuf[:],
                                                      ALU.mult, ALU.add), "dve_up")
                branch.free[bi].append(t)
                need("act", t)
                t_s = mark(act.activation(cbuf[:], cbuf[:], ACT.Silu), "act_up")
                b, bank, free = psum.take()
                need("pe", *free)
                t = chain(bank[:, :], [(w[:, c, 256 + v * P:256 + (v + 1) * P], xnT[:, c, META:NK]) for c in range(KC)], "pe_up")
                need("dve", t, t_s)
                t_g[f] = mark(dve.tensor_tensor(gT[:, f, :], bank[:, :], cbuf[:], ALU.mult), "dve_up")
                psum.release(b, t_g[f])
                acc.free[ai].append(t_g[f])
            free_w.append(t)
            mod_now, mod_ahead = mod_ahead, mod_sums(u + 1)
            t_mod = mod_finish(*mod_now)
        def context_input():
            t_mod = mod_finish(*mod_ahead)
            need("dve", t_mod)
            for r in range(2):
                t_gain = mark(dve.scalar_tensor_tensor(gain1[:, r, :], modc[:, r, KC:2 * KC], 1.0, col("norm1_g", 0, KC),
                                                       ALU.add, ALU.mult), "dve_mod")
            need("dve", t_ctx)
            ready_c = []
            for i in range(2):
                t = token_rstd(ctxn[:, i, :], P, 5 + i, scratch, t_ctx, "norm3")
                need("dve", t)
                ready_c.append(mark(dve.tensor_scalar(ctxn[:, i, :], ctxn[:, i, :], stat[:, 2, 5 + i:6 + i], None, ALU.mult), "dve_norm3"))
            need("act", t_gain)
            need("dve", t_gain)
            return transposed(ctxn, range(2), hcT, [gain1[:, 1, c:c + 1] for c in range(KC)], [modc[:, 1, c:c + 1] for c in range(KC)], "norm3", ready_c)

        ready, t_hT = [], []

        def norm3(i):
            t = token_rstd(x[:, i, :], P, i, scratch, t_x3[i], "norm3")
            need("dve", t, t_final1)
            t = mark(dve.scalar_tensor_tensor(x[:, i, :], x[:, i, :], stat[:, 2, i:i + 1], final1[:], ALU.mult, ALU.mult), "dve_norm3")
            t = token_rstd(x[:, i, :], P, i, scratch, t, "norm3")
            need("dve", t)
            ready.append(mark(dve.tensor_scalar(xn[:, i, :], x[:, i, :], stat[:, 2, i:i + 1], None, ALU.mult), "dve_norm3"))

        def turn3(i):
            t_hT.append(transposed(xn, [i], hT, [gain1[:, 0, c:c + 1] for c in range(KC)], [modc[:, 0, c:c + 1] for c in range(KC)],
                                   "norm3", ready))

        t_x3 = [None] * NT
        splits = [(0, 8), (8, 16), (16, NF)]
        for half in range(2):
            banks = [psum.take() for _ in range(NT)]
            for s, (f0, f1) in enumerate(splits):
                w, arrived, free_w = weights("w_down", half * len(splits) + s, f1 - f0, 512)
                need("pe", arrived, t_g[f1 - 1])
                for i in range(NT):
                    need("pe", *banks[i][2])
                    t = chain(banks[i][1][:, :], [(gT[:, f, i * P:(i + 1) * P], w[:, f - f0, :]) for f in range(f0, f1)],
                              "pe_down", start=s == 0, stop=s == len(splits) - 1)
                    if s == len(splits) - 1:
                        need("dve", t)
                        dst = x[:, i, half * 512:(half + 1) * 512]
                        t_x3[i] = mark(dve.tensor_tensor(dst, dst, banks[i][1][:, :], ALU.add), "dve_down")
                        psum.release(banks[i][0], t_x3[i])
                        if half:
                            norm3(i)
                            if i:
                                turn3(i - 1)
                free_w.append(t)
                if half == 0 and s == 0:
                    t_hcT = context_input()
        turn3(NT - 1)

        S.fence()
        ffn.close()
        block2 = ctx.enter_context(ExitStack())
        merged = sb(block2, "merged", [P, KC, SEQ])
        sig_a = xn[:].rearrange("p i (a n) -> p (i a) n", n=SEQ)
        latent = sb(block2, "latent", [P, 2 * SEQ + NKV])
        K0 = sb(block2, "Ks0", [P, 2, NKV])
        cq = latent[:, 0:2 * SEQ].rearrange("p (k n) -> p k n", k=2)
        ckv = latent[:, 2 * SEQ:]
        kr = K0[:, 0, :]
        swap2 = spare_row[:, NKV:NKV + P]
        rope2 = sb(block2, "rope2", [P, 2, SEQ])
        t_rope2 = [mark(act.dma_start(d, A[n]), "ld_rope2", 16) for d, n in ((swap2, "swap2"), (rope2[:], "rope2"))][-1]

        conv = ctx.enter_context(ExitStack())
        sig_c = sb(conv, "sig_c", [P, KC, SEQ])
        EDGE = TAPS // 2
        padded = sb(conv, "padded", [P, KC, SEQ + 2 * EDGE])
        sg = Ring([sb(conv, f"sg{i}", [P, SEQ]) for i in range(3)])
        mark(pool.memset(padded[:, :, 0:EDGE], 0.0), "pool_pad")
        t_pad = mark(pool.memset(padded[:, :, EDGE + SEQ:], 0.0), "pool_pad")
        need("dve", t_pad)
        t_conv = [None] * KC

        def convolve(channels, ready):
            need("dve", ready)
            for j in range(TAPS):
                for k in channels:
                    src = padded[:, k, j:j + SEQ]
                    if j == 0:
                        t_conv[k] = mark(dve.tensor_scalar(merged[:, k, :], src, col("dw_w", k), col("dw_b", k), ALU.mult, ALU.add), "dve_conv")
                    else:
                        need("dve", t_conv[k])
                        t_conv[k] = mark(dve.scalar_tensor_tensor(merged[:, k, :], src, col("dw_w", j * KC + k), merged[:, k, :],
                                                                  ALU.mult, ALU.add), "dve_conv")


        for u in range(4):
            w, arrived, free_w = weights("w_in2", 1 + u, KC, 512)
            need("pe", arrived, *t_hT)
            for v in range(2):
                k = 2 * u + v
                b, bank, free = psum.take()
                need("pe", *free)
                t = chain(bank[:, :], [(w[:, c, 256 + v * P:256 + (v + 1) * P], hT[:, c, :]) for c in range(KC)], "pe_glu")
                gi, gbuf, gfree = sg.take()
                need("act", t, *gfree)
                t_sg = mark(act.activation(gbuf[:], bank[:, :], ACT.Sigmoid), "act_glu")
                psum.release(b, t_sg)
                b, bank, free = psum.take()
                need("pe", *free)
                t = chain(bank[:, :], [(w[:, c, v * P:(v + 1) * P], hT[:, c, :]) for c in range(KC)], "pe_glu")
                need("dve", t, t_sg)
                t_y = mark(dve.tensor_tensor(padded[:, k, EDGE:EDGE + SEQ], bank[:, :], gbuf[:], ALU.mult), "dve_glu")
                psum.release(b, t_y)
                sg.free[gi].append(t_y)
                if u == 0:
                    convolve((k,), t_y)
            free_w.append(t)
            if u:
                convolve((2 * u, 2 * u + 1), t_y)

        t_gate = {}
        for u in range(4):
            w, arrived, free_w = weights("w_in2", 5 + u, KC, 512)
            need("pe", arrived)
            for v in range(4):
                k = 4 * u + v
                b, bank, free = psum.take()
                need("pe", *free)
                t = chain(bank[:, :], [(w[:, c, v * P:(v + 1) * P], hT[:, c, :]) for c in range(KC)], "pe_gate")
                need("act", t)
                dst = sig_a[:, k, :] if k < KC else sig_c[:, k - KC, :]
                t_gate[k] = mark(act.activation(dst, bank[:, :], ACT.Sigmoid), "act_gate")
                psum.release(b, t_gate[k])
            free_w.append(t)

        w_latent, arrived, free_in = weights("w_in2", 0, KC, 416)
        need("pe", arrived, *t_hcT)
        lat = {}

        def latents(j):
            b, bank, free = psum.take()
            need("pe", *free)
            t = chain(bank[:, :], [(w_latent[:, c, j * P:(j + 1) * P], hT[:, c, :]) for c in range(KC)], "pe_ckv")
            dst = cq[:, j, :] if j < 2 else ckv[:, 0:SEQ]
            need("act", t)
            lat[j] = mark(act.activation(dst, bank[:, :], ACT.Copy), "act_ckv")
            psum.release(b, lat[j])
        latents(0)
        latents(1)

        b, bank, free = psum.take()
        need("pe", *free, *t_conv)
        t = chain(bank[:, :], [(ones[:], merged[:, k, :]) for k in range(KC)], "pe_ln")
        mi, mean, mfree = sg.take()
        need("act", t, *mfree)
        t_mean = mark(act.activation(mean[:], bank[:, :], ACT.Copy, scale=1.0 / D), "act_ln")
        psum.release(b, t_mean)
        t_cent = []
        for k in range(KC):
            need("dve", t_mean, t_conv[k])
            t_cent.append(mark(dve.tensor_tensor(merged[:, k, :], merged[:, k, :], mean[:], ALU.subtract), "dve_ln"))
        sg.free[mi].append(t_cent[-1])
        latents(2)
        b, bank, free = psum.take()
        need("pe", *free)
        for k in range(KC):
            gi, sq, gfree = sg.take()
            need("act", *gfree, t_cent[k])
            t = mark(act.activation(sq[:], merged[:, k, :], ACT.Square), "act_ln")
            need("pe", t)
            t = mark(pe.matmul(bank[:, :], ones[:], sq[:], start=k == 0, stop=k == KC - 1), "pe_ln")
            sg.free[gi].append(t)
        gi, root, gfree = sg.take()
        need("act", t, *gfree)
        t = mark(act.activation(root[:], bank[:, :], ACT.Sqrt, bias=eps[:, :], scale=1.0 / D), "act_ln")
        psum.release(b, t)
        need("dve", t)
        t = mark(dve.reciprocal(root[:], root[:]), "dve_ln")
        need("dve", t)
        t_sw = []
        for k in range(KC):
            t = mark(dve.tensor_tensor(padded[:, k, 0:SEQ], merged[:, k, :], root[:], ALU.mult), "dve_ln")
            if k == KC - 1:
                sg.free[gi].append(t)
            need("act", t)
            t_sw.append(mark(act.activation(padded[:, k, 0:SEQ], padded[:, k, 0:SEQ], ACT.Silu, scale=col("ln_g", k),
                                            bias=col("ln_b", k)), "act_ln"))
        b, bank, free = psum.take()
        need("pe", *free)
        t = chain(bank[:, 0:CTX], [(w_latent[:, c, 2 * P:3 * P], hcT[:, c, :]) for c in range(KC)], "pe_ckv")
        need("act", t)
        t_ckv = mark(act.activation(ckv[:, SEQ:NKV], bank[:, 0:CTX], ACT.Copy), "act_ckv")
        psum.release(b, t_ckv)
        R = slice(NOPE, QK)
        for src, n, at in ((hT, SEQ, 0), (hcT, CTX, SEQ)):
            b, bank, free = psum.take()
            need("pe", *free)
            t = chain(bank[R, 0:n], [(w_latent[:, c, 3 * P:3 * P + ROPE], src[:, c, :]) for c in range(KC)], "pe_ckv")
            need("act", t)
            t_kr = mark(act.activation(kr[R, at:at + n], bank[R, 0:n], ACT.Copy), "act_ckv")
            psum.release(b, t_kr)
        free_in.append(t)

        def feature_norm(views, n, rank, gains, name, ready):
            b, bank, free = psum.take()
            need("pe", *free, t_ones)
            for k, view in enumerate(views):
                gi, sq, gfree = sg.take()
                need("act", *gfree, *ready)
                t = mark(act.activation(sq[:, 0:n], view, ACT.Square), f"act_{name}")
                need("pe", t)
                t = mark(pe.matmul(bank[:, 0:n], ones[:], sq[:, 0:n], start=k == 0, stop=k == len(views) - 1), f"pe_{name}")
                sg.free[gi].append(t)
            gi, root, gfree = sg.take()
            need("act", t, *gfree)
            t = mark(act.activation(root[:, 0:n], bank[:, 0:n], ACT.Sqrt, bias=eps[:, :], scale=1.0 / rank), f"act_{name}")
            psum.release(b, t)
            need("dve", t, *ready)
            t = mark(dve.reciprocal(root[:, 0:n], root[:, 0:n]), f"dve_{name}")
            need("dve", t)
            for view, g in zip(views, gains):
                t = mark(dve.scalar_tensor_tensor(view, view, g, root[:, 0:n], ALU.mult, ALU.mult), f"dve_{name}")
            sg.free[gi].append(t)
            return t

        def finish_latents():
            b, bank, free = psum.take()
            need("pe", *free, t_kr, t_rope2)
            t = chain(bank[R, :], [(swap2[R, R], kr[R, 0:SEQ])], "pe_ckv")
            gi, gbuf, gfree = sg.take()
            need("dve", t, t_kr, t_rope2, *gfree)
            t1 = mark(dve.tensor_tensor(gbuf[R, :], bank[R, :], rope2[R, 1, :], ALU.mult), "dve_ckv")
            psum.release(b, t1)
            t2 = mark(dve.tensor_tensor(kr[R, 0:SEQ], kr[R, 0:SEQ], rope2[R, 0, :], ALU.mult), "dve_ckv")
            need("dve", t1, t2)
            t_kr1 = mark(dve.tensor_tensor(kr[R, 0:SEQ], kr[R, 0:SEQ], gbuf[R, :], ALU.add), "dve_ckv")
            sg.free[gi].append(t_kr1)
            t_cq = feature_norm([cq[:, 0, :], cq[:, 1, :]], SEQ, 256, [col("q_g", 0), col("q_g", 1)], "cnorm", [lat[0], lat[1]])
            t_ckv1 = feature_norm([ckv[:, 0:SEQ]], SEQ, 128, [col("kv_g")], "cnorm", [lat[2]])
            t_ckv2 = feature_norm([ckv[:, SEQ:NKV]], CTX, 128, [col("kv_g")], "cnorm", [t_ckv])
            return t_kr1, t_cq, t_ckv1, t_ckv2

        for u in range(2):
            w, arrived, free_w = weights("w_pw", u, KC, 512)
            need("pe", arrived)
            for v in range(4):
                k = 4 * u + v
                b, bank, free = psum.take()
                need("pe", *free)
                for c in range(KC):
                    need("pe", t_sw[c])
                    t = chain(bank[:, :], [(w[:, c, v * P:(v + 1) * P], padded[:, c, 0:SEQ])], "pe_pw", c == 0, c == KC - 1)
                need("dve", t, t_gate[KC + k])
                t_m = mark(dve.tensor_tensor(merged[:, k, :], bank[:, :], sig_c[:, k, :], ALU.mult), "dve_pw")
                psum.release(b, t_m)
            free_w.append(t)
            if u == 0:
                t_kr, t_cq, t_ckv1, t_ckv2 = finish_latents()
        S.fence()
        conv.close()

        attn = ctx.enter_context(ExitStack())
        values = sb(attn, "values", [P, NKV // P, AH * VD])
        headsT = hT
        Qs = Ring([ctxn[:].rearrange("p i (a n) -> p (i a) n", n=SEQ), hcT[:].rearrange("p (a b) n -> p a (b n)", b=2)])
        Ks = Ring([K0, sb(attn, "Ks1", [P, 2, NKV])])
        probs = Ring([sb(attn, "probs0", [P, NKV]), final1[:, 0:NKV], spare_row[:, 0:NKV]])
        turn = Ring([scratch[:, i * SEQ:(i + 1) * SEQ] for i in range(2)])
        mstat = sb(attn, "mstat", [P, 4, 4])
        ms = Ring([mstat[:, i, :] for i in range(4)])
        wq, t_wq, free_wq = weights("w_uq", 0, 2, 1536)
        wkv, t_wkv, free_wkv = weights("w_ukv", 0, 1, 2048)
        lent, lent_buffer, lent_free = wring.take()
        probsT = Ring([sb(attn, "probsT0", [P, NKV // P, SEQ]),
                       lent_buffer[:, 0:NKV // P * SEQ].rearrange("p (j t) -> p j t", t=SEQ)])
        probsT.free[1] += lent_free
        probs = Ring(probs.buffers + [lent_buffer[:, UNIT - D:UNIT - D + NKV]])
        probs.free[3] += lent_free
        t_under = []
        for buffer in Ks.buffers:
            for s in range(2):
                if buffer is K0 and s == 0:
                    continue
                t_under.append(mark(pool.tensor_copy(buffer[R, s, :], kr[R, :]), "pool_kr"))
        need("pe", t_wkv, t_ckv1, t_ckv2)
        t_values = []
        for j in range(NKV // P):
            for half in range(2):
                b, bank, free = psum.take()
                need("pe", *free)
                t = chain(bank[:, :], [(ckv[:, j * P:(j + 1) * P], wkv[:, 0, 1024 + half * 512:1024 + (half + 1) * 512])], "pe_values2")
                need("act", t)
                t_values.append(mark(act.activation(values[:, j, half * 512:(half + 1) * 512], bank[:, :], ACT.Copy), "act_values2"))
                psum.release(b, t_values[-1])
        t_heads = []
        KH = NKV // 2

        def queries(g):
            qi, Q, qfree = Qs.take()
            need("pe", t_wq, t_cq)
            done = []
            for v in range(2):
                b, bank, free = psum.take()
                need("pe", *free)
                t = chain(bank[:, :], [(wq[:, c, (2 * g + v) * P:(2 * g + v + 1) * P], cq[:, c, :]) for c in range(2)], "pe_q")
                need("act", t, *qfree)
                mark(act.activation(Q[0:NOPE, 2 * v, :], bank[0:NOPE, :], ACT.Copy), "act_q")
                t = mark(act.activation(Q[0:NOPE, 2 * v + 1, :], bank[NOPE:P, :], ACT.Copy), "act_q")
                psum.release(b, t)
                done.append(t)
            b, bank, free = psum.take()
            need("pe", *free)
            t = chain(bank[:, :], [(wq[:, c, AH * NOPE + g * P:AH * NOPE + (g + 1) * P], cq[:, c, :]) for c in range(2)], "pe_q")
            ti, plain, tfree = turn.take()
            need("act", t, *tfree)
            t_plain = mark(act.activation(plain[:], bank[:, :], ACT.Copy), "act_q")
            psum.release(b, t_plain)
            b, bank, free = psum.take()
            need("pe", *free, t_plain)
            t = chain(bank[:, :], [(swap2, plain[:])], "pe_q")
            ui, cross, ufree = turn.take()
            need("dve", t, *ufree)
            t1 = mark(dve.tensor_tensor(cross[:], bank[:, :], rope2[:, 1, :], ALU.mult), "dve_q")
            psum.release(b, t1)
            t2 = mark(dve.tensor_tensor(plain[:], plain[:], rope2[:, 0, :], ALU.mult), "dve_q")
            need("dve", t1, t2, *qfree)
            for j in range(4):
                t = mark(dve.tensor_tensor(Q[R, j, :], plain[j * ROPE:(j + 1) * ROPE, :], cross[j * ROPE:(j + 1) * ROPE, :], ALU.add), "dve_q")
            done.append(t)
            turn.free[ti].append(t)
            turn.free[ui].append(t)
            return qi, Q, done

        def keys(p):
            ki, K, kfree = Ks.take()
            b, pair, free = psum.take(2)
            need("pe", *free)
            for a in range(2):
                t = chain(pair[:, a, 0:KH], [(wkv[:, 0, p * P:(p + 1) * P], ckv[:, a * KH:(a + 1) * KH])], "pe_k")
            need("act", t, *kfree)
            mark(act.activation(K[0:NOPE, 0, :].rearrange("p (a n) -> p a n", a=2), pair[0:NOPE, :, 0:KH], ACT.Copy), "act_k")
            t = mark(act.activation(K[0:NOPE, 1, :].rearrange("p (a n) -> p a n", a=2), pair[NOPE:P, :, 0:KH], ACT.Copy), "act_k")
            psum.release(b, t, n=2)
            return ki, K, t

        scale2 = QK ** -0.5

        def scores2(h, i, head):
            b, pair, free = psum.take(2)
            need("pe", *free, *head["Q"][2], head["K"][2], t_kr, *t_under)
            for a in range(2):
                last = pe.matmul(pair[:, a, 0:KH], head["Q"][1][0:QK, h % 4, i * P:(i + 1) * P],
                                 head["K"][1][0:QK, h % 2, a * KH:(a + 1) * KH], start=True, stop=True)
            t_s = mark(last, "pe_scores2")
            if i == NT - 1:
                if h % 4 == 3:
                    Qs.free[head["Q"][0]].append(t_s)
                if h % 2 == 1:
                    Ks.free[head["K"][0]].append(t_s)
            mi, st, mfree = ms.take()
            need("dve", t_s, *mfree)
            t = mark(dve.tensor_reduce(st[:, 0:1], pair[:, :, 0:KH], mybir.AxisListType.XY, ALU.max), "dve_attn2")
            need("dve", t)
            t = mark(dve.tensor_scalar(st[:, 1:2], st[:, 0:1], -scale2, None, ALU.mult), "dve_attn2")
            li, L, lfree = probs.take()
            need("act", t, t_s, *lfree)
            t = mark(act.activation(L[:].rearrange("p (a n) -> p a n", a=2), pair[:, :, 0:KH], ACT.Exp, bias=st[:, 1:2],
                                    scale=scale2, accum_out=st[:, 2:3]), "act_attn2")
            psum.release(b, t, n=2)
            return dict(h=h, i=i, mi=mi, st=st, li=li, L=L, exp=t, head=head)

        def weights2(c):
            st, L = c["st"], c["L"]
            need("dve", c["exp"])
            t = mark(dve.reciprocal(st[:, 3:4], st[:, 2:3]), "dve_attn2")
            need("dve", t)
            c["p"] = mark(dve.tensor_scalar(L[:], L[:], st[:, 3:4], None, ALU.mult), "dve_attn2")
            ms.free[c["mi"]].append(c["p"])

        def transpose2(c):
            i, L, head = c["i"], c["L"], c["head"]
            if "pt" not in head:
                head["pt"] = probsT.take()
            pi, pt, pfree = head["pt"]
            b, pair, free = psum.take(2)
            need("pe", *free, c["p"])
            for j in range(NKV // P):
                last = pe.transpose(pair[:, j // 3, (j % 3) * P:(j % 3 + 1) * P], L[:, j * P:(j + 1) * P], ident[:])
            t = mark(last, "pe_attn2")
            probs.free[c["li"]].append(t)
            need("act", t, *pfree)
            t = mark(act.activation(pt[:, :, i * P:(i + 1) * P].rearrange("p (a j) t -> p a j t", a=2),
                                    pair[:, :, 0:KH].rearrange("p a (j t) -> p a j t", t=P), ACT.Copy), "act_attn2")
            psum.release(b, t, n=2)
            head["done"].append(t)

        def values2(h, head):
            rows = slice((h % 2) * VD, (h % 2) * VD + VD)
            pi, pt, _ = head["pt"]
            b, bank, free = psum.take()
            need("pe", *free, *head["done"], *t_values)
            t = chain(bank[rows, :], [(values[:, j, h * VD:(h + 1) * VD], pt[:, j, :]) for j in range(NKV // P)], "pe_attn2")
            probsT.free[pi].append(t)
            need("dve", t)
            t_heads.append(mark(dve.tensor_copy(headsT[rows, h // 2, :], bank[rows, :]), "dve_heads"))
            psum.release(b, t_heads[-1])
            return t

        heads = [dict(done=[]) for _ in range(AH)]
        Q_now, K_now = queries(0), keys(0)
        items, flow = [(h, i) for h in range(AH) for i in range(NT)], []
        for c in range(len(items) + 4):
            if c < len(items):
                h, i = items[c]
                if i == 0:
                    if h and h % 4 == 0:
                        Q_now = Q_next
                    if h and h % 2 == 0:
                        K_now = K_next
                    heads[h].update(Q=Q_now, K=K_now)
                flow.append(scores2(h, i, heads[h]))
                if i == 1 and h % 4 == 3 and h + 1 < AH:
                    Q_next = queries(h // 4 + 1)
                    if h // 4 + 2 == AH // 4:
                        free_wq.append(S.last["pe"])
                if i == 1 and h % 2 == 1 and h + 1 < AH:
                    K_next = keys(h // 2 + 1)
                    if h // 2 + 2 == AH // 2:
                        free_wkv.append(S.last["pe"])
            if 0 <= c - 1 < len(items):
                weights2(flow[c - 1])
            if 0 <= c - 3 < len(items):
                transpose2(flow[c - 3])
            if c >= 4 and flow[c - 4]["i"] == NT - 1:
                t = values2(flow[c - 4]["h"], flow[c - 4]["head"])
        wring.free[lent].append(t)

        for u in range(2):
            w, arrived, free_w = weights("w_o_mla", u, KC, 512)
            need("pe", arrived)
            for v in range(4):
                k = 4 * u + v
                b, bank, free = psum.take()
                need("pe", *free)
                for c in range(KC):
                    need("pe", t_heads[2 * c], t_heads[2 * c + 1])
                    t = chain(bank[:, :], [(w[:, c, v * P:(v + 1) * P], headsT[:, c, :])], "pe_o", c == 0, c == KC - 1)
                need("dve", t, t_gate[k])
                t1 = mark(dve.tensor_tensor(sig_a[:, k, :], bank[:, :], sig_a[:, k, :], ALU.mult), "dve_o")
                psum.release(b, t1)
                need("dve", t1, t_m)
                t_merged = mark(dve.tensor_tensor(merged[:, k, :], merged[:, k, :], sig_a[:, k, :], ALU.add), "dve_o")
            free_w.append(t)
        S.fence()
        attn.close()

        rest = ctx.enter_context(ExitStack())
        h2 = hT[:].rearrange("p (i a) n -> p i (a n)", i=NT)
        final2 = final1
        qT = sb(rest, "qT", [P, 2 * PH, SEQ])
        subkeys = sb(rest, "subkeys", [P, 2 * PH, NKEY])
        peer = ctx.enter_context(ExitStack())
        hc_rows = hcT[:].rearrange("p (a b) n -> p a (b n)", a=2)
        mod_rows = [ctxn[:, 0, :], ctxn[:, 1, :], hc_rows[:, 0, :], hc_rows[:, 1, :]]
        rows_ = dict(zip(("g1", "sh2", "sc2", "g2"), mod_rows))
        spread = spare_row

        def modulation_row(k, after):
            need("dve", after)
            t = mark(dve.tensor_tensor(spread[:].rearrange("p (c n) -> p c n", c=KC), ident[:].unsqueeze(1).to_broadcast([P, KC, P]),
                                       modc[:, 0, (2 + k) * KC:(3 + k) * KC].unsqueeze(2).to_broadcast([P, KC, P]), ALU.mult), "dve_row")
            b, pair, free = psum.take(2)
            need("pe", *free, t)
            for a in range(2):
                t = chain(pair[:, a, :], [(ones[:], spread[:, a * 512:(a + 1) * 512])], "pe_row")
            need("act", t)
            t_row = mark(act.activation(mod_rows[k].rearrange("p (a n) -> p a n", a=2), pair, ACT.Copy), "act_row")
            psum.release(b, t_row, n=2)
            return t, t_row

        t_norm2 = mark(act.dma_start(final2[:], A["norm2_g"]), "ld_norm2", 16)
        t_sub = mark(act.dma_start(subkeys[:], A["sub_keys"]), "ld_sub", 16)
        t_x4 = [[] for _ in range(NT)]
        spread_read, t_rows = None, []
        ready, t_h2T = [], []

        def norm4(i):
            t = token_rstd(x[:, i, :], P, i, scratch, t_x4[i], "norm4")
            need("dve", t, t_gain2)
            t = mark(dve.scalar_tensor_tensor(h2[:, i, :], x[:, i, :], stat[:, 2, i:i + 1], rows_["sc2"], ALU.mult, ALU.mult), "dve_norm4")
            need("dve", t)
            ready.append(mark(dve.tensor_tensor(h2[:, i, :], h2[:, i, :], rows_["sh2"], ALU.add), "dve_norm4"))

        def turn4(i):
            t_h2T.append(transposed(h2, [i], merged, [ones[:, 0:1]] * KC, None, "norm4", ready))

        for half in range(2):
            cut = slice(half * 512, (half + 1) * 512)
            w, arrived, free_w = weights("w_out2", half, KC, 512)
            need("pe", arrived, t_merged)
            for i in range(NT):
                b, bank, free = psum.take()
                need("pe", *free)
                t = chain(bank[:, :], [(merged[:, c, i * P:(i + 1) * P], w[:, c, :]) for c in range(KC)], "pe_out2")
                if half == 0:
                    spread_read, t_row = modulation_row(i, spread_read)
                    t_rows.append(t_row)
                need("dve", t, t_rows[0])
                t1 = mark(dve.tensor_tensor(h2[:, i, cut], bank[:, :], rows_["g1"][:, cut], ALU.mult), "dve_out2")
                psum.release(b, t1)
                need("dve", t1)
                t_x4[i].append(mark(dve.tensor_tensor(x[:, i, cut], x[:, i, cut], h2[:, i, cut], ALU.add), "dve_out2"))
                if half:
                    norm4(i)
                    if i:
                        turn4(i - 1)
            free_w.append(t)
            if half == 0:
                need("dve", t_norm2, *t_rows)
                t_gain2 = mark(dve.scalar_tensor_tensor(rows_["sc2"], rows_["sc2"], 1.0, final2[:], ALU.add, ALU.mult), "dve_mod2")
                need("act", t_gain2, t_merged)
                t_final2 = mark(act.dma_start(final2[:], A["final_g"]), "ld_final2", 16)
        turn4(NT - 1)
        h2T = merged

        GROUP = 2
        STEPS = 1
        BH = PH // 2
        PICKS = BH * TOPK
        scores = mod_rows[0].rearrange("p (r k) -> p r k", k=NKEY)
        left = mod_rows[1].rearrange("p (r k) -> p r k", k=NKEY)
        cand_rows_ = latent[:, 0:BH * TOPK * TOPK].rearrange("p (h n) -> p h n", h=BH)
        cand_ = cand_rows_.rearrange("p h (a b) -> p h a b", a=TOPK)
        rest2_ = K0[:].rearrange("p a n -> p (a n)")[:, 0:BH * TOPK * TOPK].rearrange("p (h n) -> p h n", h=BH)
        top_ = sb(peer, "top", [P, 2 * BH, TOPK])
        topi_ = sb(peer, "topi", [P, 2 * BH, TOPK], U32)
        topf_ = sb(peer, "topf", [P, 2 * BH, TOPK])
        best_ = sb(peer, "best", [P, BH, TOPK])
        besti_ = sb(peer, "besti", [P, BH, TOPK], U32)
        part_ = sb(peer, "part", [P, 2, BH, TOPK], U32)
        partf_ = sb(peer, "partf", [P, 2, BH, TOPK])
        picked_ = sb(peer, "picked", [P, 2, BH, TOPK])
        gsum = sb(peer, "gsum", [P, 2, BH])
        count = sb(peer, "count", [P, TOPK])
        t_count = mark(act.dma_start(count[:], A["count16"]), "ld_count", 16)
        batches = Ring([dict(expert=sb(peer, f"expert{i}", [P, PICKS], U32), gate=sb(peer, f"gate{i}", [P, BH, TOPK]),
                             hidden=sb(peer, f"hidden{i}", [P, PICKS]), coef=sb(peer, f"coef{i}", [P, PICKS])) for i in range(2)])
        diags = Ring([spread[:, a:a + P] for a in range(0, D, P)])
        need("dve", *ready)
        need("act", *ready)
        LOW = -3.0e38

        def top16(n, row, spare, values_, index, ready):
            need("dve", *ready)
            def each(step):
                return [mark(step(r), "dve_top") for r in range(n)]
            a = each(lambda r: dve.max(values_[:, r, 0:8], row(r)))
            yield
            need("dve", *a)
            each(lambda r: dve.max_index(index[:, r, 0:8], values_[:, r, 0:8], row(r)))
            yield
            b_ = each(lambda r: dve.match_replace(spare(r), values_[:, r, 0:8], row(r), LOW))
            yield
            need("dve", *b_)
            c_ = each(lambda r: dve.max(values_[:, r, 8:16], spare(r)))
            yield
            need("dve", *c_)
            yield each(lambda r: dve.max_index(index[:, r, 8:16], values_[:, r, 8:16], spare(r)))

        t_qT = []
        scores_read = []
        flat = lambda ap: ap.rearrange("p h k -> p (h k)")

        def route(i, h0, BH, batch):
            bi, bufs, bfree = batches.take()
            batch.update(index=bi, **bufs)
            top, topi, topf = (ap[:, 0:2 * BH, :] for ap in (top_, topi_, topf_))
            best, besti = best_[:, 0:BH, :], besti_[:, 0:BH, :]
            part, partf, picked = (ap[:, :, 0:BH, :] for ap in (part_, partf_, picked_))
            cand, rest2 = cand_[:, 0:BH], rest2_[:, 0:BH]
            cand_rows = cand_rows_[:, 0:BH]
            t_sc = []
            for u in range(BH // 2):
                b, bank, free = psum.take()
                need("pe", *free, t_sub, *t_qT[0:2 * (h0 + BH)])
                for v in range(4):
                    r = 4 * u + v
                    last = pe.matmul(bank[:, v * P:(v + 1) * P], qT[:, 2 * h0 + r, i * P:(i + 1) * P], subkeys[:, 2 * h0 + r, :],
                                     start=True, stop=True)
                t = mark(last, "pe_route")
                need("act", t, *scores_read)
                t_sc.append(mark(act.activation(scores[:, 4 * u:4 * u + 4, :].rearrange("p r k -> p (r k)"), bank[:, :], ACT.Copy), "act_route"))
                psum.release(b, t_sc[-1])
            yield
            for t in top16(2 * BH, lambda r: scores[:, r, :], lambda r: left[:, r, :], top, topi, t_sc):
                yield
            need("dve", *t)
            by_head = top.rearrange("p (h a) k -> p h a k", a=2)
            t = mark(dve.tensor_tensor(cand, by_head[:, :, 0, :].unsqueeze(3).to_broadcast([P, BH, TOPK, TOPK]),
                                       by_head[:, :, 1, :].unsqueeze(2).to_broadcast([P, BH, TOPK, TOPK]), ALU.add), "dve_route")
            yield
            for t in top16(BH, lambda r: cand_rows[:, r, :], lambda r: rest2[:, r, :], best, besti, [t]):
                yield
            need("dve", *t, *bfree)
            g, e = batch["gate"][:, 0:BH, :], batch["expert"][:, 0:BH * TOPK]
            t = mark(dve.tensor_tensor(g, best, best[:, :, 0:1].to_broadcast([P, BH, TOPK]), ALU.subtract), "dve_route")
            need("act", t)
            t_exp = mark(act.activation(flat(g), flat(g), ACT.Exp), "act_route")
            t1 = mark(dve.tensor_scalar(flat(part[:, 0]), flat(besti), 4, None, ALU.logical_shift_right), "dve_route")
            t2 = mark(dve.tensor_scalar(flat(part[:, 1]), flat(besti), 15, None, ALU.bitwise_and), "dve_route")
            need("dve", t1, t2)
            t1 = mark(dve.tensor_copy(partf, part), "dve_route")
            t2 = mark(dve.tensor_copy(topf, topi), "dve_route")
            need("dve", t1, t2, t_count)
            yield
            topf_h = topf.rearrange("p (h a) k -> p h a k", a=2)
            for a, hot in enumerate((cand, rest2.rearrange("p h (a b) -> p h a b", a=TOPK))):
                t = mark(dve.tensor_tensor(hot, partf[:, a].unsqueeze(3).to_broadcast([P, BH, TOPK, TOPK]),
                                           count[:].unsqueeze(1).unsqueeze(1).to_broadcast([P, BH, TOPK, TOPK]), ALU.is_equal), "dve_route")
                need("dve", t)
                t = mark(dve.tensor_tensor(hot, hot, topf_h[:, :, a, :].unsqueeze(2).to_broadcast([P, BH, TOPK, TOPK]), ALU.mult), "dve_route")
                yield
                need("dve", t)
                t = mark(dve.tensor_reduce(picked[:, a], hot, AX_X, ALU.add), "dve_route")
                need("dve", t)
                yield
            batch["t_expert"] = mark(dve.scalar_tensor_tensor(e, flat(picked[:, 0]), float(NKEY), flat(picked[:, 1]),
                                                              ALU.mult, ALU.add), "dve_route")
            need("dve", t_exp)
            t = mark(dve.tensor_reduce(gsum[:, 0, 0:BH], g, AX_X, ALU.add), "dve_route")
            need("dve", t)
            t = mark(dve.reciprocal(gsum[:, 1, 0:BH], gsum[:, 0, 0:BH]), "dve_route")
            need("dve", t)
            t = mark(dve.tensor_tensor(g, g, gsum[:, 1, 0:BH].unsqueeze(2).to_broadcast([P, BH, TOPK]), ALU.mult), "dve_route")
            batch["t_gate"] = t
            scores_read[:] = [t]
            need("dve", t, batch["t_expert"])

        order = [(0, 0, 2), (0, 2, 2), (0, 4, 4)] + [(i, h0, 4) for i in range(1, NT) for h0 in (0, 4)]
        batch = {}
        first_route = route(*order[0], batch)
        for u in range(4):
            w, arrived, free_w = weights("w_pq", u, KC, 512)
            need("pe", arrived, *t_h2T)
            for v in range(4):
                b, bank, free = psum.take()
                need("pe", *free)
                t = chain(bank[:, :], [(w[:, c, v * P:(v + 1) * P], h2T[:, c, :]) for c in range(KC)], "pe_pq")
                need("act", t)
                t_qT.append(mark(act.activation(qT[:, 4 * u + v, :], bank[:, :], ACT.Copy), "act_pq"))
                psum.release(b, t_qT[-1])
            free_w.append(t)
            if u == 0:
                for _ in first_route:
                    pass
        t_pq = t
        slots = Ring([sig_a[:, a:a + 4, :].rearrange("p a n -> p (a n)") for a in (0, 4)]
                     + [wring.buffers[(wring.at + k) % 3][:, a:a + 2 * D] for k in range(3) for a in (0, 2 * D)]
                     + [merged[:, a:a + 4, :].rearrange("p a n -> p (a n)") for a in (0, 4)])
        for k in range(2):
            slots.free[k].append(t_merged)
            slots.free[8 + k].append(t_pq)
        for k in range(6):
            slots.free[2 + k] += wring.free[(wring.at + k // 2) % 3]

        def gather(batch, j):
            s, slot, free = slots.take()
            need("pool", batch["t_expert"], *free)
            t = mark(pool.indirect_dma_start(slot, None, A["experts"],
                                             bass.IndirectOffsetOnAxis(ap=batch["expert"][:, j:j + 1], axis=0)), f"ld_slot{s}", 16)
            return s, slot, t

        def finish_tile(i, ob, opair, t_acc):
            y = h2[:, i, :]
            need("dve", t_acc)
            t = mark(dve.tensor_tensor(y.rearrange("p (a n) -> p a n", a=2), opair, rows_["g2"].rearrange("p (a n) -> p a n", a=2), ALU.mult), "dve_last")
            psum.release(ob, t, n=2)
            yield
            need("dve", t)
            t = mark(dve.tensor_tensor(x[:, i, :], x[:, i, :], y, ALU.add), "dve_last")
            yield
            need("dve", t)
            t = token_rstd(x[:, i, :], P, i, y, t, "last")
            yield
            need("dve", t, t_final2)
            t = mark(dve.scalar_tensor_tensor(y, x[:, i, :], stat[:, 2, i:i + 1], final2[:], ALU.mult, ALU.mult), "dve_last")
            need("sp", t)
            stored.append(mark(sp.dma_start(out[i * P:(i + 1) * P, :], y), "st_out", 16))

        stored = []
        finishing = iter(())
        for n, (i, h0, nh) in enumerate(order):
            now, batch = batch, {}
            follows = n + 1 < len(order)
            beside = chained(finishing, route(*order[n + 1], batch) if follows else ())
            g, hid, cf = now["gate"], now["hidden"], now["coef"]
            picks, last_batch = nh * TOPK, h0 + nh == PH
            if h0 == 0:
                ob, opair, ofree = psum.take(2)
                need("pe", *ofree)
            sizes = [GROUP] * (picks // GROUP)
            if not follows:
                sizes[-1:] = [1] * GROUP
            j0 = 0
            for size in sizes:
                group = range(j0, j0 + size)
                gathered = {j: gather(now, j) for j in group}
                for j in group:
                    s, slot, t = gathered[j]
                    need("dve", t)
                    t = mark(dve.tensor_tensor_reduce(slot[:, 0:D], slot[:, 0:D], h2[:, i, :], 1.0, 0.0, ALU.mult, ALU.add,
                                                      hid[:, j:j + 1]), "dve_hidden")
                need("act", t)
                t = mark(act.activation(cf[:, j0:j0 + size], hid[:, j0:j0 + size], ACT.Gelu), "act_gelu")
                need("dve", t, now["t_gate"])
                t = mark(dve.tensor_tensor(cf[:, j0:j0 + size], cf[:, j0:j0 + size], flat(g[:])[:, j0:j0 + size], ALU.mult), "dve_coef")
                need("act", t)
                for j in group:
                    s, slot, arrived = gathered[j]
                    di, dg, dfree = diags.take()
                    need("act", *dfree)
                    t = mark(act.activation(dg, ident[:], ACT.Copy, scale=cf[:, j:j + 1]), "act_diag")
                    need("pe", t, arrived)
                    for half in range(2):
                        last = pe.matmul(opair[:, half, :], dg, slot[:, D + half * 512:D + (half + 1) * 512],
                                         start=h0 == 0 and j == 0, stop=last_batch and j == picks - 1)
                    t_acc = mark(last, "pe_peer")
                    slots.free[s].append(t_acc)
                    diags.free[di].append(t_acc)
                j0 += size
                for _ in range(STEPS if picks == PICKS else 2 * STEPS):
                    next(beside, None)
            for _ in beside:
                pass
            batches.free[now["index"]].append(t_acc)
            if last_batch:
                finishing = finish_tile(i, ob, opair, t_acc)
        for _ in finishing:
            pass
        need("sp", stored[-1])
        peer.close()
        rest.close()
        block2.close()
        late.close()


def constants():
    c = {"ident": np.eye(P, dtype=np.float32)}
    n = np.arange(P)
    pos = (np.arange(NK) + PREFIX - META).astype(np.float64)
    half = RDK // 2
    inv = (1.0 / (np.float32(10000.0) ** (np.arange(half, dtype=np.float32) / np.float32(half)))).astype(np.float32)
    ang = (pos.astype(np.float32)[None, :] * inv[:, None]).astype(np.float32).astype(np.float64)
    cos, sin = np.cos(ang), np.sin(ang)
    log_g = np.log1p(-np.exp2(-5.0 - np.arange(RH)))
    rope1 = np.zeros((4, P, 2, NK))
    mid = pos.mean()
    for j in range(4):
        for s in range(2):
            h = 2 * (j % 2) + s
            decay = np.exp((pos - mid) * log_g[h]) if j < 2 else RDK ** -0.5 * np.exp((mid - pos) * log_g[h])
            for k in range(RDK):
                r = s * RDK + k
                rope1[j, r, 0] = cos[k % half] * decay
                rope1[j, r, 1] = (-sin[k] if k < half else sin[k - half]) * decay
    c["rope1"] = rope1.astype(np.float32)
    swap = np.zeros((P, P), np.float32)
    for b in range(P):
        swap[b + half if b % RDK < half else b - half, b] = 1
    c["swap1"] = swap
    d = n[:, None] - n[None, :]
    same = (n[:, None] // CHUNK) == (n[None, :] // CHUNK)
    c["ret_diag"] = np.stack([np.where(d <= 0, 1.0, np.where(same, np.exp(2.0 * d * log_g[h]), 0.0)) for h in range(RH)],
                             axis=1).astype(np.float32)
    c["causal"] = np.where(d >= 0, 0.0, NEG).astype(np.float32)
    c["sel"] = np.repeat(np.eye(FH, dtype=np.float32)[:, :, None], P, axis=2)
    nf = ROPE // 4
    freq = (np.float32(10000.0) ** (-np.arange(nf, dtype=np.float32) / np.float32(nf))).astype(np.float32)
    t = np.arange(SEQ)
    angle = np.stack([(t // 64)[:, None].astype(np.float32) * freq, (t % 64)[:, None].astype(np.float32) * freq], axis=1)
    angle = angle.astype(np.float32).astype(np.float64)
    rope2 = np.zeros((P, 2, SEQ))
    swap2 = np.zeros((P, P), np.float32)
    for r in range(P):
        a, b, f = (r % ROPE) // 16, (r % 16) // nf, r % nf
        rope2[r, 0] = np.cos(angle[:, a, f])
        rope2[r, 1] = np.sin(angle[:, a, f]) * (-1 if b == 0 else 1)
        swap2[r + nf if b == 0 else r - nf, r] = 1
    c["rope2"] = rope2.astype(np.float32)
    c["swap2"] = swap2
    c["count16"] = np.repeat(np.arange(TOPK, dtype=np.float32)[None], P, axis=0)
    return c


def units(w, pieces, k=KC):
    w3 = w.reshape(k, P, -1).transpose(1, 0, 2)
    out = np.zeros((len(pieces), P, UNIT), w.dtype)
    for u, ranges in enumerate(pieces):
        block = np.concatenate([w3[:, :, a:b] for a, b in ranges], axis=2)
        out[u, :, 0:block.shape[1] * block.shape[2]] = block.reshape(P, -1)
    return out


def plain(n):
    return [[(a, a + 512)] for a in range(0, n, 512)]


def arrange(i):
    f = {k: np.ascontiguousarray(v) for k, v in i.items()}
    a = dict(constants())
    a["x"] = f["x"][0]
    a["meta"] = f["meta_tokens"]
    w = f["w_in"][0]
    a["w_in_v"] = units(w, [[(512, 1024)], [(2560, 3072)]])
    a["w_in_t"] = units(w, [[(0, 512)], [(1024, 1536)], [(1536, 2048)], [(2048, 2560)]])
    a["w_ff"] = w[:, 3072:3080].reshape(KC, P, FH).transpose(1, 0, 2)
    a["fox_b"] = f["fox_forget_b"].reshape(FH, 1)
    a["w_out"] = units(f["w_out"][0], plain(D))
    a["w_up"] = units(f["w_up"][0], [[(256 * u, 256 * u + 256), (F + 256 * u, F + 256 * u + 256)] for u in range(NF // 2)])
    wd = f["w_down"][0]
    down = []
    for half in range(2):
        for f0, f1 in ((0, 8), (8, 16), (16, NF)):
            down.append(units(wd[f0 * P:f1 * P], [[(half * 512, half * 512 + 512)]], f1 - f0))
    a["w_down"] = np.concatenate(down)
    col = lambda v: v.reshape(-1, P).T
    cols = dict(attn_g=col(f["attn_norm_g"][0]), ret_g=col(f["ret_norm_g"][0]), ffn_g=col(f["ffn_norm_g"][0]),
                conv_w=col(f["conv_w"][0].reshape(-1)), conv_b=col(f["conv_b"][0]), norm1_g=col(f["norm1_g_2"][0]),
                q_g=col(f["q_norm_g_2"][0]), kv_g=col(f["kv_norm_g_2"][0]), dw_w=col(f["conv_w_2"][0].reshape(-1)),
                dw_b=col(f["conv_b_2"][0]), ln_g=col(f["conv_ln_g_2"][0]), ln_b=col(f["conv_ln_b_2"][0]),
                cond=np.stack([col(f["c_2"][0]), col(f["c_ctx_2"])], axis=2).reshape(P, -1),
                b_mod=col(f["b_mod_2"][0]))
    a["cols"] = np.concatenate([cols[k] for k in COLUMNS], axis=1)
    a["ctx"] = f["ctx_2"][0].reshape(2, P, D).transpose(1, 0, 2)
    rows = lambda v: np.repeat(v.reshape(1, D), P, axis=0)
    a["final1"], a["norm2_g"], a["final_g"] = rows(f["final_norm_g"]), rows(f["norm2_g_2"]), rows(f["final_g_2"])
    a["w_mod"] = units(f["w_mod_2"][0], plain(6 * D))
    w = f["w_in_2"][0]
    conv0, gate0 = 416, 416 + 2 * D
    a["w_in2"] = units(w, [[(0, 416)]] + [[(conv0 + 256 * u, conv0 + 256 * u + 256),
                                          (conv0 + D + 256 * u, conv0 + D + 256 * u + 256)] for u in range(4)]
                       + [[(gate0 + 512 * u, gate0 + 512 * u + 512)] for u in range(4)])
    uq = f["w_uq_2"][0].reshape(256, AH, QK)
    uq = np.concatenate([uq[:, :, 0:NOPE].reshape(256, -1), uq[:, :, NOPE:].reshape(256, -1)], axis=1)
    a["w_uq"] = units(uq, [[(0, 1536)]], 2)
    ukv = f["w_ukv_2"][0].reshape(P, AH, NOPE + VD)
    ukv = np.concatenate([ukv[:, :, 0:NOPE].reshape(P, -1), ukv[:, :, NOPE:].reshape(P, -1)], axis=1)
    a["w_ukv"] = units(ukv, [[(0, 2048)]], 1)
    a["w_o_mla"] = units(f["w_o_mla_2"][0], plain(D))
    a["w_pw"] = units(f["w_pw_2"][0], plain(D))
    a["w_out2"] = units(f["w_out_2"][0], plain(D))
    a["w_pq"] = units(f["w_pq_2"][0], plain(2048))
    a["sub_keys"] = f["sub_keys_2"][0].reshape(2 * PH, NKEY, P).transpose(2, 0, 1)
    a["experts"] = np.concatenate([f["u_experts_2"][0], f["v_experts_2"][0]], axis=1)
    return {k: np.ascontiguousarray(v) for k, v in a.items()}


def kernel(**inputs):
    import concourse.bacc as bacc
    from concourse.bass_utils import run_bass_kernel_spmd

    nc = bacc.Bacc("TRN2", target_bir_lowering=False, num_devices=1)
    arrays = arrange(inputs)
    A = {name: nc.dram_tensor(f"in_{name}", a.shape, mybir.dt.from_np(a.dtype), kind="ExternalInput").ap()
         for name, a in arrays.items()}
    out = nc.dram_tensor("out_y", (SEQ, D), F32, kind="ExternalOutput").ap()
    program(nc, A, out)
    r = run_bass_kernel_spmd(nc, [{f"in_{name}": a for name, a in arrays.items()}], core_ids=[0])
    return r.results[0]["out_y"].reshape(1, SEQ, D)
```
